# Optimizing a Trainium2 kernel written in Bass

```python
import jax, jax.numpy as jnp
from jax import lax
import numpy as np
import math

D_MODEL = 1024
BATCH = 1
SEQ = 512
DEPTH = 2

CHUNK = 64
N_A_LAYERS = DEPTH // 2
N_B_LAYERS = DEPTH - N_A_LAYERS
MIX_WIDTH = D_MODEL
MEM_TOKENS = 256
MEM_HEADS = 4
MEM_WIDTH = D_MODEL // 4
MEM_HEAD_DIM = MEM_WIDTH // MEM_HEADS
A_WIDTH = MIX_WIDTH - MEM_WIDTH
A_HEADS = 4
A_HEAD_DIM = A_WIDTH // A_HEADS
A_CONV = 4
B_HEAD_DIM = 64
B_HEADS = A_WIDTH // B_HEAD_DIM
B_WIDTH = B_HEADS * B_HEAD_DIM
BAND_CHUNKS = 9
BAND = BAND_CHUNKS * CHUNK
KV_PAD = BAND - CHUNK
MAX_REL = 128
REL_SIZE = MAX_REL + CHUNK
D_FF = ((8 * D_MODEL // 3 + 127) // 128) * 128
FFN_CONV = 3
A_IN = 4 * A_WIDTH + 2 * A_HEADS + MEM_WIDTH
B_IN = B_WIDTH + MEM_WIDTH
EPS = 1e-6


def rmsnorm(x, g):
    x32 = x.astype(jnp.float32)
    y = x32 * lax.rsqrt(jnp.mean(x32 * x32, axis=-1, keepdims=True) + EPS)
    return (y * g.astype(jnp.float32)).astype(x.dtype)

def causal_dwconv(x, w, b):
    k = w.shape[0]
    s = x.shape[1]
    xp = jnp.pad(x, ((0, 0), (k - 1, 0), (0, 0)))
    y = xp[:, 0:s] * w[0]
    for j in range(1, k):
        y = y + xp[:, j:j + s] * w[j]
    return y + b

def mlstm_chunkwise(q, k, v, ig, logf):
    bsz, seq, nh, dh = q.shape
    nc = seq // CHUNK
    f32 = jnp.float32

    def to_chunks(t):
        t = t.astype(f32).reshape((bsz, nc, CHUNK) + t.shape[2:])
        perm = (1, 0, 3, 2) + tuple(range(4, t.ndim))
        return t.transpose(perm)

    qc, kc, vc = to_chunks(q), to_chunks(k * (dh ** -0.5)), to_chunks(v)
    igc, lfc = to_chunks(ig), to_chunks(logf)
    tril = jnp.tril(jnp.ones((CHUNK, CHUNK), dtype=bool))

    def step(carry, inp):
        c_st, n_st, m_st = carry
        qq, kk, vv, ii, lf = inp
        b = jnp.cumsum(lf, axis=-1)
        d = b[..., :, None] - b[..., None, :] + ii[..., None, :]
        d = jnp.where(tril, d, -jnp.inf)
        m_inter = b + m_st[..., None]
        m_t = jnp.maximum(m_inter, jnp.max(d, axis=-1))
        inter = jnp.exp(m_inter - m_t)
        s = jnp.einsum('bhtd,bhsd->bhts', qq, kk) * jnp.exp(d - m_t[..., None])
        num = jnp.einsum('bhts,bhse->bhte', s, vv) + inter[..., None] * jnp.einsum('bhtd,bhde->bhte', qq, c_st)
        den = jnp.sum(s, axis=-1) + inter * jnp.einsum('bhtd,bhd->bht', qq, n_st)
        h = num / jnp.maximum(jnp.abs(den), jnp.exp(-m_t))[..., None]
        b_last = b[..., -1]
        w = b_last[..., None] - b + ii
        m_new = jnp.maximum(b_last + m_st, jnp.max(w, axis=-1))
        w_exp = jnp.exp(w - m_new[..., None])
        decay = jnp.exp(b_last + m_st - m_new)
        c_new = decay[..., None, None] * c_st + jnp.einsum('bhs,bhsd,bhse->bhde', w_exp, kk, vv)
        n_new = decay[..., None] * n_st + jnp.einsum('bhs,bhsd->bhd', w_exp, kk)
        return (c_new, n_new, m_new), h

    init = (jnp.zeros((bsz, nh, dh, dh), f32), jnp.zeros((bsz, nh, dh), f32), jnp.zeros((bsz, nh), f32))
    _, h = lax.scan(step, init, (qc, kc, vc, igc, lfc))
    return h.transpose(1, 0, 3, 2, 4).reshape(bsz, seq, nh, dh)

def band_attention(q, k_pad, v_pad, rel_table):
    bsz, seq, _ = q.shape
    nc = seq // CHUNK
    q = q.reshape(bsz, seq, B_HEADS, B_HEAD_DIM)
    qi = jnp.arange(CHUNK)
    kj = jnp.arange(BAND)
    rel = KV_PAD + qi[:, None] - kj[None, :]
    idx = jnp.clip(rel, -(CHUNK - 1), MAX_REL) + (CHUNK - 1)
    bias = rel_table.astype(jnp.float32)[:, idx]
    scale = B_HEAD_DIM ** -0.5

    def one_chunk(c):
        start = c * CHUNK
        qc = lax.dynamic_slice_in_dim(q, start, CHUNK, axis=1)
        kc = lax.dynamic_slice_in_dim(k_pad, start, BAND, axis=1)
        vc = lax.dynamic_slice_in_dim(v_pad, start, BAND, axis=1)
        s = jnp.einsum('bqhd,bkhd->bhqk', qc, kc).astype(jnp.float32) * scale + bias
        valid = (start - KV_PAD + kj) >= 0
        s = jnp.where(valid, s, -jnp.inf)
        p = jax.nn.softmax(s, axis=-1).astype(vc.dtype)
        return jnp.einsum('bhqk,bkhd->bqhd', p, vc)

    out = lax.map(one_chunk, jnp.arange(nc))
    return out.transpose(1, 0, 2, 3, 4).reshape(bsz, seq, B_WIDTH)

def memory_attention(q, mem, w_kv):
    bsz, seq, _ = q.shape
    q = q.reshape(bsz, seq, MEM_HEADS, MEM_HEAD_DIM)
    mk, mv = jnp.split(mem @ w_kv, 2, axis=-1)
    mk = mk.reshape(bsz, -1, MEM_HEADS, MEM_HEAD_DIM)
    mv = mv.reshape(bsz, -1, MEM_HEADS, MEM_HEAD_DIM)
    s = jnp.einsum('bshd,bmhd->bhsm', q, mk).astype(jnp.float32) * (MEM_HEAD_DIM ** -0.5)
    p = jax.nn.softmax(s, axis=-1).astype(mv.dtype)
    return jnp.einsum('bhsm,bmhd->bshd', p, mv).reshape(bsz, seq, MEM_WIDTH)

def conv_ffn(h, w_up, conv_w, conv_b, w_down):
    u, g = jnp.split(h @ w_up, 2, axis=-1)
    g = causal_dwconv(g, conv_w, conv_b)
    return (jax.nn.silu(g) * u) @ w_down

def first_inputs(seed: int = 0) -> dict:
    key = jax.random.key(seed)
    ks = jax.random.split(key, 24)
    f32 = jnp.float32

    def nrm(k, shape, scale):
        return jax.random.normal(k, shape, f32) * scale

    gate_b = jnp.concatenate([
        nrm(ks[5], (N_A_LAYERS, A_HEADS), 0.1),
        jnp.linspace(3.0, 6.0, A_HEADS, dtype=f32)[None, :] + nrm(ks[6], (N_A_LAYERS, A_HEADS), 0.1),
    ], axis=-1)
    return {
        "x": nrm(ks[0], (BATCH, SEQ, D_MODEL), 1.0),
        "mem": nrm(ks[1], (BATCH, MEM_TOKENS, D_MODEL), 1.0),
        "norm_mix_g": 1.0 + nrm(ks[2], (DEPTH, D_MODEL), 0.1),
        "norm_ffn_g": 1.0 + nrm(ks[3], (DEPTH, D_MODEL), 0.1),
        "a_w_in": nrm(ks[4], (N_A_LAYERS, D_MODEL, A_IN), D_MODEL ** -0.5),
        "a_gate_b": gate_b,
        "a_conv_w": nrm(ks[7], (N_A_LAYERS, A_CONV, 2 * A_WIDTH), A_CONV ** -0.5),
        "a_conv_b": nrm(ks[8], (N_A_LAYERS, 2 * A_WIDTH), 0.02),
        "a_head_g": 1.0 + nrm(ks[9], (N_A_LAYERS, A_WIDTH), 0.1),
        "a_w_out": nrm(ks[10], (N_A_LAYERS, MIX_WIDTH, D_MODEL), MIX_WIDTH ** -0.5),
        "kv_norm_g": 1.0 + nrm(ks[11], (D_MODEL,), 0.1),
        "w_kv": nrm(ks[12], (D_MODEL, 2 * B_WIDTH), D_MODEL ** -0.5),
        "b_w_in": nrm(ks[13], (N_B_LAYERS, D_MODEL, B_IN), D_MODEL ** -0.5),
        "b_rel_bias": nrm(ks[14], (N_B_LAYERS, B_HEADS, REL_SIZE), 0.5),
        "b_w_out": nrm(ks[15], (N_B_LAYERS, MIX_WIDTH, D_MODEL), MIX_WIDTH ** -0.5),
        "mem_w_kv": nrm(ks[16], (DEPTH, D_MODEL, 2 * MEM_WIDTH), D_MODEL ** -0.5),
        "ffn_w_up": nrm(ks[17], (DEPTH, D_MODEL, 2 * D_FF), D_MODEL ** -0.5),
        "ffn_conv_w": nrm(ks[18], (DEPTH, FFN_CONV, D_FF), FFN_CONV ** -0.5),
        "ffn_conv_b": nrm(ks[19], (DEPTH, D_FF), 0.02),
        "ffn_w_down": nrm(ks[20], (DEPTH, D_FF, D_MODEL), D_FF ** -0.5),
        "final_g": 1.0 + nrm(ks[21], (D_MODEL,), 0.1),
    }

def first_block(x, mem, norm_mix_g, norm_ffn_g, a_w_in, a_gate_b, a_conv_w, a_conv_b, a_head_g, a_w_out,
              kv_norm_g, w_kv, b_w_in, b_rel_bias, b_w_out, mem_w_kv, ffn_w_up, ffn_conv_w, ffn_conv_b,
              ffn_w_down, final_g):
    bsz, seq, _ = x.shape
    k_pad = None
    v_pad = None
    for l in range(DEPTH):
        h = rmsnorm(x, norm_mix_g[l])
        if l < N_A_LAYERS:
            a = l
            proj = h @ a_w_in[a]
            qk, v, o, gates, q_mem = jnp.split(
                proj, [2 * A_WIDTH, 3 * A_WIDTH, 4 * A_WIDTH, 4 * A_WIDTH + 2 * A_HEADS], axis=-1)
            qk = jax.nn.silu(causal_dwconv(qk, a_conv_w[a], a_conv_b[a]))
            q, k = jnp.split(qk, 2, axis=-1)
            gates = gates.astype(jnp.float32) + a_gate_b[a].astype(jnp.float32)
            ig, fg = jnp.split(gates, 2, axis=-1)
            hm = mlstm_chunkwise(q.reshape(bsz, seq, A_HEADS, A_HEAD_DIM),
                                 k.reshape(bsz, seq, A_HEADS, A_HEAD_DIM),
                                 v.reshape(bsz, seq, A_HEADS, A_HEAD_DIM),
                                 ig, jax.nn.log_sigmoid(fg))
            hm = hm * lax.rsqrt(jnp.mean(hm * hm, axis=-1, keepdims=True) + EPS)
            hm = hm.reshape(bsz, seq, A_WIDTH) * a_head_g[a].astype(jnp.float32)
            mix_out = (hm * jax.nn.sigmoid(o.astype(jnp.float32))).astype(x.dtype)
            w_out = a_w_out[a]
        else:
            bl = l - N_A_LAYERS
            proj = h @ b_w_in[bl]
            q, q_mem = jnp.split(proj, [B_WIDTH], axis=-1)
            mix_out = band_attention(q, k_pad, v_pad, b_rel_bias[bl])
            w_out = b_w_out[bl]
        mem_out = memory_attention(q_mem, mem, mem_w_kv[l])
        x = x + jnp.concatenate([mix_out, mem_out], axis=-1) @ w_out
        x = x + conv_ffn(rmsnorm(x, norm_ffn_g[l]), ffn_w_up[l], ffn_conv_w[l], ffn_conv_b[l], ffn_w_down[l])
        if l == N_A_LAYERS - 1:
            ks_, vs_ = jnp.split(rmsnorm(x, kv_norm_g) @ w_kv, 2, axis=-1)
            pad = ((0, 0), (KV_PAD, 0), (0, 0), (0, 0))
            k_pad = jnp.pad(ks_.reshape(bsz, seq, B_HEADS, B_HEAD_DIM), pad)
            v_pad = jnp.pad(vs_.reshape(bsz, seq, B_HEADS, B_HEAD_DIM), pad)
    return rmsnorm(x, final_g)


DEPTH_2 = 1

QBLOCK = 128
MIX_WIDTH_2 = D_MODEL
DIFF_HEADS = 4
DIFF_DH = 64
DIFF_VD = 2 * DIFF_DH
FOX_HEADS = 8
FOX_DH = 64
ROPE_THETA = 500000.0
ROPE_DIM = DIFF_DH // 4
D_FF_2 = ((8 * D_MODEL // 3 + 255) // 256) * 256
EPS_2 = 1e-5
NEG = -1e30

DIFF_QK_W = DIFF_HEADS * 2 * DIFF_DH
DIFF_V_W = DIFF_HEADS * DIFF_VD
FOX_W = FOX_HEADS * FOX_DH
PROJ_W = 2 * DIFF_QK_W + DIFF_V_W + 3 * FOX_W + FOX_HEADS
SPLITS = (DIFF_QK_W,
          2 * DIFF_QK_W,
          2 * DIFF_QK_W + DIFF_V_W,
          2 * DIFF_QK_W + DIFF_V_W + FOX_W,
          2 * DIFF_QK_W + DIFF_V_W + 2 * FOX_W,
          2 * DIFF_QK_W + DIFF_V_W + 3 * FOX_W)


def rmsnorm_2(x, g):
    xf = x.astype(jnp.float32)
    y = xf * lax.rsqrt(jnp.mean(xf * xf, axis=-1, keepdims=True) + EPS_2)
    return (y * g.astype(jnp.float32)).astype(x.dtype)

def rope_partial(t, cos, sin):
    half = ROPE_DIM // 2
    shp = (1, t.shape[1]) + (1,) * (t.ndim - 3) + (half,)
    c = cos.reshape(shp).astype(t.dtype)
    s = sin.reshape(shp).astype(t.dtype)
    t1 = t[..., :half]
    t2 = t[..., half:ROPE_DIM]
    return jnp.concatenate([t1 * c - t2 * s, t2 * c + t1 * s, t[..., ROPE_DIM:]], axis=-1)

def to_blocks(t, nb):
    b, _, h, d = t.shape
    return t.reshape(b, nb, QBLOCK, h, d).transpose(1, 0, 3, 2, 4)

def from_blocks(t):
    nb, b, h, q, d = t.shape
    return t.transpose(1, 0, 3, 2, 4).reshape(b, nb * q, h * d)

def second_inputs(seed: int = 0) -> dict:
    key = jax.random.key(seed)
    ks = jax.random.split(key, 16)
    f32 = jnp.float32
    nrm = lambda k, shp, s: jax.random.normal(k, shp, f32) * s
    return {
        "x": jax.random.normal(ks[0], (BATCH, SEQ, D_MODEL), f32),
        "norm1_g": 1.0 + nrm(ks[1], (DEPTH_2, D_MODEL), 0.02),
        "w_in": nrm(ks[2], (DEPTH_2, D_MODEL, PROJ_W), D_MODEL ** -0.5),
        "b_f": 3.0 + nrm(ks[3], (DEPTH_2, FOX_HEADS), 0.5),
        "lam_q1": nrm(ks[4], (DEPTH_2, DIFF_DH), 0.1),
        "lam_k1": nrm(ks[5], (DEPTH_2, DIFF_DH), 0.1),
        "lam_q2": nrm(ks[6], (DEPTH_2, DIFF_DH), 0.1),
        "lam_k2": nrm(ks[7], (DEPTH_2, DIFF_DH), 0.1),
        "subln_g": 1.0 + nrm(ks[8], (DEPTH_2, DIFF_VD), 0.02),
        "w_out": nrm(ks[9], (DEPTH_2, MIX_WIDTH_2, D_MODEL), MIX_WIDTH_2 ** -0.5),
        "norm2_g": 1.0 + nrm(ks[10], (DEPTH_2, D_MODEL), 0.02),
        "w_gate": nrm(ks[11], (DEPTH_2, D_MODEL, D_FF_2), D_MODEL ** -0.5),
        "w_up": nrm(ks[12], (DEPTH_2, D_MODEL, D_FF_2), D_MODEL ** -0.5),
        "w_down": nrm(ks[13], (DEPTH_2, D_FF_2, D_MODEL), D_FF_2 ** -0.5),
        "normf_g": 1.0 + nrm(ks[14], (D_MODEL,), 0.02),
    }

def second_block(x, norm1_g, w_in, b_f, lam_q1, lam_k1, lam_q2, lam_k2, subln_g, w_out,
              norm2_g, w_gate, w_up, w_down, normf_g):
    f32 = jnp.float32
    B, S, _ = x.shape
    nb = S // QBLOCK
    pos = jnp.arange(S, dtype=jnp.int32)
    inv_freq = ROPE_THETA ** (-jnp.arange(0, ROPE_DIM, 2, dtype=f32) / ROPE_DIM)
    ang = pos.astype(f32)[:, None] * inv_freq[None, :]
    cos, sin = jnp.cos(ang), jnp.sin(ang)
    k_chunk = pos // CHUNK
    scale_d = DIFF_DH ** -0.5
    scale_f = FOX_DH ** -0.5

    for l in range(DEPTH_2):
        lam_init = 0.8 - 0.6 * math.exp(-0.3 * l)
        h = rmsnorm_2(x, norm1_g[l])
        proj = jnp.einsum('bsd,de->bse', h, w_in[l])
        dq, dk, dv, fq, fk, fv, fg = jnp.split(proj, SPLITS, axis=-1)

        dq = rope_partial(dq.reshape(B, S, DIFF_HEADS, 2, DIFF_DH), cos, sin)
        dk = rope_partial(dk.reshape(B, S, DIFF_HEADS, 2, DIFF_DH), cos, sin)
        dv_t = dv.reshape(B, S, DIFF_HEADS, DIFF_VD).transpose(0, 2, 1, 3)
        k1 = dk[:, :, :, 0].transpose(0, 2, 1, 3)
        k2 = dk[:, :, :, 1].transpose(0, 2, 1, 3)
        lam = (jnp.exp(jnp.sum(lam_q1[l].astype(f32) * lam_k1[l].astype(f32)))
               - jnp.exp(jnp.sum(lam_q2[l].astype(f32) * lam_k2[l].astype(f32)))
               + lam_init)

        fq = fq.reshape(B, S, FOX_HEADS, FOX_DH)
        fk_t = fk.reshape(B, S, FOX_HEADS, FOX_DH).transpose(0, 2, 1, 3)
        fv_t = fv.reshape(B, S, FOX_HEADS, FOX_DH).transpose(0, 2, 1, 3)
        log_f = jax.nn.log_sigmoid((fg + b_f[l]).astype(f32))
        cum = jnp.cumsum(log_f, axis=1).transpose(0, 2, 1)
        cum_blocks = cum.reshape(B, FOX_HEADS, nb, QBLOCK).transpose(2, 0, 1, 3)

        def block(args):
            i, q1b, q2b, qfb, cqb = args
            qpos = i * QBLOCK + jnp.arange(QBLOCK, dtype=jnp.int32)
            chunk_mask = k_chunk[None, :] <= (qpos // CHUNK)[:, None]
            causal = pos[None, :] <= qpos[:, None]
            s1 = jnp.einsum('bhqd,bhkd->bhqk', q1b, k1, preferred_element_type=f32) * scale_d
            s2 = jnp.einsum('bhqd,bhkd->bhqk', q2b, k2, preferred_element_type=f32) * scale_d
            p = (jax.nn.softmax(jnp.where(chunk_mask, s1, NEG), axis=-1)
                 - lam * jax.nn.softmax(jnp.where(chunk_mask, s2, NEG), axis=-1))
            od = jnp.einsum('bhqk,bhkd->bhqd', p.astype(dv_t.dtype), dv_t)
            sf = (jnp.einsum('bhqd,bhkd->bhqk', qfb, fk_t, preferred_element_type=f32) * scale_f
                  + cqb[:, :, :, None] - cum[:, :, None, :])
            pf = jax.nn.softmax(jnp.where(causal, sf, NEG), axis=-1)
            of = jnp.einsum('bhqk,bhkd->bhqd', pf.astype(fv_t.dtype), fv_t)
            return od, of

        od_b, of_b = lax.map(block, (jnp.arange(nb, dtype=jnp.int32),
                                     to_blocks(dq[:, :, :, 0], nb),
                                     to_blocks(dq[:, :, :, 1], nb),
                                     to_blocks(fq, nb),
                                     cum_blocks))
        od_b = rmsnorm_2(od_b, subln_g[l]) * (1.0 - lam_init)
        mix = jnp.concatenate([from_blocks(od_b), from_blocks(of_b)], axis=-1)
        x = x + jnp.einsum('bse,ed->bsd', mix, w_out[l])

        h2 = rmsnorm_2(x, norm2_g[l])
        g = jnp.einsum('bsd,df->bsf', h2, w_gate[l])
        u = jnp.einsum('bsd,df->bsf', h2, w_up[l])
        x = x + jnp.einsum('bsf,fd->bsd', jax.nn.silu(g) * u, w_down[l])

    return rmsnorm_2(x, normf_g)


def setup_inputs(seed=0):
    out = dict(first_inputs(seed))
    for name, value in second_inputs(seed + 1).items():
        if name != "x":
            out[name + "_2"] = value
    return out


def reference(
    x, mem, norm_mix_g, norm_ffn_g, a_w_in, a_gate_b, a_conv_w, a_conv_b, a_head_g, a_w_out,
    kv_norm_g, w_kv, b_w_in, b_rel_bias, b_w_out, mem_w_kv, ffn_w_up, ffn_conv_w, ffn_conv_b,
    ffn_w_down, final_g, norm1_g_2, w_in_2, b_f_2, lam_q1_2, lam_k1_2, lam_q2_2, lam_k2_2,
    subln_g_2, w_out_2, norm2_g_2, w_gate_2, w_up_2, w_down_2, normf_g_2,
):
    x = first_block(
        x, mem, norm_mix_g, norm_ffn_g, a_w_in, a_gate_b, a_conv_w, a_conv_b, a_head_g, a_w_out,
        kv_norm_g, w_kv, b_w_in, b_rel_bias, b_w_out, mem_w_kv, ffn_w_up, ffn_conv_w,
        ffn_conv_b, ffn_w_down, final_g,
    )
    return second_block(
        x, norm1_g_2, w_in_2, b_f_2, lam_q1_2, lam_k1_2, lam_q2_2, lam_k2_2, subln_g_2, w_out_2,
        norm2_g_2, w_gate_2, w_up_2, w_down_2, normf_g_2,
    )


_drawn_inputs = setup_inputs


def setup_inputs(seed=0):
    import zlib

    import numpy as np

    out = dict(_drawn_inputs(seed))
    spreads = {}
    factors = {'a_conv_b': 5.89,
     'ffn_conv_b': 3.694,
     'norm1_g_2': 3.664,
     'lam_q1_2': 198.712,
     'lam_k1_2': 3.925,
     'lam_q2_2': 24.067,
     'subln_g_2': 14.808,
     'norm2_g_2': 4.481,
     'normf_g_2': 23.194,
     'lam_k2_2': 5.022}
    for name, (base, spread) in spreads.items():
        noise = np.random.default_rng([zlib.crc32(name.encode()), seed]).standard_normal(out[name].shape)
        drawn = base * np.exp(spread * noise) if base else spread * noise
        out[name] = __import__('jax').numpy.asarray(drawn.astype(out[name].dtype))
    for name, factor in factors.items():
        out[name] = (out[name] * factor).astype(out[name].dtype)
    return out
```

```python
from contextlib import ExitStack

import numpy as np
import concourse.bass as bass
from concourse import mybir

F32 = mybir.dt.float32
F32R = mybir.dt.float32r
ALU = mybir.AluOpType
ACT = mybir.ActivationFunctionType
AX = mybir.AxisListType

NEG = -1e30
NT = 4
DFF = 2816
SLOT = 2048
NRAW = 2
NCV = 2
CAUSAL = [(3, 512, 0, 0), (2, 384, 1, 0), (0, 128, 1, 384), (1, 256, 2, 0)]
FULL256 = [(0, 256, 0, 0), (1, 256, 0, 256), (2, 256, 1, 0), (3, 256, 1, 256)]


def ffn_plan(up, upo, gate, gateo, down, idx):
    out = []
    for j0, j1, ks in ((0, 6, ((0, 4), (4, 4), (8, 4))), (6, 11, ((12, 4), (16, 4), (20, 2)))):
        for j in range(j0, j1):
            out.append((gate, idx, 0, 8, gateo + 256 * j, 256))
            out.append((up, idx, 0, 8, upo + 256 * j, 256))
        for mg in range(2):
            for k0, nk in ks:
                out.append((down, idx, k0, nk, 512 * mg, 512))
    return out


def plan():
    u = [("mem_w_kv", 0, 0, 8, 0, 256), ("mem_w_kv", 0, 0, 8, 256, 256)]
    u += [("a_w_in", 0, 0, 8, 3072, 128), ("a_w_in", 0, 0, 8, 3080, 256)]
    u += [("a_w_in", 0, 0, 8, 256 * j, 256) for j in range(12)]
    u += [("a_w_out", 0, 0, 8, 256 * j, 256) for j in range(4)]
    u += ffn_plan("ffn_w_up", 0, "ffn_w_up", DFF, "ffn_w_down", 0)
    u += [("w_kv", None, 0, 8, 256 * j, 256) for j in range(6)]
    u += [("mem_w_kv", 1, 0, 8, 0, 256), ("mem_w_kv", 1, 0, 8, 256, 256)]
    u += [("b_w_in", 0, 0, 8, 256 * j, 256) for j in (3, 0, 1, 2)]
    u += [("b_w_out", 0, 0, 8, 256 * j, 256) for j in range(4)]
    u += ffn_plan("ffn_w_up", 0, "ffn_w_up", DFF, "ffn_w_down", 1)
    u += [("w_in_2", 0, 0, 8, 2952, 128)]
    u += [("w_in_2", 0, 0, 8, 256 * j, 256) for j in range(12)]
    u += [("w_out_2", 0, 0, 8, 256 * j, 256) for j in range(4)]
    u += ffn_plan("w_up_2", 0, "w_gate_2", 0, "w_down_2", 0)
    return u


def columns():
    at, out = 0, {}
    for name, n in [("mix0", 8), ("mix1", 8), ("ffn0", 8), ("ffn1", 8), ("kv", 8), ("final", 8),
                    ("n1", 8), ("n2", 8), ("nf", 8), ("cw", 48), ("cb", 12), ("hg", 6),
                    ("fw0", 66), ("fb0", 22), ("fw1", 66), ("fb1", 22), ("sub", 1), ("gi", 1), ("gf", 1),
                    ("bf", 1), ("lam", 4)]:
        out[name] = (at, n)
        at += n
    return out, at


COLS, NCOLS = columns()


class Lane:

    def __init__(self, sem):
        self.sem, self.q, self.n, self.seen = sem, [], 0, {}

    def wait(self, *marks):
        for m in marks:
            if m is None:
                continue
            if isinstance(m, list):
                self.wait(*m)
                continue
            sem, v = m
            if self.seen.get(sem.name, 0) < v:
                self.seen[sem.name] = v
                self.q.append(lambda e, sem=sem, v=v: e.wait_ge(sem, v))

    def do(self, fn, *marks):
        self.wait(*marks)
        self.n += 1
        self.q.append(lambda e: fn(e).then_inc(self.sem, 1))
        return (self.sem, self.n)

    def go(self, fn, *marks):
        self.wait(*marks)
        self.q.append(fn)

    def load(self, fn, sem, value, *marks):
        self.wait(*marks)
        self.q.append(lambda e: fn(e).then_inc(sem, 16))
        return (sem, value)

    def last(self):
        return (self.sem, self.n) if self.n else None

    def play(self, e):
        for f in self.q:
            f(e)


def program(nc, wall, xt, memt, colsd, biasd, consts, rope, seld, out, stop=None):
    ctx = ExitStack()
    with ctx:
        def sem(name):
            return ctx.enter_context(nc.semaphore(name))

        def sbt(c, name, shape, dt=F32):
            return c.enter_context(nc.sbuf_tensor(name, shape, dt))

        pe, act, dve, pool, sp = (Lane(sem(n)) for n in ("s_pe", "s_act", "s_dve", "s_pool", "s_sp"))

        def fence():
            return [x.last() for x in (pe, act, dve, pool)]

        ps = [ctx.enter_context(nc.psum_tensor(f"ps{i}", [128, 512], F32)) for i in range(8)]
        bank_free = [None] * 8
        bank_at = [0]

        held = set()

        def bank(hold=False):
            while bank_at[0] % 8 in held:
                bank_at[0] += 1
            b = bank_at[0] % 8
            bank_at[0] += 1
            if hold:
                held.add(b)
            return b

        X = sbt(ctx, "X", [128, 8, 512])
        hH = sbt(ctx, "hH", [128, 8, 512], F32R)
        hL = sbt(ctx, "hL", [128, 8, 512], F32R)
        raw = [sbt(ctx, f"raw{i}", [128, SLOT]) for i in range(NRAW)]
        WH = [sbt(ctx, f"WH{i}", [128, SLOT], F32R) for i in range(NCV)]
        WL = [sbt(ctx, f"WL{i}", [128, SLOT], F32R) for i in range(NCV)]
        cols = sbt(ctx, "cols", [128, NCOLS])
        K = sbt(ctx, "K", [128, 5, 128])
        ident, ones, mchunk, mcaus, rotm = (K[:, i, :] for i in range(5))
        acc = sbt(ctx, "acc", [128, 512])
        sq = [sbt(ctx, f"sq{i}", [128, 512]) for i in range(2)]
        diag = sbt(ctx, "diag", [128, 512])
        Rsb = sbt(ctx, "Rsb", [128, 512])
        tt = [sbt(ctx, f"tt{i}", [128, 512]) for i in range(2)]
        small = sbt(ctx, "small", [128, 64])

        def col(name, i=0, n=1, p=slice(0, 128)):
            a = COLS[name][0] + i
            return cols[p, a:a + n]

        units = plan()
        woff = [0]
        for u in units:
            woff.append(woff[-1] + u[3] * u[5])
        s_raw = [sem(f"s_raw{i}") for i in range(NRAW)]
        w_lo = {}
        w_free = {}
        wst = {"load": 0, "conv": 0, "next": 0}
        state = {"stop": False}

        def w_load(n):
            size = woff[n + 1] - woff[n]
            r = n % NRAW
            return sp.load(lambda e: e.dma_start(raw[r][:, 0:size], wall[:, woff[n]:woff[n + 1]]),
                           s_raw[r], 16 * (n // NRAW + 1), w_lo.get(n - NRAW))

        def w_convert(n):
            size = woff[n + 1] - woff[n]
            loaded = w_load(n)
            r, c = n % NRAW, n % NCV
            half = size // 2
            for a, b in ((0, half), (half, size)):
                m = act.do(lambda e, a=a, b=b: e.activation(WH[c][:, a:b], raw[r][:, a:b], ACT.Copy),
                           loaded, w_free.get(n - NCV))
                lo = dve.do(lambda e, a=a, b=b: e.tensor_tensor(
                    WL[c][:, a:b], raw[r][:, a:b], WH[c][:, a:b].bitcast(F32), ALU.subtract), m)
            w_lo[n] = lo

        def take():
            n = wst["next"]
            wst["next"] += 1
            while wst["conv"] < min(n + 2, len(units)):
                w_convert(wst["conv"])
                wst["conv"] += 1
            pe.wait(w_lo[n])
            _, _, k0, nk, _, ncl = units[n]
            v = [WH[n % NCV][:, 0:nk * ncl].rearrange("p (k c) -> p k c", k=nk),
                 WL[n % NCV][:, 0:nk * ncl].rearrange("p (k c) -> p k c", k=nk)]
            return n, k0, nk, ncl, v

        deferred = []

        def run_deferred():
            while deferred:
                deferred.pop(0)()

        def linear_fm(nunits, AH, AL, marks, sink, N=512, m0=0):
            m = m0
            for _ in range(nunits):
                n, _, nk, ncl, (wh, wl) = take()
                for c in range(0, ncl, 128):
                    b = bank()
                    pe.wait(bank_free[b])
                    o = ps[b][:, 0:N]
                    for k in range(nk):
                        pe.wait(marks[k])
                        for i, (w, x) in enumerate(((wh, AH), (wh, AL), (wl, AH))):
                            f = (lambda e, o=o, w=w, x=x, k=k, c=c, i=i: e.matmul(
                                o, w[:, k, c:c + 128], x[:, k, 0:N], start=(k == 0 and i == 0),
                                stop=(k == nk - 1 and i == 2)))
                            if k == nk - 1 and i == 2:
                                mk = pe.do(f)
                            else:
                                pe.go(f)
                    run_deferred()
                    sink(m, b, mk)
                    m += 1
                w_free[n] = mk

        def linear_tm(nunits, AH, AL, marks, dst, ntt=4, off=0, eng=None):
            eng = eng or act
            got = []
            for un in range(nunits):
                n, _, nk, ncl, (wh, wl) = take()
                for t0 in range(0, ntt, 2):
                    b = bank()
                    pe.wait(bank_free[b])
                    for t in (t0, t0 + 1):
                        o = ps[b][:, (t - t0) * 256:(t - t0) * 256 + 256]
                        for k in range(nk):
                            pe.wait(marks[k])
                            for i, (w, x) in enumerate(((wh, AH), (wl, AH), (wh, AL))):
                                f = (lambda e, o=o, w=w, x=x, k=k, t=t, i=i: e.matmul(
                                    o, x[:, k, t * 128:t * 128 + 128], w[:, k, :],
                                    start=(k == 0 and i == 0), stop=(k == nk - 1 and i == 2)))
                                if k == nk - 1 and i == 2:
                                    mk = pe.do(f)
                                else:
                                    pe.go(f)
                    run_deferred()
                    src = ps[b][:, :].rearrange("p (t c) -> p t c", t=2)
                    bank_free[b] = copy(eng, dst[:, t0:t0 + 2, off + 256 * un:off + 256 * un + 256], src, mk)
                    got.append(bank_free[b])
                w_free[n] = mk
            return got

        def copy(eng, o, i, *marks, scale=None):
            if eng is act:
                return act.do(lambda e: e.activation(o, i, ACT.Copy, scale=1.0 if scale is None else scale),
                              *marks)
            return eng.do(lambda e: e.tensor_copy(o, i), *marks)

        acc_free = [None]
        sq_free = [None, None]
        x_mark = [None] * 8
        acc_mark = [None]

        def square(k, mark):
            if k == 0:
                acc_mark[0] = act.do(lambda e: e.activation(acc[:, :], X[:, 0, :], ACT.Square), mark, acc_free[0])
                return
            i = k % 2
            m = act.do(lambda e: e.activation(sq[i][:, :], X[:, k, :], ACT.Square), mark, sq_free[i])
            acc_mark[0] = sq_free[i] = pool.do(
                lambda e: e.tensor_tensor(acc[:, :], acc[:, :], sq[i][:, :], ALU.add), m, acc_mark[0])

        def col_sums(parts, outs):
            pass

        diag_free = [None]
        r_free = [None]

        def bcast(colap, mark, dst, rows=slice(0, 128), bnk=None, done=True):
            ms = [mark, diag_free[0]]
            for i in range(4):
                d = dve.do(lambda e, i=i: e.tensor_scalar(diag[:, i * 128:i * 128 + 128], ident,
                                                          colap[:, i:i + 1], None, ALU.mult), *ms)
            n = rows.stop - rows.start
            diag_free[0] = pe.do(lambda e: e.matmul(ps[bnk][rows, :], ones[:, 0:n], diag[:, :],
                                                    start=True, stop=True), d, bank_free[bnk])
            return diag_free[0]

        def rstd(eps, scale):
            b = bank()
            pe.wait(bank_free[b], acc_mark[0], c_mark)
            for i in range(4):
                m = pe.do(lambda e, i=i: e.matmul(ps[b][:, i:i + 1], acc[:, i * 128:i * 128 + 128],
                                                  ones[:, 0:1], start=True, stop=True))
            acc_free[0] = m
            bank_free[b] = m = act.do(lambda e: e.activation(small[:, 0:4], ps[b][:, 0:4], ACT.Sqrt,
                                                             bias=small[:, eps:eps + 1], scale=scale), m)
            m = dve.do(lambda e: e.reciprocal(small[:, 4:8], small[:, 0:4]), m)
            b = bank()
            m = bcast(small[:, 4:8], m, None, bnk=b)
            bank_free[b] = m = copy(act, Rsb[:, :], ps[b][:, :], m, r_free[0])
            return m

        tt_free = [None, None]

        def split(src, mark, k, *free):
            hi = copy(act, hH[:, k, :], src, mark, *free)
            lo_eng = pool if k % 2 else dve
            lo = lo_eng.do(lambda e: e.tensor_tensor(hL[:, k, :], src, hH[:, k, :].bitcast(F32),
                                                     ALU.subtract), hi, *free)
            return hi, lo

        def normed(g, rm, free):
            marks = []
            for k in range(8):
                i = k % 2
                m = dve.do(lambda e, k=k, i=i: e.scalar_tensor_tensor(
                    out=tt[i][:, :], in0=X[:, k, :], scalar=col(g, k), in1=Rsb[:, :],
                    op0=ALU.mult, op1=ALU.mult), rm, x_mark[k], tt_free[i])
                hi, lo = split(tt[i][:, :], m, k, free)
                tt_free[i] = lo
                marks.append([hi, lo])
            r_free[0] = m
            return marks

        def residual(last):
            def sink(m, b, mk):
                bank_free[b] = x_mark[m] = dve.do(lambda e: e.tensor_tensor(
                    X[:, m, :], X[:, m, :], ps[b][:, :], ALU.add), mk)
                if last:
                    square(m, x_mark[m])
            return sink

        s_c = [sem(f"s_c{i}") for i in range(8)]
        c_cols = act.load(lambda e: e.dma_start(cols[:, :], colsd), s_c[0], 16)
        c_K = act.load(lambda e: e.dma_start(K[:, :, :], consts.rearrange("p (i c) -> p i c", i=5)), s_c[1], 16)
        eps6 = pool.do(lambda e: e.memset(small[:, 60:61], 1e-6))
        eps5 = pool.do(lambda e: e.memset(small[:, 61:62], 1e-5))
        c_mark = [c_cols, c_K, eps6, eps5]
        for x in (act, dve, pool):
            x.wait(eps5)

        class Soft:

            def __init__(self, c, tag, nP=2):
                self.P = [sbt(c, f"P{tag}{i}", [128, 1536]) for i in range(nP)]
                self.PT = [sbt(c, f"PT{tag}{i}", [128, 4, 512]) for i in range(2)]
                self.st = sbt(c, f"st{tag}", [128, 4, 16])
                self.Pfree = [None] * nP
                self.PTfree = [None] * 2
                self.npt = 0
                self.n = 0

            def scores(self, u):
                u["i"] = self.n
                self.n += 1
                lay = u["lay"]
                bs = [bank() for _ in range(max(x[2] for x in lay) + 1)]
                u["b"] = bs
                u["sm"] = {}
                for t, L, bi, off in lay:
                    b = bs[bi]
                    msk = u.get("mask")
                    pe.wait(bank_free[b], *u["qk"])
                    f = (lambda e, t=t, L=L, b=b, off=off: e.matmul(
                        ps[b][:, off:off + L], u["q"](t), u["k"](L), start=True, stop=msk is None))
                    if msk is None:
                        u["sm"][bi] = pe.do(f)
                    else:
                        pe.go(f)
                        u["sm"][bi] = pe.do(lambda e, L=L, b=b, off=off: e.matmul(
                            ps[b][:, off + L - 128:off + L], ident, msk, start=False, stop=True))

            def probs(self, u):
                lay, i = u["lay"], u["i"]
                P = self.P[i % len(self.P)]
                u["P"] = P
                st = self.st[:, i % 4, :]
                pf = self.Pfree[i % len(self.P)]
                rd = {}
                for t, L, bi, off in lay:
                    b = u["b"][bi]
                    src, o = ps[b][:, off:off + L], bi * 512 + off
                    if "bias" in u:
                        m = dve.do(lambda e, t=t, src=src, o=o, L=L: e.tensor_tensor_reduce(
                            P[:, o:o + L], src, u["bias"](L), 1.0, -3e38, ALU.add, ALU.max,
                            st[:, t:t + 1]), u["sm"][bi], pf, *u.get("bm", []))
                        bank_free[b] = m
                    else:
                        m = dve.do(lambda e, t=t, src=src: e.tensor_reduce(
                            st[:, t:t + 1], src, AX.X, ALU.max), u["sm"][bi])
                    rd[t] = m
                m = dve.do(lambda e: e.tensor_scalar(st[:, 4:8], st[:, 0:4], -1.0, None, ALU.mult), m)
                for t, L, bi, off in lay:
                    b = u["b"][bi]
                    o = bi * 512 + off
                    src = P[:, o:o + L] if "bias" in u else ps[b][:, off:off + L]
                    x = act.do(lambda e, t=t, src=src, o=o, L=L: e.activation(
                        P[:, o:o + L], src, ACT.Exp, bias=st[:, 4 + t:5 + t],
                        accum_out=st[:, 8 + t:9 + t]), m, pf)
                    if "bias" not in u:
                        bank_free[b] = x
                rc = dve.do(lambda e: e.reciprocal(st[:, 12:16], st[:, 8:12]), x)
                if u.get("neg") is not None:
                    nm, nmm = u["neg"]
                    rc = dve.do(lambda e: e.tensor_scalar(st[:, 12:16], st[:, 12:16], nm, None, ALU.mult),
                                rc, nmm)
                prev = u.get("prev")
                for t, L, bi, off in lay:
                    o = bi * 512 + off
                    if prev is None:
                        y = dve.do(lambda e, t=t, o=o, L=L: e.tensor_scalar(
                            P[:, o:o + L], P[:, o:o + L], st[:, 12 + t:13 + t], None, ALU.mult), rc)
                    else:
                        y = dve.do(lambda e, t=t, o=o, L=L: e.scalar_tensor_tensor(
                            out=P[:, o:o + L], in0=P[:, o:o + L], scalar=st[:, 12 + t:13 + t],
                            in1=prev["P"][:, o:o + L], op0=ALU.mult, op1=ALU.add), rc, prev["pm"])
                if prev is not None:
                    self.Pfree[prev["i"] % len(self.P)] = y
                u["pm"] = y

            def turn(self, u):
                if u.get("part"):
                    return
                lay = u["lay"]
                PT = self.PT[self.npt % 2]
                u["PT"] = PT
                u["ipt"] = self.npt
                ptf = self.PTfree[self.npt % 2]
                self.npt += 1
                bs = [bank() for _ in range(max(x[2] for x in lay) + 1)]
                mk = {}
                P = u["P"]
                for t, L, bi, off in lay:
                    b = bs[bi]
                    pe.wait(bank_free[b], u["pm"])
                    for j in range(L // 128):
                        f = (lambda e, b=b, o=off + j * 128, s=bi * 512 + off + j * 128: e.transpose(
                            ps[b][:, o:o + 128], P[:, s:s + 128], ident))
                        if j == L // 128 - 1:
                            mk[bi] = pe.do(f)
                        else:
                            pe.go(f)
                self.Pfree[u["i"] % len(self.P)] = mk[bi]
                out = []
                for t, L, bi, off in lay:
                    b = bs[bi]
                    eng = act if bi == 0 else dve
                    src = ps[b][:, off:off + L].rearrange("p (j t) -> p j t", t=128)
                    bank_free[b] = copy(eng, PT[:, 0:L // 128, t * 128:t * 128 + 128], src, mk[bi], ptf)
                    out.append(bank_free[b])
                u["tm"] = out

            def values(self, u):
                if u.get("part"):
                    return
                if u["bank"] is None:
                    u["bank"] = u["pair"]["bank"] if u.get("pair") else bank(not u.get("sink"))
                    if not u.get("pair"):
                        pe.wait(bank_free[u["bank"]])
                b, rows = u["bank"], u["rows"]
                pe.wait(*u["tm"])
                pe.wait(*u["vm"])
                nj = 2 if u["lay"] is FULL256 else 4
                for j in range(nj):
                    t0 = 0 if nj == 2 else j * 128
                    f = (lambda e, j=j, t0=t0: e.matmul(
                        ps[b][rows, t0:512], u["v"](j), u["PT"][:, j, t0:512],
                        start=(j == 0), stop=(j == nj - 1)))
                    if j == nj - 1:
                        m = pe.do(f)
                    else:
                        pe.go(f)
                self.PTfree[u["ipt"] % 2] = m
                if u.get("sink"):
                    held.discard(b)
                    u["sink"](b, m)

            def run(self, us):
                n = len(us)
                for s in range(n + 2):
                    if s < n:
                        self.scores(us[s])
                        self.probs(us[s])
                    if 1 <= s <= n:
                        self.turn(us[s - 1])
                    if s >= 2:
                        self.values(us[s - 2])

        def to_h(k, free, marks):
            def sink(b, m):
                hi = copy(act, hH[:, k, :], ps[b][:, :], m, *free)
                lo = dve.do(lambda e: e.tensor_tensor(hL[:, k, :], ps[b][:, :], hH[:, k, :].bitcast(F32),
                                                      ALU.subtract), hi)
                bank_free[b] = lo
                marks[k] = [hi, lo]
            return sink

        def pair_units(nh, lay, q, k, v, kw, sink):
            us = []
            for h in range(nh):
                r = slice(64 * (h % 2), 64 * (h % 2) + 64)
                u = {"lay": lay, "q": q(h, r), "k": k(h, r), "v": v(h), "rows": r, "bank": None}
                u.update(kw(h))
                if h % 2:
                    u["pair"] = us[-1]
                    u["sink"] = sink(h // 2)
                us.append(u)
            return us

        def mem_kv(c, layer, fen, mk_t, mv_t):
            cc = ExitStack()
            mr = sbt(cc, f"mr{layer}", [128, 8, 256])
            mH = sbt(cc, f"mH{layer}", [128, 8, 256], F32R)
            mL = sbt(cc, f"mL{layer}", [128, 8, 256], F32R)
            ld = act.load(lambda e: e.dma_start(mr[:, :, :], memt.rearrange("p (k t) -> p k t", k=8)),
                          s_c[2], 16 * (layer + 1), *fen)
            marks = []
            for k in range(0, 8, 2):
                hi = copy(act, mH[:, k:k + 2, :], mr[:, k:k + 2, :], ld, *fen)
                lo = pool.do(lambda e, k=k: e.tensor_tensor(mL[:, k:k + 2, :], mr[:, k:k + 2, :],
                                                            mH[:, k:k + 2, :].bitcast(F32), ALU.subtract), hi, *fen)
                marks += [[hi, lo], [hi, lo]]

            got = []

            def sink(m, b, mk):
                bank_free[b] = copy(act, mk_t[:, m, :], ps[b][:, 0:256], mk, *fen)
                got.append(bank_free[b])

            linear_fm(1, mH, mL, marks, sink, N=256)
            act.wait(*fen)
            got += linear_tm(1, mH, mL, marks, mv_t, ntt=2)
            cc.close()
            return got

        def mem_attention(c, tag, qm, qmm, mk_t, mv_t, kvm, free, marks):
            S = Soft(c, tag)
            us = pair_units(
                4, FULL256,
                lambda h, r: (lambda t: qm[r, h // 2, t * 128:t * 128 + 128]),
                lambda h, r: (lambda L: mk_t[r, h // 2, 0:256]),
                lambda h: (lambda j: mv_t[:, j, 64 * h:64 * h + 64]),
                lambda h: {"qk": qmm + kvm, "vm": kvm},
                lambda tile: to_h(6 + tile, free, marks))
            return S, us

        def ffn(tag, h, conv):
            c = ExitStack()
            fen = fence()
            for x in (act, dve, pool):
                x.wait(*fen)
            fH = sbt(c, f"fH{tag}", [128, 12, 512], F32R)
            fL = sbt(c, f"fL{tag}", [128, 12, 512], F32R)
            Y = [sbt(c, f"Y{tag}{i}", [128, 512]) for i in range(4)]
            Z = [sbt(c, f"Z{tag}{i}", [128, 512]) for i in range(2)]
            yfree = [None] * 4
            zfree = [None] * 2
            ffree = [None]
            for half, (j0, j1, ks) in enumerate(((0, 6, (4, 4, 4)), (6, 11, (4, 4, 2)))):
                fm = {}
                ym = {}

                def gsink(m, b, mk):
                    y = Y[m % 4]
                    if conv is None:
                        s = act.do(lambda e: e.activation(y[:, :], ps[b][:, :], ACT.Silu), mk, yfree[m % 4])
                        bank_free[b] = s
                    else:
                        fw, fb = conv
                        s = act.do(lambda e: e.activation(y[:, :], ps[b][:, :], ACT.Identity,
                                                          bias=col(fb, m), scale=col(fw, 44 + m)),
                                   mk, yfree[m % 4])
                        for d, w in ((1, 22 + m), (2, m)):
                            s = dve.do(lambda e, d=d, w=w: e.scalar_tensor_tensor(
                                out=y[:, d:512], in0=ps[b][:, 0:512 - d], scalar=col(fw, w),
                                in1=y[:, d:512], op0=ALU.mult, op1=ALU.add), s)
                        bank_free[b] = s
                        s = act.do(lambda e: e.activation(y[:, :], y[:, :], ACT.Silu), s)
                    ym[m] = s

                def usink(m, b, mk):
                    y, z, k = Y[m % 4], Z[m % 2], m - 2 * j0
                    bank_free[b] = yfree[m % 4] = s = dve.do(lambda e: e.tensor_tensor(
                        z[:, :], ps[b][:, :], y[:, :], ALU.mult), mk, ym[m], zfree[m % 2])
                    hi = copy(act, fH[:, k, :], z[:, :], s, ffree[0])
                    eng = pool if m % 2 else dve
                    lo = eng.do(lambda e: e.tensor_tensor(fL[:, k, :], z[:, :], fH[:, k, :].bitcast(F32),
                                                          ALU.subtract), hi, ffree[0])
                    zfree[m % 2] = lo
                    fm[k] = [hi, lo]

                for j in range(j0, j1):
                    linear_fm(1, hH, hL, h, gsink, m0=2 * j)
                    linear_fm(1, hH, hL, h, usink, m0=2 * j)
                res = residual(half == 1)
                for mg in range(2):
                    bs = [bank() for _ in range(4)]
                    k0 = 0
                    for gi, nk in enumerate(ks):
                        n, _, _, ncl, (wh, wl) = take()
                        for mi in range(4):
                            b = bs[mi]
                            pe.wait(bank_free[b])
                            for kk in range(nk):
                                pe.wait(*fm[k0 + kk])
                                for i, (w, x) in enumerate(((wh, fH), (wh, fL), (wl, fH))):
                                    f = (lambda e, b=b, w=w, x=x, k=k0 + kk, kk=kk, mi=mi, i=i, gi=gi, nk=nk: e.matmul(
                                        ps[b][:, :], w[:, kk, mi * 128:mi * 128 + 128], x[:, k, :],
                                        start=(gi == 0 and kk == 0 and i == 0),
                                        stop=(gi == len(ks) - 1 and kk == nk - 1 and i == 2)))
                                    if kk == nk - 1 and i == 2:
                                        mk = pe.do(f)
                                    else:
                                        pe.go(f)
                            if gi == len(ks) - 1:
                                res(4 * mg + mi, b, mk)
                        w_free[n] = mk
                        k0 += nk
                ffree[0] = mk
            c.close()

        for k in range(8):
            pass
        s_x = sem("s_x")
        xl = act.load(lambda e: e.dma_start(X[:, :, :], xt.rearrange("p (k t) -> p k t", k=8)), s_x, 16)
        A = ExitStack()
        q = sbt(A, "q", [128, 6, 512])
        kk_ = sbt(A, "k", [128, 6, 512])
        v = sbt(A, "v", [128, 4, 768])
        O = sbt(A, "O", [128, 6, 512])
        qm = sbt(A, "qm", [128, 2, 512])
        mkA = sbt(A, "mkA", [128, 2, 256])
        mvA = sbt(A, "mvA", [128, 2, 256])
        for k in range(8):
            square(k, xl)
            x_mark[k] = xl
        kvm = mem_kv(A, 0, [], mkA, mvA)
        rm = rstd(60, 1.0 / 1024)
        h = normed("mix0", rm, None)
        fen = fence()
        B = ExitStack()
        sel = sbt(B, "selA", [8, 8, 128])
        c_sel = act.load(lambda e: e.dma_start(sel[:, :, :], seld.rearrange("p (i c) -> p i c", i=8)),
                         s_c[3], 16, *fen)
        G = sbt(B, "G", [8, 512])
        G2 = [sbt(B, f"G2{i}", [4, 512]) for i in range(4)]
        colA = sbt(B, "colA", [128, 4, 8])
        rs = sbt(B, "rs", [128, 6, 16])
        Mb = [sbt(B, f"Mb{i}", [128, 512]) for i in range(2)]
        Eb = sbt(B, "Eb", [128, 1536])
        Pm = [sbt(B, f"Pm{i}", [128, 1536]) for i in range(2)]
        for x in (act, dve, pool):
            x.wait(*fen)

        gm = {}

        def gate_sink(m, b, mk):
            bank_free[b] = g = act.do(lambda e: e.activation(G[:, :], ps[b][0:8, :], ACT.Copy), mk)
            gm["G"] = g

        linear_fm(1, hH, hL, h, gate_sink)

        def gates_later():
            b = bank()
            m = pe.do(lambda e: e.matmul(ps[b][0:4, :], ident[0:8, 4:8], G[:, :], start=True, stop=True),
                      gm["G"], bank_free[b])
            z, t, a, mm = G2
            bank_free[b] = m = dve.do(lambda e: e.tensor_scalar(z[:, :], ps[b][0:4, :], col("gf", p=slice(0, 4)),
                                                                None, ALU.add), m)
            m1 = act.do(lambda e: e.activation(t[:, :], z[:, :], ACT.Abs), m)
            m1 = act.do(lambda e: e.activation(t[:, :], t[:, :], ACT.Exp, scale=-1.0), m1)
            m1 = act.do(lambda e: e.activation(t[:, :], t[:, :], ACT.Ln, bias=1.0), m1)
            m2 = dve.do(lambda e: e.tensor_scalar(z[:, :], z[:, :], -1.0, 0.0, ALU.mult, ALU.max), m1)
            m2 = dve.do(lambda e: e.tensor_tensor(t[:, :], t[:, :], z[:, :], ALU.add), m2)
            onem = dve.do(lambda e: e.memset(a[:, :], 1.0))
            m2 = dve.do(lambda e: e.tensor_tensor_scan(z[:, :], a[:, :], t[:, :], 0.0, ALU.mult, ALU.add), m2, onem)
            m3 = dve.do(lambda e: e.tensor_scalar(t[:, :], G[0:4, :], col("gi", p=slice(0, 4)), None, ALU.add), m2)
            m3 = dve.do(lambda e: e.tensor_tensor(t[:, :], t[:, :], z[:, :], ALU.add), m3)
            m4 = dve.do(lambda e: e.tensor_tensor_scan(mm[:, :], a[:, :], t[:, :], 0.0, ALU.mult, ALU.max), m3)
            m5 = dve.do(lambda e: e.tensor_tensor(z[:, :], z[:, :], mm[:, :], ALU.subtract), m4)
            gm["rows"] = m4
            b2 = bank()
            pe.wait(bank_free[b2], m5)
            for i in range(4):
                pe.go(lambda e, i=i: e.transpose(ps[b2][:, 8 * i:8 * i + 4], t[:, i * 128:i * 128 + 128],
                                                 ident[0:4, 0:4]))
                m = pe.do(lambda e, i=i: e.transpose(ps[b2][:, 8 * i + 4:8 * i + 8], z[:, i * 128:i * 128 + 128],
                                                     ident[0:4, 0:4]))
            bank_free[b2] = gm["col"] = copy(dve, colA[:, :, :],
                                             ps[b2][:, 0:32].rearrange("p (i c) -> p i c", i=4), m)

        qmm = []

        def qm_sink(dst, lst, scale=None, eng=None):
            def sink(m, b, mk):
                bank_free[b] = copy(eng or act, dst[:, m, :], ps[b][:, :], mk, scale=scale)
                lst.append(bank_free[b])
            return sink

        deferred.append(gates_later)
        linear_fm(1, hH, hL, h, qm_sink(qm, qmm, 0.125))
        qkm = {}

        def conv_sink(dst, base):
            def sink(m, b, mk):
                y = dst[:, m, :]
                s = act.do(lambda e: e.activation(y, ps[b][:, :], ACT.Identity, bias=col("cb", base + m),
                                                  scale=col("cw", 36 + base + m)), mk)
                for d in (1, 2, 3):
                    s = dve.do(lambda e, d=d: e.scalar_tensor_tensor(
                        out=dst[:, m, d:512], in0=ps[b][:, 0:512 - d], scalar=col("cw", 12 * (3 - d) + base + m),
                        in1=dst[:, m, d:512], op0=ALU.mult, op1=ALU.add), s)
                bank_free[b] = s
                qkm[(base, m)] = act.do(lambda e: e.activation(y, y, ACT.Silu), s)
            return sink

        linear_fm(3, hH, hL, h, conv_sink(q, 0))
        linear_fm(3, hH, hL, h, conv_sink(kk_, 6))
        vm = linear_tm(3, hH, hL, h, v)
        om = {}

        def o_sink(m, b, mk):
            bank_free[b] = om[m] = act.do(lambda e: e.activation(O[:, m, :], ps[b][:, :], ACT.Sigmoid), mk)

        linear_fm(3, hH, hL, h, o_sink)
        h_read = pe.last()

        SC = 192.0 ** -0.5
        JL = [(0, 512, 0, 0), (1, 384, 1, 0), (3, 128, 1, 384), (2, 256, 2, 0)]
        bd = bank(True)
        pe.wait(bank_free[bd])
        mbf = [None, None]
        pf = [None, None]
        eb_free = [None]
        numm = {}
        hs = {}

        def pieces(hd):
            t = 3 * (hd // 2)
            if hd % 2 == 0:
                return [(t, slice(0, 128), 192 * hd, 128), (t + 1, slice(0, 64), 192 * hd + 128, 64)]
            return [(t + 2, slice(0, 128), 192 * hd + 64, 128), (t + 1, slice(64, 128), 192 * hd, 64)]

        def m_scores(hd):
            bm = bank()
            m = pe.do(lambda e: e.matmul(ps[bm][:, :], sel[0:4, hd, :], G2[3][:, :], start=True, stop=True),
                      gm["rows"], c_sel, bank_free[bm])
            i = hd % 2
            bank_free[bm] = mb = copy(act, Mb[i][:, :], ps[bm][:, :], m, mbf[i])
            bs = [bank() for _ in range(3)]
            hs[hd] = {"b": bs, "s": {}}
            for j, L, bi, off in JL:
                pe.wait(bank_free[bs[bi]], *[qkm[x] for x in qkm])
                for n, (t, r, _, _) in enumerate(pieces(hd)):
                    f = (lambda e, j=j, L=L, b=bs[bi], off=off, t=t, r=r, n=n: e.matmul(
                        ps[b][:, off:off + L], kk_[r, t, j * 128:j * 128 + 128], q[r, t, j * 128:512],
                        start=(n == 0), stop=(n == 1)))
                    if n:
                        hs[hd]["s"][bi] = pe.do(f)
                    else:
                        pe.go(f)
            P = Pm[i]
            for j, L, bi, off in JL:
                o = bi * 512 + off
                m = dve.do(lambda e, j=j, o=o, L=L: e.tensor_scalar(
                    Eb[:, o:o + L], Mb[i][:, j * 128:512], colA[:, j, hd:hd + 1], 0.0,
                    ALU.subtract, ALU.max), mb, gm["col"], eb_free[0])
            mbf[i] = m
            m = act.do(lambda e: e.activation(Eb[:, 0:1280], Eb[:, 0:1280], ACT.Exp, scale=-1.0), m)
            for j, L, bi, off in JL:
                o = bi * 512 + off
                b = bs[bi]
                y = dve.do(lambda e, o=o, L=L, b=b, off=off: e.scalar_tensor_tensor(
                    out=P[:, o:o + L], in0=ps[b][:, off:off + L], scalar=SC, in1=Eb[:, o:o + L],
                    op0=ALU.mult, op1=ALU.mult), m, hs[hd]["s"][bi], pf[i])
                bank_free[b] = y
            eb_free[0] = y
            for j, L, bi, off in JL:
                o = bi * 512 + off
                z = pool.do(lambda e, o=o: e.affine_select(
                    out=P[:, o:o + 128], in_=P[:, o:o + 128], compare_op=ALU.is_ge, fill=0.0, base=0,
                    pattern=[[1, 128]], channel_multiplier=-1), y)
            hs[hd]["P"] = z

        nb = {}

        def m_values(hd):
            P = Pm[hd % 2]
            pos = {j: bi * 512 + off for j, L, bi, off in JL}
            pe.wait(hs[hd]["P"], *vm)
            for i in range(4):
                for j in range(i + 1):
                    o = pos[j] + (i - j) * 128
                    f = (lambda e, i=i, j=j, o=o: e.matmul(
                        ps[bd][:, hd * 4 + i:hd * 4 + i + 1], P[:, o:o + 128], ones[:, 0:1],
                        start=(j == 0), stop=(j == i)))
                    if i == 3 and j == 3:
                        pe.do(f)
                    else:
                        pe.go(f)
            for t, r, c0, w in pieces(hd):
                if t not in nb:
                    nb[t] = bank(w == 64)
                    pe.wait(bank_free[nb[t]])
                b = nb[t]
                for j in range(4):
                    o = pos[j]
                    f = (lambda e, b=b, j=j, r=r, c0=c0, w=w, o=o: e.matmul(
                        ps[b][r, j * 128:512], v[:, j, c0:c0 + w], P[:, o:o + 512 - j * 128],
                        start=(j == 0), stop=(j == 3)))
                    if j == 3:
                        mk = pe.do(f)
                    else:
                        pe.go(f)
                m = copy(act, q[r, t, :], ps[b][r, :], mk)
                numm[(t, r.start)] = bank_free[b] = m
                if r.start == 64:
                    held.discard(b)
                si = t % 2
                s2 = dve.do(lambda e, b=b, r=r, t=t, si=si: e.tensor_tensor(
                    sq[si][r, :], q[r, t, :], q[r, t, :], ALU.mult), m, sq_free[si])
                numm[("s", hd, t)] = s2
                deferred.append(lambda t=t, r=r, si=si, s2=s2, w=w: sums(hd, t, r, si, s2, w))
            pf[hd % 2] = mk

        def sums(hd, t, r, si, s2, w):
            o = 16 + 32 * (0 if w == 128 else 1) + hd * 4
            for i in range(4):
                m = pe.do(lambda e, i=i: e.matmul(ps[bd][:, o + i:o + i + 1], sq[si][r, i * 128:i * 128 + 128],
                                                  ones[r, 0:1], start=True, stop=True), s2)
            sq_free[si] = m
            gm["sums"] = m

        mix = [None] * 8
        m_scores(0)
        for hd in range(4):
            if hd < 3:
                m_scores(hd + 1)
            m_values(hd)
            run_deferred()
        md = gm["sums"]
        den, d2, s1, s2_, fac, em = (rs[:, i, :] for i in range(6))
        m0 = act.do(lambda e: e.activation(em.rearrange("p (h i) -> p i h", h=4), colA[:, :, 4:8], ACT.Exp),
                    gm["col"])
        m1 = act.do(lambda e: e.activation(den, ps[bd][:, 0:16], ACT.Abs), md)
        m1 = dve.do(lambda e: e.tensor_tensor(den, den, em, ALU.max), m0, m1)
        m2 = dve.do(lambda e: e.tensor_copy(s1, ps[bd][:, 16:32]), md)
        m2 = dve.do(lambda e: e.tensor_tensor(s1, s1, ps[bd][:, 48:64], ALU.add), m2)
        bank_free[bd] = m2
        held.discard(bd)
        m1 = dve.do(lambda e: e.scalar_tensor_tensor(out=d2, in0=den, scalar=1e-6, in1=den, op0=ALU.mult,
                                                     op1=ALU.mult), m1)
        m2 = dve.do(lambda e: e.scalar_tensor_tensor(out=s1, in0=s1, scalar=1.0 / 192, in1=d2, op0=ALU.mult,
                                                     op1=ALU.add), m1, m2)
        m2 = dve.do(lambda e: e.tensor_scalar(s1, s1, 1e-34, 1e35, ALU.max, ALU.min), m2)
        m2 = act.do(lambda e: e.activation(s2_, s1, ACT.Sqrt), m2)
        facm = dve.do(lambda e: e.reciprocal(fac, s2_), m2)
        fb = {}
        for hd in range(4):
            dm = None
            for i in range(4):
                dm = dve.do(lambda e, i=i, hd=hd: e.tensor_scalar(
                    diag[:, i * 128:i * 128 + 128], ident, fac[:, hd * 4 + i:hd * 4 + i + 1], None, ALU.mult),
                    facm, diag_free[0])
            for t, r, _, w in pieces(hd):
                if t not in fb:
                    fb[t] = bank(w == 64)
                    pe.wait(bank_free[fb[t]])
                diag_free[0] = fm_ = pe.do(lambda e, t=t, r=r, w=w: e.matmul(
                    ps[fb[t]][r, :], ones[:, 0:w], diag[:, :], start=True, stop=True), dm)
                fb[(t, r.start)] = fm_
            done = {0: [], 1: [0, 1], 2: [], 3: [3, 4]}[hd] + ([2] if hd == 1 else []) + ([5] if hd == 3 else [])
            for t in done:
                ms = [fb[x] for x in fb if isinstance(x, tuple) and x[0] == t]
                nm = [numm[x] for x in numm if x[0] == t]
                m = dve.do(lambda e, t=t: e.scalar_tensor_tensor(
                    out=q[:, t, :], in0=q[:, t, :], scalar=col("hg", t), in1=ps[fb[t]][:, :],
                    op0=ALU.mult, op1=ALU.mult), ms, nm)
                bank_free[fb[t]] = m
                held.discard(fb[t])
                m = dve.do(lambda e, t=t: e.tensor_tensor(q[:, t, :], q[:, t, :], O[:, t, :], ALU.mult), m, om[t])
                mix[t] = list(split(q[:, t, :], m, t, h_read))
        B.close()
        fen = fence()
        for x in (act, dve, pool):
            x.wait(*fen)
        C = ExitStack()
        S, us = mem_attention(C, "mA", qm, qmm, mkA, mvA, kvm, [h_read], mix)
        S.run(us)
        C.close()
        A.close()
        linear_fm(4, hH, hL, mix, residual(True))

        def dump(src, mark):
            o = out.rearrange("p (k t) -> p k t", k=8)
            state["stop"] = True
            return sp.load(lambda e: e.dma_start(o, src), s_out, 16, *mark)

        s_out = sem("s_out")

        def body():
            if stop == "A1":
                return dump(X[:, :, :], x_mark)
            rm = rstd(60, 1.0 / 1024)
            h = normed("ffn0", rm, pe.last())
            ffn("a", h, ("fw0", "fb0"))
            if stop == "A":
                return dump(X[:, :, :], x_mark)
            rm = rstd(60, 1.0 / 1024)
            h = normed("kv", rm, pe.last())
            fen = fence()
            for x in (act, dve, pool):
                x.wait(*fen)
            A = ExitStack()
            k = sbt(A, "kB", [128, 6, 512])
            q = sbt(A, "qB", [128, 6, 512])
            v = sbt(A, "vB", [128, 4, 768])
            qm = sbt(A, "qmB", [128, 2, 512])
            mk_t = sbt(A, "mkB", [128, 2, 256])
            mv_t = sbt(A, "mvB", [128, 2, 256])
            km, qmk, qmm = [], [], []
            linear_fm(3, hH, hL, h, qm_sink(k, km))
            vm = linear_tm(3, hH, hL, h, v)
            h_read = pe.last()
            h = normed("mix1", rm, h_read)
            kvm = mem_kv(A, 1, fence(), mk_t, mv_t)
            linear_fm(1, hH, hL, h, qm_sink(qm, qmm, 0.125))
            linear_fm(3, hH, hL, h, qm_sink(q, qmk, 0.125))
            h_read = pe.last()
            fen = fence()
            for x in (act, dve, pool):
                x.wait(*fen)
            C = ExitStack()
            bias = [sbt(C, f"bias{i}", [128, 512]) for i in range(3)]
            s_b = [sem(f"s_b{i}") for i in range(3)]
            S = Soft(C, "B")
            mix = [None] * 8
            bmm = {}
            bfree = [None] * 3

            def load_bias(h):
                i = h % 3
                l = act.load(lambda e: e.dma_start(bias[i][:, :], biasd[:, h * 512:h * 512 + 512]), s_b[i],
                             16 * (h // 3 + 1), bfree[i])
                bmm[h] = pool.do(lambda e: e.memset(bias[i][0:64, 448:512], NEG), l)

            def kw(h):
                return {"qk": qmk + km, "vm": vm, "bias": lambda L: bias[h % 3][:, 512 - L:512], "h": h}

            us = pair_units(
                12, CAUSAL,
                lambda h, r: (lambda t: q[r, h // 2, t * 128:t * 128 + 128]),
                lambda h, r: (lambda L: k[r, h // 2, 0:L]),
                lambda h: (lambda j: v[:, j, 64 * h:64 * h + 64]),
                kw, lambda tile: to_h(tile, [h_read], mix))
            us += pair_units(
                4, FULL256,
                lambda h, r: (lambda t: qm[r, h // 2, t * 128:t * 128 + 128]),
                lambda h, r: (lambda L: mk_t[r, h // 2, 0:256]),
                lambda h: (lambda j: mv_t[:, j, 64 * h:64 * h + 64]),
                lambda h: {"qk": qmm + kvm, "vm": kvm},
                lambda tile: to_h(6 + tile, [h_read], mix))
            n = len(us)
            for hh in range(2):
                load_bias(hh)
            for s in range(n + 2):
                if s < n:
                    if s < 12:
                        us[s]["bm"] = [bmm[s]]
                    S.scores(us[s])
                    S.probs(us[s])
                    if s < 12:
                        bfree[s % 3] = us[s]["pm"]
                    if s + 2 < 12:
                        load_bias(s + 2)
                if 1 <= s <= n:
                    S.turn(us[s - 1])
                if s >= 2:
                    S.values(us[s - 2])
            C.close()
            A.close()
            linear_fm(4, hH, hL, mix, residual(True))
            rm = rstd(60, 1.0 / 1024)
            h = normed("ffn1", rm, pe.last())
            ffn("b", h, ("fw1", "fb1"))
            if stop == "B":
                return dump(X[:, :, :], x_mark)
            rm = rstd(60, 1.0 / 1024)
            for kx in range(8):
                m = dve.do(lambda e, kx=kx: e.scalar_tensor_tensor(
                    out=X[:, kx, :], in0=X[:, kx, :], scalar=col("final", kx), in1=Rsb[:, :],
                    op0=ALU.mult, op1=ALU.mult), rm, x_mark[kx])
                x_mark[kx] = m
                square(kx, m)
            r_free[0] = m
            rm = rstd(61, 1.0 / 1024)
            h = normed("n1", rm, pe.last())
            fen = fence()
            for x in (act, dve, pool):
                x.wait(*fen)
            A = ExitStack()
            dq = sbt(A, "dq", [128, 4, 512])
            dk = sbt(A, "dk", [128, 4, 512])
            fq = sbt(A, "fq", [128, 4, 512])
            fk = sbt(A, "fk", [128, 4, 512])
            dv = sbt(A, "dv", [128, 4, 512])
            fv = sbt(A, "fv", [128, 4, 512])
            ncum = sbt(A, "ncum", [8, 512])
            B = ExitStack()
            RC = sbt(B, "RC", [128, 512])
            RS = sbt(B, "RS", [128, 512])
            U1 = [sbt(B, f"U1{i}", [128, 512]) for i in range(2)]
            U2 = [sbt(B, f"U2{i}", [128, 512]) for i in range(2)]
            Gf = sbt(B, "Gf", [128, 512])
            g3 = [sbt(B, f"g3{i}", [8, 512]) for i in range(3)]
            c_r1 = act.load(lambda e: e.dma_start(RC[:, :], rope[:, 0:512]), s_c[4], 16)
            c_r2 = act.load(lambda e: e.dma_start(RS[:, :], rope[:, 512:1024]), s_c[5], 16)
            fgm = {}

            def fg_sink(m, b, mk):
                bank_free[b] = fgm["G"] = act.do(lambda e: e.activation(Gf[96:128, :], ps[b][96:128, :], ACT.Copy), mk)

            def fg_later():
                b = bank()
                m = pe.do(lambda e: e.matmul(ps[b][0:8, :], ident[96:128, 120:128], Gf[96:128, :],
                                             start=True, stop=True), fgm["G"], bank_free[b])
                z, t, a = g3
                bank_free[b] = m = dve.do(lambda e: e.tensor_scalar(z[:, :], ps[b][0:8, :], col("bf", p=slice(0, 8)),
                                                                    None, ALU.add), m)
                m1 = act.do(lambda e: e.activation(t[:, :], z[:, :], ACT.Abs), m)
                m1 = act.do(lambda e: e.activation(t[:, :], t[:, :], ACT.Exp, scale=-1.0), m1)
                m1 = act.do(lambda e: e.activation(t[:, :], t[:, :], ACT.Ln, bias=1.0), m1)
                m2 = dve.do(lambda e: e.tensor_scalar(z[:, :], z[:, :], -1.0, 0.0, ALU.mult, ALU.max), m1)
                m2 = dve.do(lambda e: e.tensor_tensor(t[:, :], t[:, :], z[:, :], ALU.add), m2)
                onem = dve.do(lambda e: e.memset(a[:, :], 1.0))
                fgm["n"] = dve.do(lambda e: e.tensor_tensor_scan(ncum[:, :], a[:, :], t[:, :], 0.0, ALU.mult,
                                                                 ALU.add), m2, onem)

            linear_fm(1, hH, hL, h, fg_sink)
            deferred.append(fg_later)
            lm = dve.do(lambda e: e.tensor_tensor(small[0:64, 8:10], col("lam", 0, 2, slice(0, 64)),
                                                  col("lam", 2, 2, slice(0, 64)), ALU.mult))
            bl = bank()
            lm = pe.do(lambda e: e.matmul(ps[bl][:, 0:2], ones[0:64, :], small[0:64, 8:10], start=True, stop=True),
                       lm, bank_free[bl])
            bank_free[bl] = lm = act.do(lambda e: e.activation(small[:, 10:12], ps[bl][:, 0:2], ACT.Exp), lm)
            lm = dve.do(lambda e: e.tensor_tensor(small[:, 12:13], small[:, 11:12], small[:, 10:11], ALU.subtract), lm)
            lam_m = dve.do(lambda e: e.tensor_scalar(small[:, 12:13], small[:, 12:13], -0.2, None, ALU.add), lm)
            u1f, u2f = [None] * 2, [None] * 2
            dqm, dkm = [], []

            def rope_sink(dst, lst, scale, cnt=[0]):
                def sink(m, b, mk):
                    i = cnt[0] % 2
                    cnt[0] += 1
                    bank_free[b] = a = copy(act, U1[i][:, :], ps[b][:, :], mk, u1f[i], scale=scale)

                    def later():
                        b2 = bank()
                        r = pe.do(lambda e: e.matmul(ps[b2][:, :], rotm, U1[i][:, :], start=True, stop=True),
                                  a, bank_free[b2])
                        x = dve.do(lambda e: e.tensor_tensor(U2[i][:, :], ps[b2][:, :], RS[:, :], ALU.mult),
                                   r, c_r2, u2f[i])
                        bank_free[b2] = x
                        y = pool.do(lambda e: e.tensor_tensor(dst[:, m, :], U1[i][:, :], RC[:, :], ALU.mult),
                                    a, c_r1)
                        u1f[i] = [r, y]
                        z = dve.do(lambda e: e.tensor_tensor(dst[:, m, :], dst[:, m, :], U2[i][:, :], ALU.add), x, y)
                        u2f[i] = z
                        lst.append(z)
                    deferred.append(later)
                return sink

            linear_fm(2, hH, hL, h, rope_sink(dq, dqm, 0.125))
            linear_fm(2, hH, hL, h, rope_sink(dk, dkm, 1.0))
            dvm = linear_tm(2, hH, hL, h, dv)
            fqm, fkm = [], []
            linear_fm(2, hH, hL, h, qm_sink(fq, fqm, 0.125))
            linear_fm(2, hH, hL, h, qm_sink(fk, fkm))
            fvm = linear_tm(2, hH, hL, h, fv)
            h_read = pe.last()
            B.close()
            fen = fence()
            for x in (act, dve, pool):
                x.wait(*fen)
            C = ExitStack()
            sel = sbt(C, "selC", [8, 8, 128])
            c_sel = act.load(lambda e: e.dma_start(sel[:, :, :], seld.rearrange("p (i c) -> p i c", i=8)),
                             s_c[6], 16)
            S = Soft(C, "C", 3)
            CB = [sbt(C, f"CB{i}", [128, 512]) for i in range(2)]
            od = tt
            mix = [None] * 8
            odf = tt_free
            post = []

            def od_sink(hd):
                def sink(b, m):
                    i = hd % 2
                    bank_free[b] = a = copy(act, od[i][:, :], ps[b][:, :], m, odf[i], scale=2.0 ** -40)
                    a = dve.do(lambda e: e.tensor_scalar(od[i][:, :], od[i][:, :], 2.0 ** 60, -2.0 ** 60,
                                                         ALU.min, ALU.max), a)
                    s = pool.do(lambda e: e.tensor_tensor(sq[i][:, :], od[i][:, :], od[i][:, :], ALU.mult),
                                a, sq_free[i])

                    def later():
                        b2 = bank()
                        pe.wait(bank_free[b2], s)
                        for t in range(4):
                            m = pe.do(lambda e, t=t: e.matmul(ps[b2][:, t:t + 1], sq[i][:, t * 128:t * 128 + 128],
                                                              ones[:, 0:1], start=True, stop=True))
                        sq_free[i] = m
                        ss = small[:, 16 + 8 * i:24 + 8 * i]
                        m = dve.do(lambda e: e.tensor_scalar(
                            ss[:, 0:4], ps[b2][:, 0:4], 1.0 / 128, 1e-5 * 2.0 ** -80, ALU.mult, ALU.add), m)
                        m = dve.do(lambda e: e.reciprocal(ss[:, 4:8], ss[:, 0:4]), m)
                        m = act.do(lambda e: e.activation(ss[:, 0:4], ss[:, 4:8], ACT.Sqrt, scale=0.64), m)
                        m = bank_free[b2] = dve.do(lambda e: e.scalar_tensor_tensor(
                            out=ss[:, 0:4], in0=ps[b2][:, 0:4], scalar=2.0 ** 48, in1=ss[:, 0:4],
                            op0=ALU.is_lt, op1=ALU.mult), m)
                        b3 = bank()
                        m = bcast(ss[:, 0:4], m, None, bnk=b3)
                        m = bank_free[b3] = dve.do(lambda e: e.scalar_tensor_tensor(
                            out=od[i][:, :], in0=od[i][:, :], scalar=col("sub"), in1=ps[b3][:, :],
                            op0=ALU.mult, op1=ALU.mult), m)
                        hi, lo = split(od[i][:, :], m, hd, h_read)
                        odf[i] = lo
                        mix[hd] = [hi, lo]
                    post.append(later)
                return sink

            us = []
            for hd in range(4):
                for mp in range(2):
                    r = slice(64 * mp, 64 * mp + 64)
                    u = {"lay": CAUSAL, "mask": mchunk,
                         "q": lambda t, r=r, hd=hd: dq[r, hd, t * 128:t * 128 + 128],
                         "k": lambda L, r=r, hd=hd: dk[r, hd, 0:L],
                         "qk": dqm + dkm, "vm": dvm, "rows": slice(0, 128), "bank": None}
                    if mp == 0:
                        u["part"] = True
                    else:
                        u["prev"] = us[-1]
                        u["neg"] = (small[:, 12:13], lam_m)
                        u["v"] = lambda j, hd=hd: dv[:, j, hd * 128:hd * 128 + 128]
                        u["sink"] = od_sink(hd)
                    us.append(u)
            cbm = {}
            cbf = [None] * 2

            def load_cb(h):
                i = h % 2
                b = bank()
                m = pe.do(lambda e: e.matmul(ps[b][:, :], sel[:, h, :], ncum[:, :], start=True, stop=True),
                          fgm["n"], c_sel, bank_free[b])
                bank_free[b] = cbm[h] = copy(act, CB[i][:, :], ps[b][:, :], m, cbf[i])

            us += pair_units(
                8, CAUSAL,
                lambda h, r: (lambda t: fq[r, h // 2, t * 128:t * 128 + 128]),
                lambda h, r: (lambda L: fk[r, h // 2, 0:L]),
                lambda h: (lambda j: fv[:, j, 64 * h:64 * h + 64]),
                lambda h: {"qk": fqm + fkm, "vm": fvm, "mask": mcaus, "bias": lambda L: CB[h % 2][:, 0:L]},
                lambda tile: to_h(4 + tile, [h_read], mix))
            n = len(us)
            for s in range(n + 2):
                if s < n:
                    if s >= 8:
                        us[s]["bm"] = [cbm[s - 8]]
                    S.scores(us[s])
                    S.probs(us[s])
                    if s >= 8:
                        cbf[(s - 8) % 2] = us[s]["pm"]
                    if 0 <= s - 7 < 8:
                        load_cb(s - 7)
                if 1 <= s <= n:
                    S.turn(us[s - 1])
                if s >= 2:
                    S.values(us[s - 2])
                if s >= n - 2:
                    while post:
                        post.pop(0)()
                elif s % 2 == 0 and post:
                    post.pop(0)()
            C.close()
            A.close()
            linear_fm(4, hH, hL, mix, residual(True))
            if stop == "C1":
                return dump(X[:, :, :], x_mark)
            rm = rstd(61, 1.0 / 1024)
            h = normed("n2", rm, pe.last())
            ffn("c", h, None)
            rm = rstd(61, 1.0 / 1024)
            o = out.rearrange("p (k t) -> p k t", k=8)
            for kx in range(8):
                m = dve.do(lambda e, kx=kx: e.scalar_tensor_tensor(
                    out=X[:, kx, :], in0=X[:, kx, :], scalar=col("nf", kx), in1=Rsb[:, :],
                    op0=ALU.mult, op1=ALU.mult), rm, x_mark[kx])
                if kx % 2:
                    last = sp.load(lambda e, kx=kx: e.dma_start(o[:, kx - 1:kx + 1, :], X[:, kx - 1:kx + 1, :]),
                                   s_out, 16 * (kx // 2 + 1), m)
            return last

        sp.wait(body())

        block = ctx.enter_context(nc.Block())

        @block.sync
        def _(e):
            sp.play(e)

        @block.scalar
        def _(e):
            act.play(e)

        @block.vector
        def _(e):
            dve.play(e)

        @block.gpsimd
        def _(e):
            pool.play(e)

        @block.tensor
        def _(e):
            pe.play(e)


def shape_constants():
    ident = np.eye(128, dtype=np.float32)
    ones = np.ones((128, 128), np.float32)
    chunk = np.zeros((128, 128), np.float32)
    chunk[0:64, 64:128] = NEG
    i = np.arange(128)
    causal = np.where(i[None, :] <= i[:, None], np.float32(0), np.float32(NEG)).astype(np.float32)
    rot = np.zeros((128, 128), np.float32)
    for b in (0, 64):
        for d in range(8):
            rot[b + d + 8, b + d] = -1.0
            rot[b + d, b + d + 8] = 1.0
    consts = np.concatenate([ident, ones, chunk, causal, rot], 1)
    inv = np.float32(500000.0) ** (-np.arange(0, 16, 2, dtype=np.float32) / np.float32(16))
    ang = np.arange(512, dtype=np.float32)[None, :] * inv.astype(np.float32)[:, None]
    C, S = np.ones((128, 512), np.float32), np.zeros((128, 512), np.float32)
    for b in (0, 8, 64, 72):
        C[b:b + 8] = np.cos(ang)
        S[b:b + 8] = np.sin(ang)
    sel = np.zeros((8, 8, 128), np.float32)
    for h in range(8):
        sel[h, h, :] = 1.0
    return consts, np.concatenate([C, S], 1), sel.reshape(8, 1024)


def kernel(_stop=None, **inputs):
    import concourse.bacc as _bacc
    from concourse.bass_utils import run_bass_kernel_spmd as _run

    z = {n: np.asarray(a) for n, a in inputs.items()}
    parts = []
    for name, idx, k0, nk, c0, ncl in plan():
        w = z[name] if idx is None else z[name][idx]
        w = w[k0 * 128:(k0 + nk) * 128, c0:c0 + ncl].reshape(nk, 128, ncl)
        parts.append(w.transpose(1, 0, 2).reshape(128, nk * ncl))
    wall = np.ascontiguousarray(np.concatenate(parts, 1))

    def pk(a):
        return np.asarray(a).reshape(-1, 128).T

    def short(a):
        a = np.asarray(a).reshape(-1, 1)
        return np.concatenate([a, np.zeros((128 - len(a), 1), np.float32)], 0)

    got = {
        "mix0": pk(z["norm_mix_g"][0]), "mix1": pk(z["norm_mix_g"][1]), "ffn0": pk(z["norm_ffn_g"][0]),
        "ffn1": pk(z["norm_ffn_g"][1]), "kv": pk(z["kv_norm_g"]), "final": pk(z["final_g"]),
        "n1": pk(z["norm1_g_2"][0]), "n2": pk(z["norm2_g_2"][0]), "nf": pk(z["normf_g_2"]),
        "cw": pk(z["a_conv_w"][0]), "cb": pk(z["a_conv_b"][0]), "hg": pk(z["a_head_g"][0]),
        "fw0": pk(z["ffn_conv_w"][0]), "fb0": pk(z["ffn_conv_b"][0]), "fw1": pk(z["ffn_conv_w"][1]),
        "fb1": pk(z["ffn_conv_b"][1]), "sub": pk(z["subln_g_2"][0]), "gi": short(z["a_gate_b"][0][0:4]),
        "gf": short(z["a_gate_b"][0][4:8]), "bf": short(z["b_f_2"][0]),
        "lam": np.concatenate([short(z[n][0]) for n in ("lam_q1_2", "lam_q2_2", "lam_k1_2", "lam_k2_2")], 1),
    }
    cols = np.ascontiguousarray(np.concatenate([got[n] for n in COLS], 1))
    t, c = np.arange(128)[:, None], np.arange(512)[None, :]
    idx = np.clip(t + 384 - c, -63, 128) + 63
    bias = np.ascontiguousarray(z["b_rel_bias"][0][:, idx].transpose(1, 0, 2).reshape(128, 12 * 512))
    consts, rope, sel = shape_constants()
    arrays = {
        "wall": wall, "xt": z["x"][0].T.reshape(8, 128, 512).transpose(1, 0, 2).reshape(128, 4096),
        "memt": z["mem"][0].T.reshape(8, 128, 256).transpose(1, 0, 2).reshape(128, 2048),
        "cols": cols, "bias": bias, "consts": consts, "rope": rope, "sel": sel,
    }
    arrays = {n: np.ascontiguousarray(a) for n, a in arrays.items()}
    nc = _bacc.Bacc("TRN2", target_bir_lowering=False, num_devices=1)
    args = [nc.dram_tensor("in_" + n, a.shape, F32, kind="ExternalInput").ap() for n, a in arrays.items()]
    args.append(nc.dram_tensor("out_y", (128, 4096), F32, kind="ExternalOutput").ap())
    program(nc, *args, stop=_stop)
    r = _run(nc, [{"in_" + n: a for n, a in arrays.items()}], core_ids=[0])
    y = np.asarray(r.results[0]["out_y"])
    return np.ascontiguousarray(y.reshape(128, 8, 512).transpose(1, 0, 2).reshape(1024, 512).T.reshape(1, 512, 1024))
```

```python
from contextlib import ExitStack

import numpy as np
import concourse.bass as bass
from concourse import mybir

F32 = mybir.dt.float32
F32R = mybir.dt.float32r
ALU = mybir.AluOpType
ACT = mybir.ActivationFunctionType
AX = mybir.AxisListType

NEG = -1e30
NT = 4
DFF = 2816
SLOT = 2048
NRAW = 2
NCV = 2
CAUSAL = [(3, 512, 0, 0), (2, 384, 1, 0), (0, 128, 1, 384), (1, 256, 2, 0)]
FULL256 = [(0, 256, 0, 0), (1, 256, 0, 256), (2, 256, 1, 0), (3, 256, 1, 256)]


def ffn_plan(up, upo, gate, gateo, down, idx):
    out = []
    for j0, j1, ks in ((0, 6, ((0, 4), (4, 4), (8, 4))), (6, 11, ((12, 4), (16, 4), (20, 2)))):
        for j in range(j0, j1):
            out.append((gate, idx, 0, 8, gateo + 256 * j, 256))
            out.append((up, idx, 0, 8, upo + 256 * j, 256))
        for mg in range(2):
            for k0, nk in ks:
                out.append((down, idx, k0, nk, 512 * mg, 512))
    return out


def plan():
    u = [("mem_w_kv", 0, 0, 8, 0, 256), ("mem_w_kv", 0, 0, 8, 256, 256)]
    u += [("a_w_in", 0, 0, 8, 3072, 128), ("a_w_in", 0, 0, 8, 3080, 256)]
    u += [("a_w_in", 0, 0, 8, 256 * j, 256) for j in (0, 1, 2, 3, 4, 5, 6, 7, 8, 9, 10, 11)]
    u += [("a_w_out", 0, 0, 8, 256 * j, 256) for j in range(4)]
    u += ffn_plan("ffn_w_up", 0, "ffn_w_up", DFF, "ffn_w_down", 0)
    u += [("w_kv", None, 0, 8, 256 * j, 256) for j in range(6)]
    u += [("mem_w_kv", 1, 0, 8, 0, 256), ("mem_w_kv", 1, 0, 8, 256, 256)]
    u += [("b_w_in", 0, 0, 8, 256 * j, 256) for j in (3, 0, 1, 2)]
    u += [("b_w_out", 0, 0, 8, 256 * j, 256) for j in range(4)]
    u += ffn_plan("ffn_w_up", 0, "ffn_w_up", DFF, "ffn_w_down", 1)
    u += [("w_in_2", 0, 0, 8, 2952, 128)]
    u += [("w_in_2", 0, 0, 8, 256 * j, 256) for j in range(12)]
    u += [("w_out_2", 0, 0, 8, 256 * j, 256) for j in range(4)]
    u += ffn_plan("w_up_2", 0, "w_gate_2", 0, "w_down_2", 0)
    return u


def columns():
    at, out = 0, {}
    for name, n in [("mix0", 8), ("mix1", 8), ("ffn0", 8), ("ffn1", 8), ("kv", 8), ("final", 8),
                    ("n1", 8), ("n2", 8), ("nf", 8), ("cw", 48), ("cb", 12), ("hg", 6),
                    ("fw0", 66), ("fb0", 22), ("fw1", 66), ("fb1", 22), ("sub", 1), ("gi", 1), ("gf", 1),
                    ("bf", 1), ("lam", 4)]:
        out[name] = (at, n)
        at += n
    return out, at


COLS, NCOLS = columns()


class Lane:

    def __init__(self, sem):
        self.sem, self.q, self.n, self.seen = sem, [], 0, {}

    def wait(self, *marks):
        for m in marks:
            if m is None:
                continue
            if isinstance(m, list):
                self.wait(*m)
                continue
            sem, v = m
            if self.seen.get(sem.name, 0) < v:
                self.seen[sem.name] = v
                self.q.append(lambda e, sem=sem, v=v: e.wait_ge(sem, v))

    def do(self, fn, *marks):
        self.wait(*marks)
        self.n += 1
        self.q.append(lambda e: fn(e).then_inc(self.sem, 1))
        return (self.sem, self.n)

    def go(self, fn, *marks):
        self.wait(*marks)
        self.q.append(fn)

    def load(self, fn, sem, value, *marks):
        self.wait(*marks)
        self.q.append(lambda e: fn(e).then_inc(sem, 16))
        return (sem, value)

    def last(self):
        return (self.sem, self.n) if self.n else None

    def play(self, e):
        for f in self.q:
            f(e)


def program(nc, wall, xt, memt, colsd, biasd, consts, rope, seld, out, stop=None):
    ctx = ExitStack()
    with ctx:
        def sem(name):
            return ctx.enter_context(nc.semaphore(name))

        def sbt(c, name, shape, dt=F32):
            return c.enter_context(nc.sbuf_tensor(name, shape, dt))

        pe, act, dve, pool, sp = (Lane(sem(n)) for n in ("s_pe", "s_act", "s_dve", "s_pool", "s_sp"))

        def fence():
            return [x.last() for x in (pe, act, dve, pool)]

        ps = [ctx.enter_context(nc.psum_tensor(f"ps{i}", [128, 512], F32)) for i in range(8)]
        bank_free = [None] * 8
        bank_at = [0]

        held = set()

        def bank(hold=False):
            while bank_at[0] % 8 in held:
                bank_at[0] += 1
            b = bank_at[0] % 8
            bank_at[0] += 1
            if hold:
                held.add(b)
            return b

        X = sbt(ctx, "X", [128, 8, 512])
        hH = sbt(ctx, "hH", [128, 8, 512], F32R)
        hL = sbt(ctx, "hL", [128, 8, 512], F32R)
        raw = [sbt(ctx, f"raw{i}", [128, SLOT]) for i in range(NRAW)]
        WH = [sbt(ctx, f"WH{i}", [128, SLOT], F32R) for i in range(NCV)]
        WL = [sbt(ctx, f"WL{i}", [128, SLOT], F32R) for i in range(NCV)]
        cols = sbt(ctx, "cols", [128, NCOLS])
        K = sbt(ctx, "K", [128, 5, 128])
        ident, ones, mchunk, mcaus, rotm = (K[:, i, :] for i in range(5))
        acc = sbt(ctx, "acc", [128, 512])
        sq = [sbt(ctx, f"sq{i}", [128, 512]) for i in range(2)]
        diag = sbt(ctx, "diag", [128, 512])
        Rsb = sbt(ctx, "Rsb", [128, 512])
        tt = [sbt(ctx, f"tt{i}", [128, 512]) for i in range(2)]
        small = sbt(ctx, "small", [128, 64])

        def col(name, i=0, n=1, p=slice(0, 128)):
            a = COLS[name][0] + i
            return cols[p, a:a + n]

        units = plan()
        woff = [0]
        for u in units:
            woff.append(woff[-1] + u[3] * u[5])
        s_raw = [sem(f"s_raw{i}") for i in range(NRAW)]
        w_lo = {}
        w_free = {}
        wst = {"load": 0, "conv": 0, "next": 0}
        state = {"stop": False}

        def w_load(n):
            size = woff[n + 1] - woff[n]
            r = n % NRAW
            return sp.load(lambda e: e.dma_start(raw[r][:, 0:size], wall[:, woff[n]:woff[n + 1]]),
                           s_raw[r], 16 * (n // NRAW + 1), w_lo.get(n - NRAW))

        def w_convert(n):
            size = woff[n + 1] - woff[n]
            loaded = w_load(n)
            r, c = n % NRAW, n % NCV
            half = size // 2
            for a, b in ((0, half), (half, size)):
                m = act.do(lambda e, a=a, b=b: e.activation(WH[c][:, a:b], raw[r][:, a:b], ACT.Copy),
                           loaded, w_free.get(n - NCV))
                lo = dve.do(lambda e, a=a, b=b: e.tensor_tensor(
                    WL[c][:, a:b], raw[r][:, a:b], WH[c][:, a:b].bitcast(F32), ALU.subtract), m)
            w_lo[n] = lo

        def take():
            n = wst["next"]
            wst["next"] += 1
            while wst["conv"] < min(n + 2, len(units)):
                w_convert(wst["conv"])
                wst["conv"] += 1
            pe.wait(w_lo[n])
            _, _, k0, nk, _, ncl = units[n]
            v = [WH[n % NCV][:, 0:nk * ncl].rearrange("p (k c) -> p k c", k=nk),
                 WL[n % NCV][:, 0:nk * ncl].rearrange("p (k c) -> p k c", k=nk)]
            return n, k0, nk, ncl, v

        deferred = []
        waiting = []
        norm_steps = []

        def run_deferred():
            while deferred:
                deferred.pop(0)()

        def tile_done(sink, *args):
            waiting.append(lambda: sink(*args))
            run_deferred()
            if norm_steps:
                norm_steps.pop(0)()
            if not norm_steps:
                while waiting:
                    waiting.pop(0)()

        def g_linear_fm(nunits, AH, AL, marks, sink, N=512, m0=0, order=None):
            m = m0
            for _ in range(nunits):
                n, _, nk, ncl, (wh, wl) = take()
                ks = order or list(range(nk))
                for c in range(0, ncl, 128):
                    b = bank()
                    pe.wait(bank_free[b])
                    o = ps[b][:, 0:N]
                    for k in ks:
                        pe.wait(marks[k])
                        ah, al, kx = (AH(k), AL(k), 0) if callable(AH) else (AH, AL, k)
                        for i, (w, x) in enumerate(((wh, ah), (wh, al), (wl, ah))):
                            f = (lambda e, o=o, w=w, x=x, k=k, kx=kx, c=c, i=i: e.matmul(
                                o, w[:, k, c:c + 128], x[:, kx, 0:N], start=(k == ks[0] and i == 0),
                                stop=(k == ks[-1] and i == 2)))
                            if k == ks[-1] and i == 2:
                                mk = pe.do(f)
                            else:
                                pe.go(f)
                    if c + 128 >= ncl:
                        w_free[n] = mk
                    tile_done(sink, m, b, mk)
                    m += 1
                    yield

        def g_linear_tm(nunits, AH, AL, marks, sink, ntt=4):
            for un in range(nunits):
                n, _, nk, ncl, (wh, wl) = take()
                for t0 in range(0, ntt, 2):
                    b = bank()
                    pe.wait(bank_free[b])
                    for t in (t0, t0 + 1):
                        o = ps[b][:, (t - t0) * 256:(t - t0) * 256 + 256]
                        for k in range(nk):
                            pe.wait(marks[k])
                            for i, (w, x) in enumerate(((wh, AH), (wl, AH), (wh, AL))):
                                f = (lambda e, o=o, w=w, x=x, k=k, t=t, i=i: e.matmul(
                                    o, x[:, k, t * 128:t * 128 + 128], w[:, k, :],
                                    start=(k == 0 and i == 0), stop=(k == nk - 1 and i == 2)))
                                if k == nk - 1 and i == 2:
                                    mk = pe.do(f)
                                else:
                                    pe.go(f)
                    if t0 + 2 >= ntt:
                        w_free[n] = mk
                    tile_done(sink, t0, un, b, mk)
                    yield

        def linear_fm(*args, **kw):
            for _ in g_linear_fm(*args, **kw):
                pass

        def linear_tm(*args, **kw):
            for _ in g_linear_tm(*args, **kw):
                pass

        def fill(gens, n):
            while gens and n > 0:
                try:
                    next(gens[0])
                    n -= 1
                except StopIteration:
                    gens.pop(0)

        def copy(eng, o, i, *marks, scale=None):
            if eng is act:
                return act.do(lambda e: e.activation(o, i, ACT.Copy, scale=1.0 if scale is None else scale),
                              *marks)
            return eng.do(lambda e: e.tensor_copy(o, i), *marks)

        acc_free = [None]
        sq_free = [None, None]
        x_mark = [None] * 8
        acc_mark = [None]

        def square(k, mark):
            if k == 0:
                acc_mark[0] = act.do(lambda e: e.activation(acc[:, :], X[:, 0, :], ACT.Square), mark, acc_free[0])
                return
            i = k % 2
            m = act.do(lambda e: e.activation(sq[i][:, :], X[:, k, :], ACT.Square), mark, sq_free[i])
            acc_mark[0] = sq_free[i] = pool.do(
                lambda e: e.tensor_tensor(acc[:, :], acc[:, :], sq[i][:, :], ALU.add), m, acc_mark[0])

        diag_free = [None]
        r_free = [None]

        def bcast(colap, mark, rows=slice(0, 128), bnk=None):
            ms = [mark, diag_free[0]]
            for i in range(4):
                d = dve.do(lambda e, i=i: e.tensor_scalar(diag[:, i * 128:i * 128 + 128], ident,
                                                          colap[:, i:i + 1], None, ALU.mult), *ms)
            n = rows.stop - rows.start
            diag_free[0] = pe.do(lambda e: e.matmul(ps[bnk][rows, :], ones[:, 0:n], diag[:, :],
                                                    start=True, stop=True), d, bank_free[bnk])
            return diag_free[0]

        R = {}

        def token_sums(src, mark, b, at):
            pe.wait(mark)
            for i in range(4):
                m = pe.do(lambda e, i=i: e.matmul(ps[b][:, at + i:at + i + 1], src[:, i * 128:i * 128 + 128],
                                                  ones[:, 0:1], start=True, stop=True))
            return m

        def rstd(eps):

            def first():
                b = bank()
                pe.wait(bank_free[b])
                acc_free[0] = m = token_sums(acc, acc_mark[0], b, 0)
                bank_free[b] = m = act.do(lambda e: e.activation(
                    small[:, 0:4], ps[b][:, 0:4], ACT.Sqrt, bias=small[:, eps:eps + 1], scale=1.0 / 1024), m)
                R["col"] = dve.do(lambda e: e.reciprocal(small[:, 4:8], small[:, 0:4]), m, act.last())

            def second():
                b = bank()
                m = bcast(small[:, 4:8], R["col"], bnk=b)
                bank_free[b] = R["m"] = copy(act, Rsb[:, :], ps[b][:, :], m, dve.last(), pool.last())

            norm_steps.extend([first, second])

        tt_free = [None, None]

        def split(src, mark, k, *free):
            hi = copy(act, hH[:, k, :], src, mark, *free)
            lo_eng = pool if k % 2 else dve
            lo = lo_eng.do(lambda e: e.tensor_tensor(hL[:, k, :], src, hH[:, k, :].bitcast(F32),
                                                     ALU.subtract), hi, *free)
            return hi, lo

        def scaled(k, g, free, marks):
            hi = act.do(lambda e: e.activation(hH[:, k, :], X[:, k, :], ACT.Copy, scale=g), x_mark[k], free)
            lo = dve.do(lambda e: e.scalar_tensor_tensor(
                out=hL[:, k, :], in0=X[:, k, :], scalar=g, in1=hH[:, k, :].bitcast(F32),
                op0=ALU.mult, op1=ALU.subtract), hi, free)
            marks[k] = [hi, lo]

        def residual(last, then=None, hold=None):
            def sink(m, b, mk):
                bank_free[b] = x_mark[m] = dve.do(lambda e: e.tensor_tensor(
                    X[:, m, :], X[:, m, :], ps[b][:, :], ALU.add), mk)
                if last:
                    if then:
                        then(m)
                    if m != hold:
                        square(m, x_mark[m])
            return sink

        def times_R(dst, src, *marks, scale=None, eng=None):
            rows = slice(0, 128) if scale is None or not isinstance(scale, tuple) else scale[1]
            sc = scale[0] if isinstance(scale, tuple) else scale
            if sc is None:
                return (eng or dve).do(lambda e: e.tensor_tensor(dst, src, Rsb[rows, :], ALU.mult),
                                       R["m"], *marks)
            return dve.do(lambda e: e.scalar_tensor_tensor(out=dst, in0=src, scalar=sc, in1=Rsb[rows, :],
                                                           op0=ALU.mult, op1=ALU.mult), R["m"], *marks)

        def v_sink(dst, got):
            def sink(t0, un, b, mk):
                for i in range(2):
                    m = act.do(lambda e, i=i: e.activation(
                        dst[:, t0 + i, 256 * un:256 * un + 256], ps[b][:, 256 * i:256 * i + 256], ACT.Copy,
                        scale=small[:, 4 + t0 + i:5 + t0 + i]), mk, R["col"])
                bank_free[b] = m
                got.append(m)
            return sink

        def R_sink(dst, got, scale=None):
            def sink(m, b, mk):
                bank_free[b] = x = times_R(dst[:, m, :], ps[b][:, :], mk, scale=scale)
                got.append(x)
            return sink

        s_c = [sem(f"s_c{i}") for i in range(8)]
        s_m = [sem(f"s_m{i}") for i in range(2)]
        c_cols = act.load(lambda e: e.dma_start(cols[:, :], colsd), s_c[0], 16)
        c_K = act.load(lambda e: e.dma_start(K[:, :, :], consts.rearrange("p (i c) -> p i c", i=5)), s_c[1], 16)
        eps6 = pool.do(lambda e: e.memset(small[:, 60:61], 1e-6))
        eps5 = pool.do(lambda e: e.memset(small[:, 61:62], 1e-5))
        c_mark = [c_cols, c_K, eps6, eps5]
        for x in (act, dve, pool):
            x.wait(eps5)

        class Soft:

            def __init__(self, c, tag, nP=2, width=1280):
                self.P = [sbt(c, f"P{tag}{i}", [128, width]) for i in range(nP)]
                self.PT = [sbt(c, f"PT{tag}{i}", [128, 4, 512]) for i in range(2)]
                self.st = sbt(c, f"st{tag}", [128, 4, 16])
                self.Pfree = [None] * nP
                self.PTfree = [None] * 2
                self.npt = 0
                self.n = 0

            def scores(self, u):
                u["i"] = self.n
                self.n += 1
                lay = u["lay"]
                bs = [bank() for _ in range(max(x[2] for x in lay) + 1)]
                u["b"] = bs
                u["sm"] = {}
                for t, L, bi, off in lay:
                    b = bs[bi]
                    msk = u.get("mask")
                    pe.wait(bank_free[b], *u["qk"])
                    f = (lambda e, t=t, L=L, b=b, off=off: e.matmul(
                        ps[b][:, off:off + L], u["q"](t), u["k"](L), start=True, stop=msk is None))
                    if msk is None:
                        u["sm"][bi] = pe.do(f)
                    else:
                        pe.go(f)
                        u["sm"][bi] = pe.do(lambda e, L=L, b=b, off=off: e.matmul(
                            ps[b][:, off + L - 128:off + L], ident, msk, start=False, stop=True))

            def probs(self, u):
                lay, i = u["lay"], u["i"]
                P = self.P[i % len(self.P)]
                u["P"] = P
                st = self.st[:, i % 4, :]
                pf = self.Pfree[i % len(self.P)]
                rd = {}
                for t, L, bi, off in lay:
                    b = u["b"][bi]
                    src, o = ps[b][:, off:off + L], bi * 512 + off
                    if "bias" in u:
                        m = dve.do(lambda e, t=t, src=src, o=o, L=L: e.tensor_tensor_reduce(
                            P[:, o:o + L], src, u["bias"](L), 1.0, -3e38, ALU.add, ALU.max,
                            st[:, t:t + 1]), u["sm"][bi], pf, *u.get("bm", []))
                        bank_free[b] = m
                    else:
                        m = dve.do(lambda e, t=t, src=src: e.tensor_reduce(
                            st[:, t:t + 1], src, AX.X, ALU.max), u["sm"][bi])
                    rd[t] = m
                m = dve.do(lambda e: e.tensor_scalar(st[:, 4:8], st[:, 0:4], -1.0, None, ALU.mult), m)
                for t, L, bi, off in lay:
                    b = u["b"][bi]
                    o = bi * 512 + off
                    src = P[:, o:o + L] if "bias" in u else ps[b][:, off:off + L]
                    x = act.do(lambda e, t=t, src=src, o=o, L=L: e.activation(
                        P[:, o:o + L], src, ACT.Exp, bias=st[:, 4 + t:5 + t],
                        accum_out=st[:, 8 + t:9 + t]), m, pf)
                    if "bias" not in u:
                        bank_free[b] = x
                u["xm"] = x

            def scale(self, u):
                lay, P, x = u["lay"], u["P"], u["xm"]
                st = self.st[:, u["i"] % 4, :]
                rc = dve.do(lambda e: e.reciprocal(st[:, 12:16], st[:, 8:12]), x)
                if u.get("neg") is not None:
                    nm, nmm = u["neg"]
                    rc = dve.do(lambda e: e.tensor_scalar(st[:, 12:16], st[:, 12:16], nm, None, ALU.mult),
                                rc, nmm)
                prev = u.get("prev")
                for t, L, bi, off in lay:
                    o = bi * 512 + off
                    if prev is None:
                        y = dve.do(lambda e, t=t, o=o, L=L: e.tensor_scalar(
                            P[:, o:o + L], P[:, o:o + L], st[:, 12 + t:13 + t], None, ALU.mult), rc)
                    else:
                        y = dve.do(lambda e, t=t, o=o, L=L: e.scalar_tensor_tensor(
                            out=P[:, o:o + L], in0=P[:, o:o + L], scalar=st[:, 12 + t:13 + t],
                            in1=prev["P"][:, o:o + L], op0=ALU.mult, op1=ALU.add), rc, prev["pm"])
                if prev is not None:
                    self.Pfree[prev["i"] % len(self.P)] = y
                u["pm"] = y

            def turn(self, u):
                if u.get("part"):
                    return
                lay = u["lay"]
                PT = self.PT[self.npt % 2]
                u["PT"] = PT
                u["ipt"] = self.npt
                ptf = self.PTfree[self.npt % 2]
                self.npt += 1
                bs = [bank() for _ in range(max(x[2] for x in lay) + 1)]
                mk = {}
                P = u["P"]
                for t, L, bi, off in lay:
                    b = bs[bi]
                    pe.wait(bank_free[b], u["pm"])
                    for j in range(L // 128):
                        f = (lambda e, b=b, o=off + j * 128, s=bi * 512 + off + j * 128: e.transpose(
                            ps[b][:, o:o + 128], P[:, s:s + 128], ident))
                        if j == L // 128 - 1:
                            mk[bi] = pe.do(f)
                        else:
                            pe.go(f)
                self.Pfree[u["i"] % len(self.P)] = mk[bi]
                out = []
                for t, L, bi, off in lay:
                    b = bs[bi]
                    eng = act if bi == 0 else dve
                    src = ps[b][:, off:off + L].rearrange("p (j t) -> p j t", t=128)
                    bank_free[b] = copy(eng, PT[:, 0:L // 128, t * 128:t * 128 + 128], src, mk[bi], ptf)
                    out.append(bank_free[b])
                u["tm"] = out

            def values(self, u):
                if u.get("part"):
                    return
                if u["bank"] is None:
                    u["bank"] = u["pair"]["bank"] if u.get("pair") else bank(not u.get("sink"))
                    if not u.get("pair"):
                        pe.wait(bank_free[u["bank"]])
                b, rows = u["bank"], u["rows"]
                pe.wait(*u["tm"])
                pe.wait(*u["vm"])
                nj = 2 if u["lay"] is FULL256 else 4
                for j in range(nj):
                    t0 = 0 if nj == 2 else j * 128
                    f = (lambda e, j=j, t0=t0: e.matmul(
                        ps[b][rows, t0:512], u["v"](j), u["PT"][:, j, t0:512],
                        start=(j == 0), stop=(j == nj - 1)))
                    if j == nj - 1:
                        m = pe.do(f)
                    else:
                        pe.go(f)
                self.PTfree[u["ipt"] % 2] = m
                if u.get("sink"):
                    held.discard(b)
                    u["sink"](b, m)

            def run(self, us, gens=(), per=0, before=None, after=None):
                n = len(us)
                for s in range(n + 2):
                    if s < n:
                        if before:
                            before(s)
                        self.scores(us[s])
                    if 1 <= s <= n:
                        self.scale(us[s - 1])
                    if s < n:
                        self.probs(us[s])
                        if after:
                            after(s)
                    fill(gens, per)
                    if 1 <= s <= n:
                        self.turn(us[s - 1])
                    if s >= 2:
                        self.values(us[s - 2])

        def to_parts(H, L, k, free, marks, km):
            def sink(b, m):
                hi = copy(act, H[:, k, :], ps[b][:, :], m, *free)
                lo = dve.do(lambda e: e.tensor_tensor(L[:, k, :], ps[b][:, :], H[:, k, :].bitcast(F32),
                                                      ALU.subtract), hi)
                bank_free[b] = lo
                marks[km] = [hi, lo]
            return sink

        def pair_units(nh, lay, q, k, v, kw, sink):
            us = []
            for h in range(nh):
                r = slice(64 * (h % 2), 64 * (h % 2) + 64)
                u = {"lay": lay, "q": q(h, r), "k": k(h, r), "v": v(h), "rows": r, "bank": None}
                u.update(kw(h))
                if h % 2:
                    u["pair"] = us[-1]
                    u["sink"] = sink(h // 2)
                us.append(u)
            return us

        def mem_load(cc, layer):
            mr = sbt(cc, f"mr{layer}", [128, 8, 256])
            mH = sbt(cc, f"mH{layer}", [128, 8, 256], F32R)
            mL = sbt(cc, f"mL{layer}", [128, 8, 256], F32R)
            mv = memt.rearrange("p (k t) -> p k t", k=8)
            lds = [act.load(lambda e, i=i: e.dma_start(mr[:, 4 * i:4 * i + 4, :], mv[:, 4 * i:4 * i + 4, :]),
                            s_m[i], 16 * (layer + 1)) for i in range(2)]
            return mr, mH, mL, lds

        def mem_kv(loaded, mk_t, mv_t):
            mr, mH, mL, lds = loaded
            fen = []
            marks = []
            for k in range(0, 8, 2):
                hi = copy(act, mH[:, k:k + 2, :], mr[:, k:k + 2, :], lds[k // 4])
                lo = pool.do(lambda e, k=k: e.tensor_tensor(mL[:, k:k + 2, :], mr[:, k:k + 2, :],
                                                            mH[:, k:k + 2, :].bitcast(F32), ALU.subtract), hi)
                marks += [[hi, lo], [hi, lo]]

            got = []

            def sink(m, b, mk):
                bank_free[b] = copy(act, mk_t[:, m, :], ps[b][:, 0:256], mk, *fen)
                got.append(bank_free[b])

            def vsink(t0, un, b, mk):
                bank_free[b] = copy(act, mv_t[:, t0:t0 + 2, :], ps[b][:, :].rearrange("p (t c) -> p t c", t=2),
                                    mk, *fen)
                got.append(bank_free[b])

            linear_fm(1, mH, mL, marks, sink, N=256)
            linear_tm(1, mH, mL, marks, vsink, ntt=2)
            return got

        def mem_units(qm, qmm, mk_t, mv_t, kvm, MH, ML, marks):
            return pair_units(
                4, FULL256,
                lambda h, r: (lambda t: qm[r, h // 2, t * 128:t * 128 + 128]),
                lambda h, r: (lambda L: mk_t[r, h // 2, 0:256]),
                lambda h: (lambda j: mv_t[:, j, 64 * h:64 * h + 64]),
                lambda h: {"qk": [qmm, kvm], "vm": kvm},
                lambda tile: to_parts(MH, ML, tile, [], marks, 6 + tile))

        def ffn(tag, h, conv, then=None, gain=None):
            c = ExitStack()
            fen = fence()
            for x in (act, dve, pool):
                x.wait(*fen)
            fH = sbt(c, f"fH{tag}", [128, 12, 512], F32R)
            fL = sbt(c, f"fL{tag}", [128, 12, 512], F32R)
            Y = [sbt(c, f"Y{tag}{i}", [128, 512]) for i in range(4)]
            Z = [sbt(c, f"Z{tag}{i}", [128, 512]) for i in range(2)]
            GG = [sbt(c, f"GG{tag}{i}", [128, 512]) for i in range(2)]
            gfree = [None] * 2
            yfree = [None] * 4
            zfree = [None] * 2
            ffree = [None]
            for half, (j0, j1, ks) in enumerate(((0, 6, (4, 4, 4)), (6, 11, (4, 4, 2)))):
                fm = {}
                ym = {}

                def gsink(m, b, mk):
                    y, gg = Y[m % 4], GG[m % 2]
                    bank_free[b] = g = times_R(gg[:, :], ps[b][:, :], mk, gfree[m % 2])
                    if conv is None:
                        gfree[m % 2] = s = act.do(lambda e: e.activation(y[:, :], gg[:, :], ACT.Silu), g,
                                                  yfree[m % 4])
                    else:
                        fw, fb = conv
                        s = act.do(lambda e: e.activation(y[:, :], gg[:, :], ACT.Identity,
                                                          bias=col(fb, m), scale=col(fw, 44 + m)),
                                   g, yfree[m % 4])
                        for d, w in ((1, 22 + m), (2, m)):
                            s = dve.do(lambda e, d=d, w=w: e.scalar_tensor_tensor(
                                out=y[:, d:512], in0=gg[:, 0:512 - d], scalar=col(fw, w),
                                in1=y[:, d:512], op0=ALU.mult, op1=ALU.add), s)
                        gfree[m % 2] = s
                        s = act.do(lambda e: e.activation(y[:, :], y[:, :], ACT.Silu), s)
                    ym[m] = pool.do(lambda e: e.tensor_tensor(y[:, :], y[:, :], Rsb[:, :], ALU.mult), s, R["m"])

                def usink(m, b, mk):
                    y, z, k = Y[m % 4], Z[m % 2], m - 2 * j0
                    bank_free[b] = yfree[m % 4] = s = dve.do(lambda e: e.tensor_tensor(
                        z[:, :], ps[b][:, :], y[:, :], ALU.mult), mk, ym[m], zfree[m % 2])
                    hi = copy(act, fH[:, k, :], z[:, :], s, ffree[0])
                    lo = pool.do(lambda e: e.tensor_tensor(fL[:, k, :], z[:, :], fH[:, k, :].bitcast(F32),
                                                           ALU.subtract), hi, ffree[0])
                    zfree[m % 2] = lo
                    fm[k] = [hi, lo]

                for j in range(j0, j1):
                    linear_fm(1, hH, hL, h, gsink, m0=2 * j)
                    linear_fm(1, hH, hL, h, usink, m0=2 * j)
                hread = pe.last()
                res = residual(half == 1, (lambda m: then(m, hread)) if then else None)
                for mg in range(2):
                    bs = [bank() for _ in range(4)]
                    k0 = 0
                    for gi, nk in enumerate(ks):
                        n, _, _, ncl, (wh, wl) = take()
                        for mi in range(4):
                            b = bs[mi]
                            pe.wait(bank_free[b])
                            for kk in range(nk):
                                pe.wait(*fm[k0 + kk])
                                for i, (w, x) in enumerate(((wh, fH), (wh, fL), (wl, fH))):
                                    f = (lambda e, b=b, w=w, x=x, k=k0 + kk, kk=kk, mi=mi, i=i, gi=gi, nk=nk: e.matmul(
                                        ps[b][:, :], w[:, kk, mi * 128:mi * 128 + 128], x[:, k, :],
                                        start=(gi == 0 and kk == 0 and i == 0),
                                        stop=(gi == len(ks) - 1 and kk == nk - 1 and i == 2)))
                                    if kk == nk - 1 and i == 2:
                                        mk = pe.do(f)
                                    else:
                                        pe.go(f)
                            if gi == len(ks) - 1:
                                res(4 * mg + mi, b, mk)
                                if gain and half:
                                    m = 4 * mg + mi
                                    x_mark[m] = act.do(lambda e, m=m: e.activation(
                                        X[:, m, :], X[:, m, :], ACT.Copy, scale=col(gain, m)), x_mark[m])
                                    if m == 7:
                                        rstd(61)
                        w_free[n] = mk
                        k0 += nk
                ffree[0] = mk
            c.close()

        s_x = [sem(f"s_x{i}") for i in range(8)]
        xv = xt.rearrange("p (k t) -> p k t", k=8)
        A = ExitStack()
        q = sbt(A, "q", [128, 6, 512])
        kk_ = sbt(A, "k", [128, 6, 512])
        v = sbt(A, "v", [128, 4, 768])
        O = sbt(A, "O", [128, 6, 512])
        MH = sbt(A, "MHA", [128, 2, 512], F32R)
        ML = sbt(A, "MLA", [128, 2, 512], F32R)
        Mrow = sbt(A, "Mrow", [4, 512])
        colA = sbt(A, "colA", [128, 4, 8])
        M = ExitStack()
        qm = sbt(M, "qm", [128, 2, 512])
        mkA = sbt(M, "mkA", [128, 2, 256])
        mvA = sbt(M, "mvA", [128, 2, 256])
        T = ExitStack()
        loaded = mem_load(T, 0)
        h = [None] * 8
        for k in range(8):
            x_mark[k] = act.load(lambda e, k=k: e.dma_start(X[:, k, :], xv[:, k, :]), s_x[k], 16)
        kvm = mem_kv(loaded, mkA, mvA)
        T.close()
        for k in range(8):
            scaled(k, col("mix0", k), None, h)
            square(k, x_mark[k])
        rstd(60)
        G = O[0:8, 0, :]
        G2 = [O[0:4, 1, :], O[0:4, 2, :], O[0:4, 3, :], Mrow[:, :]]
        gm = {}

        def gate_sink(m, b, mk):
            bank_free[b] = gm["G"] = times_R(G, ps[b][0:8, :], mk, scale=(None, slice(0, 8)))
            deferred.append(gates_later)

        def gates_later():
            b = bank()
            m = pe.do(lambda e: e.matmul(ps[b][0:4, :], ident[0:8, 4:8], G, start=True, stop=True),
                      gm["G"], bank_free[b])
            z, t, a, mm = G2
            bank_free[b] = m = dve.do(lambda e: e.tensor_scalar(z, ps[b][0:4, :], col("gf", p=slice(0, 4)),
                                                                None, ALU.add), m)
            m1 = act.do(lambda e: e.activation(t, z, ACT.Abs), m)
            m1 = act.do(lambda e: e.activation(t, t, ACT.Exp, scale=-1.0), m1)
            m1 = act.do(lambda e: e.activation(t, t, ACT.Ln, bias=1.0), m1)
            m2 = dve.do(lambda e: e.tensor_scalar(z, z, -1.0, 0.0, ALU.mult, ALU.max), m1)
            m2 = dve.do(lambda e: e.tensor_tensor(t, t, z, ALU.add), m2)
            onem = dve.do(lambda e: e.memset(a, 1.0))
            m2 = dve.do(lambda e: e.tensor_tensor_scan(z, a, t, 0.0, ALU.mult, ALU.add), m2, onem)
            m3 = dve.do(lambda e: e.tensor_scalar(t, O[0:4, 0, :], col("gi", p=slice(0, 4)), None, ALU.add), m2)
            m3 = dve.do(lambda e: e.tensor_tensor(t, t, z, ALU.add), m3)
            m4 = dve.do(lambda e: e.tensor_tensor_scan(mm, a, t, 0.0, ALU.mult, ALU.max), m3)
            m5 = dve.do(lambda e: e.tensor_tensor(z, z, mm, ALU.subtract), m4)
            gm["rows"] = m4
            b2 = bank()
            pe.wait(bank_free[b2], m5)
            for i in range(4):
                pe.go(lambda e, i=i: e.transpose(ps[b2][:, 8 * i:8 * i + 4], t[:, i * 128:i * 128 + 128],
                                                 ident[0:4, 0:4]))
                m = pe.do(lambda e, i=i: e.transpose(ps[b2][:, 8 * i + 4:8 * i + 8], z[:, i * 128:i * 128 + 128],
                                                     ident[0:4, 0:4]))
            bank_free[b2] = gm["col"] = copy(dve, colA[:, :, :],
                                             ps[b2][:, 0:32].rearrange("p (i c) -> p i c", i=4), m)

        qmm, qkm, vm, om = [], [], [], {}
        linear_fm(1, hH, hL, h, gate_sink)
        linear_fm(1, hH, hL, h, R_sink(qm, qmm, 0.125))

        def conv_sink(dst, base):
            def sink(m, b, mk):
                y, i = dst[:, m, :], m % 2
                bank_free[b] = g = times_R(sq[i][:, :], ps[b][:, :], mk, sq_free[i])
                s = act.do(lambda e: e.activation(y, sq[i][:, :], ACT.Identity, bias=col("cb", base + m),
                                                  scale=col("cw", 36 + base + m)), g)
                for d in (1, 2, 3):
                    s = dve.do(lambda e, d=d: e.scalar_tensor_tensor(
                        out=dst[:, m, d:512], in0=sq[i][:, 0:512 - d], scalar=col("cw", 12 * (3 - d) + base + m),
                        in1=dst[:, m, d:512], op0=ALU.mult, op1=ALU.add), s)
                sq_free[i] = s
                qkm.append(act.do(lambda e: e.activation(y, y, ACT.Silu), s))
            return sink

        def o_sink(m, b, mk):
            bank_free[b] = x = times_R(O[:, m, :], ps[b][:, :], mk)
            om[m] = act.do(lambda e: e.activation(O[:, m, :], O[:, m, :], ACT.Sigmoid), x)

        fen = fence()
        for x in (act, dve, pool):
            x.wait(*fen)
        gens = [g_linear_fm(3, hH, hL, h, conv_sink(q, 0)), g_linear_fm(3, hH, hL, h, conv_sink(kk_, 6)),
                g_linear_tm(3, hH, hL, h, v_sink(v, vm))]
        S = Soft(M, "mA", width=1024)
        mix = [None] * 8
        S.run(mem_units(qm, qmm, mkA, mvA, kvm, MH, ML, mix), gens, 2)
        M.close()
        fill(gens, 99)
        fen = fence()
        for x in (act, dve, pool):
            x.wait(*fen)
        B = ExitStack()
        sel = sbt(B, "selA", [8, 8, 128])
        c_sel = act.load(lambda e: e.dma_start(sel[:, :, :], seld.rearrange("p (i c) -> p i c", i=8)), s_c[3], 16)
        rs = sbt(B, "rs", [128, 2, 6, 8])
        Mb = [sbt(B, f"Mb{i}", [128, 512]) for i in range(2)]
        Eb = sbt(B, "Eb", [128, 1280])
        Pm = [sbt(B, f"Pm{i}", [128, 1280]) for i in range(2)]
        gens = [g_linear_fm(3, hH, hL, h, o_sink)]

        SC = 192.0 ** -0.5
        JL = [(0, 512, 0, 0), (1, 384, 1, 0), (3, 128, 1, 384), (2, 256, 2, 0)]
        bds = {}
        mbf = [None, None]
        pf = [None, None]
        eb_free = [None]
        numm = {}
        hs = {}

        def pieces(hd):
            t = 3 * (hd // 2)
            if hd % 2 == 0:
                return [(t, slice(0, 128), 192 * hd, 128), (t + 1, slice(0, 64), 192 * hd + 128, 64)]
            return [(t + 2, slice(0, 128), 192 * hd + 64, 128), (t + 1, slice(64, 128), 192 * hd, 64)]

        def m_scores(hd):
            bm = bank()
            m = pe.do(lambda e: e.matmul(ps[bm][:, :], sel[0:4, hd, :], G2[3], start=True, stop=True),
                      gm["rows"], c_sel, bank_free[bm])
            i = hd % 2
            bank_free[bm] = mb = copy(act, Mb[i][:, :], ps[bm][:, :], m, mbf[i])
            bs = [bank() for _ in range(3)]
            hs[hd] = {"b": bs, "s": {}}
            for j, L, bi, off in JL:
                pe.wait(bank_free[bs[bi]], qkm)
                for n, (t, r, _, _) in enumerate(pieces(hd)):
                    f = (lambda e, j=j, L=L, b=bs[bi], off=off, t=t, r=r, n=n: e.matmul(
                        ps[b][:, off:off + L], kk_[r, t, j * 128:j * 128 + 128], q[r, t, j * 128:512],
                        start=(n == 0), stop=(n == 1)))
                    if n:
                        hs[hd]["s"][bi] = pe.do(f)
                    else:
                        pe.go(f)
            P = Pm[i]
            for j, L, bi, off in JL:
                o = bi * 512 + off
                m = dve.do(lambda e, j=j, o=o, L=L: e.tensor_scalar(
                    Eb[:, o:o + L], Mb[i][:, j * 128:512], colA[:, j, hd:hd + 1], 0.0,
                    ALU.subtract, ALU.max), mb, gm["col"], eb_free[0])
            mbf[i] = m
            m = act.do(lambda e: e.activation(Eb[:, 0:1280], Eb[:, 0:1280], ACT.Exp, scale=-1.0), m)
            for j, L, bi, off in JL:
                o = bi * 512 + off
                b = bs[bi]
                y = dve.do(lambda e, o=o, L=L, b=b, off=off: e.scalar_tensor_tensor(
                    out=P[:, o:o + L], in0=ps[b][:, off:off + L], scalar=SC, in1=Eb[:, o:o + L],
                    op0=ALU.mult, op1=ALU.mult), m, hs[hd]["s"][bi], pf[i])
                bank_free[b] = y
            eb_free[0] = y
            for j, L, bi, off in JL:
                o = bi * 512 + off
                z = pool.do(lambda e, o=o: e.affine_select(
                    out=P[:, o:o + 128], in_=P[:, o:o + 128], compare_op=ALU.is_ge, fill=0.0, base=0,
                    pattern=[[1, 128]], channel_multiplier=-1), y)
            hs[hd]["P"] = z

        nb = {}

        def m_values(hd):
            P = Pm[hd % 2]
            pos = {j: bi * 512 + off for j, L, bi, off in JL}
            pe.wait(hs[hd]["P"], *vm)
            if hd % 2 == 0:
                bds[hd // 2] = bank(True)
                pe.wait(bank_free[bds[hd // 2]])
            bd, hc = bds[hd // 2], 4 * (hd % 2)
            for i in range(4):
                for j in range(i + 1):
                    o = pos[j] + (i - j) * 128
                    f = (lambda e, i=i, j=j, o=o: e.matmul(
                        ps[bd][:, hc + i:hc + i + 1], P[:, o:o + 128], ones[:, 0:1],
                        start=(j == 0), stop=(j == i)))
                    if i == 3 and j == 3:
                        pe.do(f)
                    else:
                        pe.go(f)
            for t, r, c0, w in pieces(hd):
                if t not in nb:
                    nb[t] = bank(w == 64)
                    pe.wait(bank_free[nb[t]])
                b = nb[t]
                for j in range(4):
                    o = pos[j]
                    f = (lambda e, b=b, j=j, r=r, c0=c0, w=w, o=o: e.matmul(
                        ps[b][r, j * 128:512], v[:, j, c0:c0 + w], P[:, o:o + 512 - j * 128],
                        start=(j == 0), stop=(j == 3)))
                    if j == 3:
                        mk = pe.do(f)
                    else:
                        pe.go(f)
                m = copy(act, q[r, t, :], ps[b][r, :], mk)
                numm[(t, r.start)] = bank_free[b] = m
                if r.start == 64:
                    held.discard(b)
                si = t % 2
                s2 = dve.do(lambda e, b=b, r=r, t=t, si=si: e.tensor_tensor(
                    sq[si][r, :], q[r, t, :], q[r, t, :], ALU.mult), m, sq_free[si])
                numm[("s", hd, t)] = s2
                deferred.append(lambda t=t, r=r, si=si, s2=s2, w=w: sums(hd, t, r, si, s2, w))
            pf[hd % 2] = mk

        def sums(hd, t, r, si, s2, w):
            o = 16 + 32 * (0 if w == 128 else 1) + 4 * (hd % 2)
            bd = bds[hd // 2]
            for i in range(4):
                m = pe.do(lambda e, i=i: e.matmul(ps[bd][:, o + i:o + i + 1], sq[si][r, i * 128:i * 128 + 128],
                                                  ones[r, 0:1], start=True, stop=True), s2)
            sq_free[si] = m
            gm["sums"] = m

        def finalize(pr):
            bd, md = bds[pr], gm["sums"]
            den, d2, s1, s2_, fac, em = (rs[:, pr, i, :] for i in range(6))
            m0 = act.do(lambda e: e.activation(em.rearrange("p (h i) -> p i h", h=2),
                                               colA[:, :, 4 + 2 * pr:6 + 2 * pr], ACT.Exp), gm["col"])
            m1 = act.do(lambda e: e.activation(den, ps[bd][:, 0:8], ACT.Abs), md)
            m1 = dve.do(lambda e: e.tensor_tensor(den, den, em, ALU.max), m0, m1)
            m2 = dve.do(lambda e: e.tensor_copy(s1, ps[bd][:, 16:24]), md)
            m2 = dve.do(lambda e: e.tensor_tensor(s1, s1, ps[bd][:, 48:56], ALU.add), m2)
            bank_free[bd] = m2
            held.discard(bd)
            m1 = dve.do(lambda e: e.scalar_tensor_tensor(out=d2, in0=den, scalar=1e-6, in1=den, op0=ALU.mult,
                                                         op1=ALU.mult), m1)
            m2 = dve.do(lambda e: e.scalar_tensor_tensor(out=s1, in0=s1, scalar=1.0 / 192, in1=d2, op0=ALU.mult,
                                                         op1=ALU.add), m1, m2)
            m2 = dve.do(lambda e: e.tensor_scalar(s1, s1, 1e-34, 1e35, ALU.max, ALU.min), m2)
            m2 = act.do(lambda e: e.activation(s2_, s1, ACT.Sqrt), m2)
            facm = dve.do(lambda e: e.reciprocal(fac, s2_), m2)
            fb = {}
            for hd in (2 * pr, 2 * pr + 1):
                for i in range(4):
                    at = 4 * (hd % 2) + i
                    dm = dve.do(lambda e, i=i, at=at: e.tensor_scalar(
                        diag[:, i * 128:i * 128 + 128], ident, fac[:, at:at + 1], None, ALU.mult),
                        facm, diag_free[0])
                for t, r, _, w in pieces(hd):
                    if t not in fb:
                        fb[t] = bank(w == 64)
                        pe.wait(bank_free[fb[t]])
                    diag_free[0] = fm_ = pe.do(lambda e, b=fb[t], r=r, w=w: e.matmul(
                        ps[b][r, :], ones[:, 0:w], diag[:, :], start=True, stop=True), dm)
                    fb[(t, r.start)] = fm_
                for t in ((3 * pr,), (3 * pr + 2, 3 * pr + 1))[hd % 2]:
                    ms = [fb[x] for x in fb if isinstance(x, tuple) and x[0] == t]
                    nm = [numm[x] for x in numm if x[0] == t]
                    b = fb[t]
                    m = dve.do(lambda e, t=t, b=b: e.scalar_tensor_tensor(
                        out=q[:, t, :], in0=q[:, t, :], scalar=col("hg", t), in1=ps[b][:, :],
                        op0=ALU.mult, op1=ALU.mult), ms, nm)
                    bank_free[b] = m
                    held.discard(b)
                    m = dve.do(lambda e, t=t: e.tensor_tensor(q[:, t, :], q[:, t, :], O[:, t, :], ALU.mult),
                               m, om[t])
                    mix[t] = list(split(q[:, t, :], m, t, h_read))

        m_scores(0)
        for hd in range(4):
            if hd < 3:
                m_scores(hd + 1)
            fill(gens, 1)
            m_values(hd)
            fill(gens, 1)
            run_deferred()
            if hd == 2:
                fill(gens, 99)
                h_read = pe.last()
                finalize(0)
        finalize(1)
        B.close()
        A.close()

        def mix_out(H1, L1, k1, order, g):
            linear_fm(4, lambda k: (H1[:, k - k1:k - k1 + 1, :] if k >= k1 else hH[:, k:k + 1, :]),
                      lambda k: (L1[:, k - k1:k - k1 + 1, :] if k >= k1 else hL[:, k:k + 1, :]),
                      mix, residual(True, hold=7), order=order)
            last, h = pe.last(), [None] * 8
            for k in range(8):
                scaled(k, g(k), last, h)
                if k == 1:
                    square(7, x_mark[7])
            return h

        h = mix_out(MH, ML, 6, [6, 7, 0, 1, 2, 3, 5, 4], lambda k: col("ffn0", k))
        rstd(60)

        def dump(src, mark):
            o = out.rearrange("p (k t) -> p k t", k=8)
            state["stop"] = True
            return sp.load(lambda e: e.dma_start(o, src), s_out, 16, *mark)

        s_out = sem("s_out")

        def body(h):
            if stop == "A1":
                return dump(X[:, :, :], x_mark)
            hn = [None] * 8
            ffn("a", h, ("fw0", "fb0"), lambda m, rd: scaled(m, col("kv", m), rd, hn))
            if stop == "A":
                return dump(X[:, :, :], x_mark)
            h = hn
            rstd(60)
            fen = fence()
            for x in (act, dve, pool):
                x.wait(*fen)
            A = ExitStack()
            k = sbt(A, "kB", [128, 6, 512])
            q = sbt(A, "qB", [128, 6, 512])
            v = sbt(A, "vB", [128, 4, 768])
            qm = sbt(A, "qmB", [128, 2, 512])
            mk_t = sbt(A, "mkB", [128, 2, 256])
            mv_t = sbt(A, "mvB", [128, 2, 256])
            MH = sbt(A, "MHB", [128, 2, 512], F32R)
            ML = sbt(A, "MLB", [128, 2, 512], F32R)
            T = ExitStack()
            loaded = mem_load(T, 1)
            km, qmk, qmm, vm, hread = [], [], [], [], []
            linear_fm(3, hH, hL, h, R_sink(k, km))
            linear_tm(3, hH, hL, h, v_sink(v, vm))
            rd, h = pe.last(), [None] * 8
            kvm = mem_kv(loaded, mk_t, mv_t)
            for i in range(8):
                scaled(i, col("mix1", i), rd, h)
            T.close()
            linear_fm(1, hH, hL, h, R_sink(qm, qmm, 0.125))
            gens = [g_linear_fm(3, hH, hL, h, R_sink(q, qmk, 0.125))]
            fen = fence()
            for x in (act, dve, pool):
                x.wait(*fen)
            C = ExitStack()
            bias = [sbt(C, f"bias{i}", [128, 512]) for i in range(3)]
            s_b = [sem(f"s_b{i}") for i in range(3)]
            S = Soft(C, "B")
            mix[:] = [None] * 8
            bmm = {}
            bfree = [None] * 3

            def load_bias(h):
                i = h % 3
                l = act.load(lambda e: e.dma_start(bias[i][:, :], biasd[:, h * 512:h * 512 + 512]), s_b[i],
                             16 * (h // 3 + 1), bfree[i])
                bmm[h] = pool.do(lambda e: e.memset(bias[i][0:64, 448:512], NEG), l)

            us = mem_units(qm, qmm, mk_t, mv_t, kvm, MH, ML, mix)
            us += pair_units(
                12, CAUSAL,
                lambda h, r: (lambda t: q[r, h // 2, t * 128:t * 128 + 128]),
                lambda h, r: (lambda L: k[r, h // 2, 0:L]),
                lambda h: (lambda j: v[:, j, 64 * h:64 * h + 64]),
                lambda h: {"qk": [qmk, km], "vm": vm, "bias": lambda L: bias[h % 3][:, 512 - L:512]},
                lambda tile: to_parts(hH, hL, tile, [hread], mix, tile))

            def before(s):
                if s == 4:
                    fill(gens, 99)
                    hread.append(pe.last())
                if s >= 4:
                    us[s]["bm"] = [bmm[s - 4]]

            def after(s):
                if s >= 4:
                    bfree[(s - 4) % 3] = dve.last()
                if 1 <= s - 2 < 12:
                    load_bias(s - 2)

            load_bias(0)
            S.run(us, gens, 2, before, after)
            C.close()
            A.close()
            h = mix_out(MH, ML, 6, [6, 7, 0, 1, 2, 3, 4, 5], lambda k: col("ffn1", k))
            rstd(60)
            D = ExitStack()
            fen = fence()
            dve.wait(*fen)
            pool.wait(*fen)
            acc2 = sbt(D, "acc2", [128, 512])
            gg = sbt(D, "gg", [128, 8])
            ggm = dve.do(lambda e: e.tensor_tensor(gg[:, :], col("final", 0, 8), col("n1", 0, 8), ALU.mult))
            act.wait(ggm)
            dve.wait(ggm)
            hn = [None] * 8
            a2 = {}

            def then(m, rd):
                scaled(m, gg[:, m:m + 1], rd, hn)
                if m == 0:
                    a2["m"] = act.do(lambda e: e.activation(acc2[:, :], X[:, 0, :], ACT.Square,
                                                            scale=col("final")), x_mark[0])
                    return
                i = (m + 1) % 2
                x = act.do(lambda e: e.activation(sq[i][:, :], X[:, m, :], ACT.Square, scale=col("final", m)),
                           x_mark[m], sq_free[i])
                a2["m"] = sq_free[i] = pool.do(lambda e: e.tensor_tensor(
                    acc2[:, :], acc2[:, :], sq[i][:, :], ALU.add), x, a2["m"])

            ffn("b", h, ("fw1", "fb1"), then)
            if stop == "B":
                D.close()
                return dump(X[:, :, :], x_mark)
            h = hn
            xs = [list(m) for m in h]

            def first():
                b = bank()
                pe.wait(bank_free[b])
                acc_free[0] = m = token_sums(acc, acc_mark[0], b, 0)
                m2 = token_sums(acc2, a2["m"], b, 4)
                m = act.do(lambda e: e.activation(small[:, 0:4], ps[b][:, 0:4], ACT.Sqrt,
                                                  bias=small[:, 60:61], scale=1.0 / 1024), m2)
                m = dve.do(lambda e: e.reciprocal(small[:, 32:36], small[:, 0:4]), m)
                R["r1"] = m
                m = dve.do(lambda e: e.scalar_tensor_tensor(
                    out=small[:, 40:44], in0=ps[b][:, 4:8], scalar=1.0 / 1024, in1=small[:, 32:36],
                    op0=ALU.mult, op1=ALU.mult), m)
                bank_free[b] = m
                m = dve.do(lambda e: e.tensor_tensor(small[:, 40:44], small[:, 40:44], small[:, 32:36],
                                                     ALU.mult), m)
                m = act.do(lambda e: e.activation(small[:, 44:48], small[:, 40:44], ACT.Sqrt,
                                                  bias=small[:, 61:62]), m)
                m = dve.do(lambda e: e.reciprocal(small[:, 36:40], small[:, 44:48]), m)
                R["col"] = dve.do(lambda e: e.tensor_tensor(small[:, 4:8], small[:, 36:40], small[:, 32:36],
                                                            ALU.mult), m, act.last())

            def second():
                b = bank()
                m = bcast(small[:, 4:8], R["col"], bnk=b)
                bank_free[b] = R["m"] = copy(act, Rsb[:, :], ps[b][:, :], m, dve.last(), pool.last())
                b = bank()
                m = bcast(small[:, 32:36], R["r1"], bnk=b)
                bank_free[b] = R["m1"] = copy(act, acc2[:, :], ps[b][:, :], m)

            norm_steps.extend([first, second])
            A = ExitStack()
            dq = sbt(A, "dq", [128, 4, 512])
            dk = sbt(A, "dk", [128, 4, 512])
            fq = sbt(A, "fq", [128, 4, 512])
            fk = sbt(A, "fk", [128, 4, 512])
            dv = sbt(A, "dv", [128, 4, 512])
            fv = sbt(A, "fv", [128, 4, 512])
            ncum = sbt(A, "ncum", [8, 512])
            B = ExitStack()
            RC = sbt(B, "RC", [128, 512])
            RS = sbt(B, "RS", [128, 512])
            U1 = [sbt(B, f"U1{i}", [128, 512]) for i in range(2)]
            U2 = [sbt(B, f"U2{i}", [128, 512]) for i in range(2)]
            Gf = sbt(B, "Gf", [128, 512])
            g3 = [sbt(B, f"g3{i}", [8, 512]) for i in range(3)]
            fen = fence()
            for x in (act, dve, pool):
                x.wait(*fen)
            c_r1 = act.load(lambda e: e.dma_start(RC[:, :], rope[:, 0:512]), s_c[4], 16)
            c_r2 = act.load(lambda e: e.dma_start(RS[:, :], rope[:, 512:1024]), s_c[5], 16)
            fgm = {}

            def fg_sink(m, b, mk):
                bank_free[b] = fgm["G"] = times_R(Gf[96:128, :], ps[b][96:128, :], mk,
                                                  scale=(None, slice(96, 128)))
                deferred.append(fg_later)

            def fg_later():
                b = bank()
                m = pe.do(lambda e: e.matmul(ps[b][0:8, :], ident[96:128, 120:128], Gf[96:128, :],
                                             start=True, stop=True), fgm["G"], bank_free[b])
                z, t, a = g3
                bank_free[b] = m = dve.do(lambda e: e.tensor_scalar(z[:, :], ps[b][0:8, :], col("bf", p=slice(0, 8)),
                                                                    None, ALU.add), m)
                m1 = act.do(lambda e: e.activation(t[:, :], z[:, :], ACT.Abs), m)
                m1 = act.do(lambda e: e.activation(t[:, :], t[:, :], ACT.Exp, scale=-1.0), m1)
                m1 = act.do(lambda e: e.activation(t[:, :], t[:, :], ACT.Ln, bias=1.0), m1)
                m2 = dve.do(lambda e: e.tensor_scalar(z[:, :], z[:, :], -1.0, 0.0, ALU.mult, ALU.max), m1)
                m2 = dve.do(lambda e: e.tensor_tensor(t[:, :], t[:, :], z[:, :], ALU.add), m2)
                onem = dve.do(lambda e: e.memset(a[:, :], 1.0))
                fgm["n"] = dve.do(lambda e: e.tensor_tensor_scan(ncum[:, :], a[:, :], t[:, :], 0.0, ALU.mult,
                                                                 ALU.add), m2, onem)

            lm = dve.do(lambda e: e.tensor_tensor(small[0:64, 8:10], col("lam", 0, 2, slice(0, 64)),
                                                  col("lam", 2, 2, slice(0, 64)), ALU.mult))
            lmx = {}

            def lam_later():
                bl = bank()
                x = pe.do(lambda e: e.matmul(ps[bl][:, 0:2], ones[0:64, :], small[0:64, 8:10], start=True,
                                             stop=True), lm, bank_free[bl])
                bank_free[bl] = x = act.do(lambda e: e.activation(small[:, 10:12], ps[bl][:, 0:2], ACT.Exp), x)
                x = dve.do(lambda e: e.tensor_tensor(small[:, 12:13], small[:, 11:12], small[:, 10:11],
                                                     ALU.subtract), x)
                lmx["m"] = dve.do(lambda e: e.tensor_scalar(small[:, 12:13], small[:, 12:13], -0.2, None,
                                                            ALU.add), x)

            deferred.append(lam_later)
            u1f, u2f = [None] * 2, [None] * 2
            dqm, dkm = [], []

            def rope_sink(dst, lst, scale, cnt=[0]):
                def sink(m, b, mk):
                    i = cnt[0] % 2
                    cnt[0] += 1
                    bank_free[b] = a = times_R(U1[i][:, :], ps[b][:, :], mk, u1f[i], scale=scale)

                    def later():
                        b2 = bank()
                        r = pe.do(lambda e: e.matmul(ps[b2][:, :], rotm, U1[i][:, :], start=True, stop=True),
                                  a, bank_free[b2])
                        x = dve.do(lambda e: e.tensor_tensor(U2[i][:, :], ps[b2][:, :], RS[:, :], ALU.mult),
                                   r, c_r2, u2f[i])
                        bank_free[b2] = x
                        y = pool.do(lambda e: e.tensor_tensor(dst[:, m, :], U1[i][:, :], RC[:, :], ALU.mult),
                                    a, c_r1)
                        u1f[i] = [r, y]
                        z = dve.do(lambda e: e.tensor_tensor(dst[:, m, :], dst[:, m, :], U2[i][:, :], ALU.add), x, y)
                        u2f[i] = z
                        lst.append(z)
                    deferred.append(later)
                return sink

            dvm, fqm, fkm, fvm, hread = [], [], [], [], []
            linear_fm(1, hH, hL, h, fg_sink)
            linear_fm(2, hH, hL, h, rope_sink(dq, dqm, 0.125))
            for kx in range(8):
                x_mark[kx] = dve.do(lambda e, kx=kx: e.scalar_tensor_tensor(
                    out=X[:, kx, :], in0=X[:, kx, :], scalar=col("final", kx), in1=acc2[:, :],
                    op0=ALU.mult, op1=ALU.mult), R["m1"], xs[kx])
            linear_fm(2, hH, hL, h, rope_sink(dk, dkm, 1.0))
            linear_tm(2, hH, hL, h, v_sink(dv, dvm))
            run_deferred()
            gens = [g_linear_fm(2, hH, hL, h, R_sink(fq, fqm, 0.125)),
                    g_linear_fm(2, hH, hL, h, R_sink(fk, fkm)),
                    g_linear_tm(2, hH, hL, h, v_sink(fv, fvm))]
            B.close()
            fen = fence()
            for x in (act, dve, pool):
                x.wait(*fen)
            C = ExitStack()
            sel = sbt(C, "selC", [8, 8, 128])
            c_sel = act.load(lambda e: e.dma_start(sel[:, :, :], seld.rearrange("p (i c) -> p i c", i=8)),
                             s_c[6], 16)
            S = Soft(C, "C", 3)
            CB = [sbt(C, f"CB{i}", [128, 512]) for i in range(2)]
            mix[:] = [None] * 8
            post = []

            def od_sink(hd):
                def sink(b, m):
                    i, od = hd % 2, dq[:, hd, :]
                    bank_free[b] = a = copy(act, od, ps[b][:, :], m, scale=2.0 ** -40)
                    a = dve.do(lambda e: e.tensor_scalar(od, od, 2.0 ** 60, -2.0 ** 60, ALU.min, ALU.max), a)
                    ss = small[:, 16 + 8 * i:24 + 8 * i]
                    pm = {}

                    def one():
                        x = pool.do(lambda e: e.tensor_tensor(sq[i][:, :], od, od, ALU.mult), a, sq_free[i])
                        pm["s"] = x

                    def two():
                        b2 = bank()
                        pe.wait(bank_free[b2])
                        sq_free[i] = m = token_sums(sq[i], pm["s"], b2, 0)
                        m = dve.do(lambda e: e.tensor_scalar(
                            ss[:, 0:4], ps[b2][:, 0:4], 1.0 / 128, 1e-5 * 2.0 ** -80, ALU.mult, ALU.add), m)
                        m = dve.do(lambda e: e.reciprocal(ss[:, 4:8], ss[:, 0:4]), m)
                        m = act.do(lambda e: e.activation(ss[:, 0:4], ss[:, 4:8], ACT.Sqrt, scale=0.64), m)
                        pm["c"] = bank_free[b2] = dve.do(lambda e: e.scalar_tensor_tensor(
                            out=ss[:, 0:4], in0=ps[b2][:, 0:4], scalar=2.0 ** 48, in1=ss[:, 0:4],
                            op0=ALU.is_lt, op1=ALU.mult), m)

                    def three():
                        b3 = bank()
                        m = bcast(ss[:, 0:4], pm["c"], bnk=b3)
                        m = bank_free[b3] = dve.do(lambda e: e.scalar_tensor_tensor(
                            out=od, in0=od, scalar=col("sub"), in1=ps[b3][:, :], op0=ALU.mult, op1=ALU.mult), m)
                        mix[hd] = list(split(od, m, hd, hread))
                    post.extend([one, two, three])
                return sink

            us = []
            for hd in range(4):
                for mp in range(2):
                    r = slice(64 * mp, 64 * mp + 64)
                    u = {"lay": CAUSAL, "mask": mchunk,
                         "q": lambda t, r=r, hd=hd: dq[r, hd, t * 128:t * 128 + 128],
                         "k": lambda L, r=r, hd=hd: dk[r, hd, 0:L],
                         "qk": [dqm, dkm], "vm": dvm, "rows": slice(0, 128), "bank": None}
                    if mp == 0:
                        u["part"] = True
                    else:
                        u["prev"] = us[-1]
                        u["neg"] = (small[:, 12:13], lmx["m"])
                        u["v"] = lambda j, hd=hd: dv[:, j, hd * 128:hd * 128 + 128]
                        u["sink"] = od_sink(hd)
                    us.append(u)
            cbm = {}
            cbf = [None] * 2

            def load_cb(h):
                i = h % 2
                b = bank()
                m = pe.do(lambda e: e.matmul(ps[b][:, :], sel[:, h, :], ncum[:, :], start=True, stop=True),
                          fgm["n"], c_sel, bank_free[b])
                bank_free[b] = cbm[h] = copy(act, CB[i][:, :], ps[b][:, :], m, cbf[i])

            us += pair_units(
                8, CAUSAL,
                lambda h, r: (lambda t: fq[r, h // 2, t * 128:t * 128 + 128]),
                lambda h, r: (lambda L: fk[r, h // 2, 0:L]),
                lambda h: (lambda j: fv[:, j, 64 * h:64 * h + 64]),
                lambda h: {"qk": [fqm, fkm], "vm": fvm, "mask": mcaus, "bias": lambda L: CB[h % 2][:, 0:L]},
                lambda tile: to_parts(hH, hL, 4 + tile, [hread], mix, 4 + tile))

            def before(s):
                if s == 6:
                    fill(gens, 99)
                    hread.append(pe.last())
                if s >= 8:
                    us[s]["bm"] = [cbm[s - 8]]
                if s >= 6 and post:
                    post.pop(0)()

            def after(s):
                if s >= 8:
                    cbf[(s - 8) % 2] = dve.last()
                if 0 <= s - 7 < 8:
                    load_cb(s - 7)
                if s >= 6 and post:
                    post.pop(0)()

            S.run(us, gens, 2, before, after)
            while post:
                post.pop(0)()
            C.close()
            A.close()
            D.close()
            h = mix_out(None, None, 8, None, lambda k: col("n2", k))
            if stop == "C1":
                return dump(X[:, :, :], x_mark)
            rstd(61)
            ffn("c", h, None, None, "nf")
            while norm_steps:
                norm_steps.pop(0)()
            o = out.rearrange("p (k t) -> p k t", k=8)
            for kx in range(8):
                m = times_R(X[:, kx, :], X[:, kx, :], x_mark[kx], eng=pool if kx % 3 == 1 else dve)
                last = sp.load(lambda e, kx=kx: e.dma_start(o[:, kx, :], X[:, kx, :]),
                               s_out, 16 * (kx + 1), m)
            return last

        sp.wait(body(h))

        block = ctx.enter_context(nc.Block())

        @block.sync
        def _(e):
            sp.play(e)

        @block.scalar
        def _(e):
            act.play(e)

        @block.vector
        def _(e):
            dve.play(e)

        @block.gpsimd
        def _(e):
            pool.play(e)

        @block.tensor
        def _(e):
            pe.play(e)


def shape_constants():
    ident = np.eye(128, dtype=np.float32)
    ones = np.ones((128, 128), np.float32)
    chunk = np.zeros((128, 128), np.float32)
    chunk[0:64, 64:128] = NEG
    i = np.arange(128)
    causal = np.where(i[None, :] <= i[:, None], np.float32(0), np.float32(NEG)).astype(np.float32)
    rot = np.zeros((128, 128), np.float32)
    for b in (0, 64):
        for d in range(8):
            rot[b + d + 8, b + d] = -1.0
            rot[b + d, b + d + 8] = 1.0
    consts = np.concatenate([ident, ones, chunk, causal, rot], 1)
    inv = np.float32(500000.0) ** (-np.arange(0, 16, 2, dtype=np.float32) / np.float32(16))
    ang = np.arange(512, dtype=np.float32)[None, :] * inv.astype(np.float32)[:, None]
    C, S = np.ones((128, 512), np.float32), np.zeros((128, 512), np.float32)
    for b in (0, 8, 64, 72):
        C[b:b + 8] = np.cos(ang)
        S[b:b + 8] = np.sin(ang)
    sel = np.zeros((8, 8, 128), np.float32)
    for h in range(8):
        sel[h, h, :] = 1.0
    return consts, np.concatenate([C, S], 1), sel.reshape(8, 1024)


def kernel(_stop=None, **inputs):
    import concourse.bacc as _bacc
    from concourse.bass_utils import run_bass_kernel_spmd as _run

    z = {n: np.asarray(a) for n, a in inputs.items()}
    parts = []
    for name, idx, k0, nk, c0, ncl in plan():
        w = z[name] if idx is None else z[name][idx]
        w = w[k0 * 128:(k0 + nk) * 128, c0:c0 + ncl].reshape(nk, 128, ncl)
        parts.append(w.transpose(1, 0, 2).reshape(128, nk * ncl))
    wall = np.ascontiguousarray(np.concatenate(parts, 1))

    def pk(a):
        return np.asarray(a).reshape(-1, 128).T

    def short(a):
        a = np.asarray(a).reshape(-1, 1)
        return np.concatenate([a, np.zeros((128 - len(a), 1), np.float32)], 0)

    got = {
        "mix0": pk(z["norm_mix_g"][0]), "mix1": pk(z["norm_mix_g"][1]), "ffn0": pk(z["norm_ffn_g"][0]),
        "ffn1": pk(z["norm_ffn_g"][1]), "kv": pk(z["kv_norm_g"]), "final": pk(z["final_g"]),
        "n1": pk(z["norm1_g_2"][0]), "n2": pk(z["norm2_g_2"][0]), "nf": pk(z["normf_g_2"]),
        "cw": pk(z["a_conv_w"][0]), "cb": pk(z["a_conv_b"][0]), "hg": pk(z["a_head_g"][0]),
        "fw0": pk(z["ffn_conv_w"][0]), "fb0": pk(z["ffn_conv_b"][0]), "fw1": pk(z["ffn_conv_w"][1]),
        "fb1": pk(z["ffn_conv_b"][1]), "sub": pk(z["subln_g_2"][0]), "gi": short(z["a_gate_b"][0][0:4]),
        "gf": short(z["a_gate_b"][0][4:8]), "bf": short(z["b_f_2"][0]),
        "lam": np.concatenate([short(z[n][0]) for n in ("lam_q1_2", "lam_q2_2", "lam_k1_2", "lam_k2_2")], 1),
    }
    cols = np.ascontiguousarray(np.concatenate([got[n] for n in COLS], 1))
    t, c = np.arange(128)[:, None], np.arange(512)[None, :]
    idx = np.clip(t + 384 - c, -63, 128) + 63
    bias = np.ascontiguousarray(z["b_rel_bias"][0][:, idx].transpose(1, 0, 2).reshape(128, 12 * 512))
    consts, rope, sel = shape_constants()
    arrays = {
        "wall": wall, "xt": z["x"][0].T.reshape(8, 128, 512).transpose(1, 0, 2).reshape(128, 4096),
        "memt": z["mem"][0].T.reshape(8, 128, 256).transpose(1, 0, 2).reshape(128, 2048),
        "cols": cols, "bias": bias, "consts": consts, "rope": rope, "sel": sel,
    }
    arrays = {n: np.ascontiguousarray(a) for n, a in arrays.items()}
    nc = _bacc.Bacc("TRN2", target_bir_lowering=False, num_devices=1)
    args = [nc.dram_tensor("in_" + n, a.shape, F32, kind="ExternalInput").ap() for n, a in arrays.items()]
    args.append(nc.dram_tensor("out_y", (128, 4096), F32, kind="ExternalOutput").ap())
    program(nc, *args, stop=_stop)
    r = _run(nc, [{"in_" + n: a for n, a in arrays.items()}], core_ids=[0])
    y = np.asarray(r.results[0]["out_y"])
    return np.ascontiguousarray(y.reshape(128, 8, 512).transpose(1, 0, 2).reshape(1024, 512).T.reshape(1, 512, 1024))
```

```python
from contextlib import ExitStack

import numpy as np
import concourse.bass as bass
from concourse import mybir

F32 = mybir.dt.float32
F32R = mybir.dt.float32r
BF16 = mybir.dt.bfloat16
ALU = mybir.AluOpType
ACT = mybir.ActivationFunctionType
AX = mybir.AxisListType

NEG = -1e30
NT = 4
DFF = 2816
SLOT = 2048
NRAW = 2
NCV = 2
CAUSAL = [(3, 512, 0, 0), (2, 384, 1, 0), (0, 128, 1, 384), (1, 256, 2, 0)]
FULL256 = [(0, 256, 0, 0), (1, 256, 0, 256), (2, 256, 1, 0), (3, 256, 1, 256)]


def ffn_plan(up, upo, gate, gateo, down, idx):
    out = []
    for j0, j1, ks in ((0, 6, ((0, 4), (4, 4), (8, 4))), (6, 11, ((12, 4), (16, 3), (19, 3)))):
        for j in range(j0, j1):
            out.append((gate, idx, 0, 8, gateo + 256 * j, 256))
            out.append((up, idx, 0, 8, upo + 256 * j, 256))
        for mg in range(2):
            for k0, nk in ks:
                out.append((down, idx, k0, nk, 512 * mg, 512))
    return out


def plan():
    u = [("mem_w_kv", 0, 0, 8, 0, 256), ("mem_w_kv", 0, 0, 8, 256, 256)]
    u += [("a_w_in", 0, 0, 8, 3072, 128), ("a_w_in", 0, 0, 8, 3080, 256)]
    u += [("a_w_in", 0, 0, 8, 256 * j, 256) for j in (0, 3, 1, 4, 6, 7, 2, 5, 8, 9, 10, 11)]
    u += [("a_w_out", 0, 0, 8, 256 * j, 256) for j in range(4)]
    u += ffn_plan("ffn_w_up", 0, "ffn_w_up", DFF, "ffn_w_down", 0)
    u += [("w_kv", None, 0, 8, 256 * j, 256) for j in range(6)]
    u += [("mem_w_kv", 1, 0, 8, 0, 256), ("mem_w_kv", 1, 0, 8, 256, 256)]
    u += [("b_w_in", 0, 0, 8, 256 * j, 256) for j in (3, 0, 1, 2)]
    u += [("b_w_out", 0, 0, 8, 256 * j, 256) for j in range(4)]
    u += ffn_plan("ffn_w_up", 0, "ffn_w_up", DFF, "ffn_w_down", 1)
    u += [("w_in_2", 0, 0, 8, 2952, 128)]
    u += [("w_in_2", 0, 0, 8, 256 * j, 256) for j in (0, 1, 2, 3, 4, 5, 6, 8, 10, 7, 9, 11)]
    u += [("w_out_2", 0, 0, 8, 256 * j, 256) for j in range(4)]
    u += ffn_plan("w_up_2", 0, "w_gate_2", 0, "w_down_2", 0)
    return u


def columns():
    at, out = 0, {}
    for name, n in [("mix0", 8), ("mix1", 8), ("ffn0", 8), ("ffn1", 8), ("kv", 8), ("final", 8),
                    ("n1", 8), ("n2", 8), ("nf", 8), ("cw", 48), ("cb", 12), ("hg", 6),
                    ("fw0", 66), ("fb0", 22), ("fw1", 66), ("fb1", 22), ("sub", 1), ("gi", 1), ("gf", 1),
                    ("bf", 1), ("lam", 4)]:
        out[name] = (at, n)
        at += n
    return out, at


COLS, NCOLS = columns()


class Lane:

    def __init__(self, sem):
        self.sem, self.q, self.n, self.seen = sem, [], 0, {}

    def wait(self, *marks):
        for m in marks:
            if m is None:
                continue
            if isinstance(m, list):
                self.wait(*m)
                continue
            sem, v = m
            if self.seen.get(sem.name, 0) < v:
                self.seen[sem.name] = v
                self.q.append(lambda e, sem=sem, v=v: e.wait_ge(sem, v))

    def do(self, fn, *marks):
        self.wait(*marks)
        self.n += 1
        self.q.append(lambda e: fn(e).then_inc(self.sem, 1))
        return (self.sem, self.n)

    def go(self, fn, *marks):
        self.wait(*marks)
        self.q.append(fn)

    def load(self, fn, sem, value, *marks):
        self.wait(*marks)
        self.q.append(lambda e: fn(e).then_inc(sem, 16))
        return (sem, value)

    def last(self):
        return (self.sem, self.n) if self.n else None

    def play(self, e):
        for f in self.q:
            f(e)


def program(nc, wall, xt, memt, colsd, biasd, consts, rope, out):
    ctx = ExitStack()
    with ctx:
        def sem(name):
            return ctx.enter_context(nc.semaphore(name))

        def sbt(c, name, shape, dt=F32):
            return c.enter_context(nc.sbuf_tensor(name, shape, dt))

        def sbt2(c, name, shape):
            t = ExitStack()
            a = sbt(t, name, shape)
            t.close()
            return a, sbt(c, name + "r", shape, F32R)

        pe, act, dve, pool, sp = (Lane(sem(n)) for n in ("s_pe", "s_act", "s_dve", "s_pool", "s_sp"))

        def fence():
            return [x.last() for x in (pe, act, dve, pool)]

        ps = [ctx.enter_context(nc.psum_tensor(f"ps{i}", [128, 512], F32)) for i in range(8)]
        bank_free = [None] * 8
        turns = list(range(8))

        def bank(hold=False):
            b = turns.pop(0)
            if not hold:
                turns.append(b)
            return b

        def release(b):
            if b not in turns:
                turns.append(b)

        X = sbt(ctx, "X", [128, 8, 512])
        hH = sbt(ctx, "hH", [128, 8, 512], F32R)
        hL = sbt(ctx, "hL", [128, 8, 512], F32R)
        raw = [sbt(ctx, f"raw{i}", [128, SLOT]) for i in range(NRAW)]
        WH = [sbt(ctx, f"WH{i}", [128, SLOT], F32R) for i in range(NCV)]
        WL = [sbt(ctx, f"WL{i}", [128, SLOT], F32R) for i in range(NCV)]
        cols = sbt(ctx, "cols", [128, NCOLS])
        K = sbt(ctx, "K", [128, 5, 128])
        KB = sbt(ctx, "KB", [128, 3, 128], BF16)
        identb, mchunk, mcaus = (KB[:, i, :] for i in range(3))
        ident, ones, rotm = (K[:, i, :] for i in (0, 1, 4))
        acc = sbt(ctx, "acc", [128, 512])
        sq = [sbt(ctx, f"sq{i}", [128, 512]) for i in range(2)]
        diag = sbt(ctx, "diag", [128, 512])
        Rsb = sbt(ctx, "Rsb", [128, 512])
        small = sbt(ctx, "small", [128, 64])

        def col(name, i=0, n=1, p=slice(0, 128)):
            a = COLS[name][0] + i
            return cols[p, a:a + n]

        units = plan()
        woff = [0]
        for u in units:
            woff.append(woff[-1] + u[3] * u[5])
        s_raw = [sem(f"s_raw{i}") for i in range(NRAW)]
        w_lo = {}
        w_free = {}
        wst = {"load": 0, "conv": 0, "next": 0}

        w_got = {}

        def w_load(n):
            if n not in w_got:
                w_got[n] = w_load_now(n)
            return w_got[n]

        def w_load_now(n):
            size = woff[n + 1] - woff[n]
            r = n % NRAW
            return sp.load(lambda e: e.dma_start(raw[r][:, 0:size], wall[:, woff[n]:woff[n + 1]]),
                           s_raw[r], 16 * (n // NRAW + 1), w_lo.get(n - NRAW))

        def w_convert(n):
            size = woff[n + 1] - woff[n]
            loaded = w_load(n)
            r, c = n % NRAW, n % NCV
            half = size // 2
            for a, b in ((0, half), (half, size)):
                m = act.do(lambda e, a=a, b=b: e.activation(WH[c][:, a:b], raw[r][:, a:b], ACT.Copy),
                           loaded, w_free.get(n - NCV))
                lo = dve.do(lambda e, a=a, b=b: e.tensor_tensor(
                    WL[c][:, a:b], raw[r][:, a:b], WH[c][:, a:b].bitcast(F32), ALU.subtract), m)
            w_lo[n] = lo

        def convert_ahead(end):
            while wst["conv"] < min(end, len(units)) and (wst["conv"] < NCV or wst["conv"] - NCV in w_free):
                w_convert(wst["conv"])
                wst["conv"] += 1

        def take(ahead=2):
            n = wst["next"]
            wst["next"] += 1
            convert_ahead(n + ahead)
            pe.wait(w_lo[n])
            _, _, k0, nk, _, ncl = units[n]
            v = [WH[n % NCV][:, 0:nk * ncl].rearrange("p (k c) -> p k c", k=nk),
                 WL[n % NCV][:, 0:nk * ncl].rearrange("p (k c) -> p k c", k=nk)]
            return n, k0, nk, ncl, v

        deferred = []
        waiting = []
        norm_steps = []

        def run_deferred():
            while deferred:
                deferred.pop(0)()

        timed = []

        def tile_done(sink, *args):
            waiting.append(lambda: sink(*args))
            run_deferred()
            for x in list(timed):
                x[0] -= 1
                if x[0] < 0:
                    timed.remove(x)
                    x[1]()
            if norm_steps:
                norm_steps.pop(0)()
            if not norm_steps:
                while waiting:
                    waiting.pop(0)()

        def g_linear_fm(nunits, AH, AL, marks, sink, N=512, m0=0):
            m = m0
            for _ in range(nunits):
                n, _, nk, ncl, (wh, wl) = take()
                ks = range(nk)
                for c in range(0, ncl, 128):
                    b = bank()
                    pe.wait(bank_free[b])
                    o = ps[b][:, 0:N]
                    for k in ks:
                        pe.wait(marks[k])
                        for i, (w, x) in enumerate(((wh, AH), (wh, AL), (wl, AH))):
                            f = (lambda e, o=o, w=w, x=x, k=k, c=c, i=i: e.matmul(
                                o, w[:, k, c:c + 128], x[:, k, 0:N], start=(k == ks[0] and i == 0),
                                stop=(k == ks[-1] and i == 2)))
                            if k == ks[-1] and i == 2:
                                mk = pe.do(f)
                            else:
                                pe.go(f)
                    if c + 128 >= ncl:
                        w_free[n] = mk
                    tile_done(sink, m, b, mk)
                    m += 1
                    yield

        def g_linear_tm(nunits, AH, AL, marks, sink, ntt=4, u0=0):
            for un in range(u0, u0 + nunits):
                n, _, nk, ncl, (wh, wl) = take()
                for t0 in range(0, ntt, 2):
                    b = bank()
                    pe.wait(bank_free[b])
                    for t in (t0, t0 + 1):
                        o = ps[b][:, (t - t0) * 256:(t - t0) * 256 + 256]
                        for k in range(nk):
                            pe.wait(marks[k])
                            for i, (w, x) in enumerate(((wh, AH), (wl, AH), (wh, AL))):
                                f = (lambda e, o=o, w=w, x=x, k=k, t=t, i=i: e.matmul(
                                    o, x[:, k, t * 128:t * 128 + 128], w[:, k, :],
                                    start=(k == 0 and i == 0), stop=(k == nk - 1 and i == 2)))
                                if k == nk - 1 and i == 2:
                                    mk = pe.do(f)
                                else:
                                    pe.go(f)
                    if t0 + 2 >= ntt:
                        w_free[n] = mk
                    tile_done(sink, t0, un, b, mk)
                    yield

        def linear_fm(*args, **kw):
            for _ in g_linear_fm(*args, **kw):
                pass

        def linear_tm(*args, **kw):
            for _ in g_linear_tm(*args, **kw):
                pass

        def fill(gens, n):
            while gens and n > 0:
                try:
                    next(gens[0])
                    n -= 1
                except StopIteration:
                    gens.pop(0)

        def copy(eng, o, i, *marks, scale=None):
            if eng is act:
                return act.do(lambda e: e.activation(o, i, ACT.Copy, scale=1.0 if scale is None else scale),
                              *marks)
            return eng.do(lambda e: e.tensor_copy(o, i), *marks)

        acc_free = [None]
        sq_free = [None, None]
        x_mark = [None] * 8
        acc_mark = [None]

        def square(k, mark, eng=pool, mul=act):
            if k == 0:
                acc_mark[0] = act.do(lambda e: e.activation(acc[:, :], X[:, 0, :], ACT.Square), mark, acc_free[0])
                return
            i = k % 2
            if mul is act:
                m = act.do(lambda e: e.activation(sq[i][:, :], X[:, k, :], ACT.Square), mark, sq_free[i])
            else:
                m = mul.do(lambda e: e.tensor_tensor(sq[i][:, :], X[:, k, :], X[:, k, :], ALU.mult), mark,
                           sq_free[i])
            acc_mark[0] = sq_free[i] = eng.do(
                lambda e: e.tensor_tensor(acc[:, :], acc[:, :], sq[i][:, :], ALU.add), m, acc_mark[0])

        diag_free = [None]

        def bcast(colap, mark, rows=slice(0, 128), bnk=None):
            ms = [mark, diag_free[0]]
            for i in range(4):
                d = dve.do(lambda e, i=i: e.tensor_scalar(diag[:, i * 128:i * 128 + 128], ident,
                                                          colap[:, i:i + 1], None, ALU.mult), *ms)
            n = rows.stop - rows.start
            diag_free[0] = pe.do(lambda e: e.matmul(ps[bnk][rows, :], ones[:, 0:n], diag[:, :],
                                                    start=True, stop=True), d, bank_free[bnk])
            return diag_free[0]

        R = {}

        def token_sums(src, mark, b, at):
            pe.wait(mark)
            for i in range(4):
                m = pe.do(lambda e, i=i: e.matmul(ps[b][:, at + i:at + i + 1], src[:, i * 128:i * 128 + 128],
                                                  ones[:, 0:1], start=True, stop=True))
            return m

        def rstd(eps):

            def first():
                b = bank()
                pe.wait(bank_free[b])
                acc_free[0] = m = token_sums(acc, acc_mark[0], b, 0)
                bank_free[b] = m = act.do(lambda e: e.activation(
                    small[:, 0:4], ps[b][:, 0:4], ACT.Sqrt, bias=small[:, eps:eps + 1], scale=1.0 / 1024), m)
                R["col"] = dve.do(lambda e: e.reciprocal(small[:, 4:8], small[:, 0:4]), m, act.last())

            def second():
                b = bank()
                m = bcast(small[:, 4:8], R["col"], bnk=b)
                bank_free[b] = R["m"] = copy(act, Rsb[:, :], ps[b][:, :], m, R.get("dve"), R.get("pool"))

            norm_steps.extend([lambda: None, first, second])


        def scaled(k, g, free, marks, eng=act):
            if eng is act:
                hi = act.do(lambda e: e.activation(hH[:, k, :], X[:, k, :], ACT.Copy, scale=g), x_mark[k], free)
            else:
                hi = eng.do(lambda e: e.tensor_scalar(hH[:, k, :], X[:, k, :], g, None, ALU.mult), x_mark[k],
                            free)
            lo = dve.do(lambda e: e.scalar_tensor_tensor(
                out=hL[:, k, :], in0=X[:, k, :], scalar=g, in1=hH[:, k, :].bitcast(F32),
                op0=ALU.mult, op1=ALU.subtract), hi, free)
            marks[k] = [hi, lo]

        def residual(last, then=None, adder=pool):
            def sink(m, b, mk):
                bank_free[b] = x_mark[m] = dve.do(lambda e: e.tensor_tensor(
                    X[:, m, :], X[:, m, :], ps[b][:, :], ALU.add), mk)
                if last:
                    if then:
                        then(m)
                    square(m, x_mark[m], adder)
            return sink

        def times_R(dst, src, *marks, scale=None, eng=None):
            rows = slice(0, 128) if scale is None or not isinstance(scale, tuple) else scale[1]
            sc = scale[0] if isinstance(scale, tuple) else scale
            if sc is None:
                m = (eng or dve).do(lambda e: e.tensor_tensor(dst, src, Rsb[rows, :], ALU.mult),
                                    R["m"], *marks)
            else:
                m = dve.do(lambda e: e.scalar_tensor_tensor(out=dst, in0=src, scalar=sc, in1=Rsb[rows, :],
                                                            op0=ALU.mult, op1=ALU.mult), R["m"], *marks)
            R["pool" if eng is pool else "dve"] = m
            return m

        def v_sink(dst, got):
            def sink(t0, un, b, mk):
                for i in range(2):
                    m = act.do(lambda e, i=i: e.activation(
                        dst[:, t0 + i, 256 * un:256 * un + 256], ps[b][:, 256 * i:256 * i + 256], ACT.Copy,
                        scale=small[:, 4 + t0 + i:5 + t0 + i]), mk, R["col"])
                bank_free[b] = m
                got.append(m)
            return sink

        def R_sink(dst, got, scale=None):
            def sink(m, b, mk):
                bank_free[b] = x = times_R(dst[:, m, :], ps[b][:, :], mk, scale=scale)
                got.append(x)
            return sink

        s_c = [sem(f"s_c{i}") for i in range(4)]
        s_m = [sem(f"s_m{i}") for i in range(4)]
        eps6 = pool.do(lambda e: e.memset(small[:, 60:61], 1e-6))
        eps5 = pool.do(lambda e: e.memset(small[:, 61:62], 1e-5))
        class Soft:

            def __init__(self, c, tag, nP=3, width=1280):
                self.P = [sbt(c, f"P{tag}{i}", [128, width]) for i in range(nP)]
                self.PT = [sbt(c, f"PT{tag}{i}", [128, 4, 512]) for i in range(2)]
                self.st = sbt(c, f"st{tag}", [128, 4, 16])
                self.Pfree = [None] * nP
                self.PTfree = [None] * 2
                self.npt = 0
                self.n = 0

            def scores(self, u):
                u["i"] = self.n
                self.n += 1
                lay = u["lay"]
                bs = [bank() for _ in range(max(x[2] for x in lay) + 1)]
                u["b"] = bs
                u["sm"] = {}
                for t, L, bi, off in lay:
                    b = bs[bi]
                    msk = u.get("mask")
                    pe.wait(bank_free[b], *(u["qk"]() if callable(u["qk"]) else u["qk"]))
                    f = (lambda e, t=t, L=L, b=b, off=off: e.matmul(
                        ps[b][:, off:off + L], u["q"](t), u["k"](L), start=True, stop=msk is None))
                    if msk is None:
                        u["sm"][bi] = pe.do(f)
                    else:
                        pe.go(f)
                        u["sm"][bi] = pe.do(lambda e, L=L, b=b, off=off: e.matmul(
                            ps[b][:, off + L - 128:off + L], identb, msk, start=False, stop=True))

            def probs(self, u):
                lay, i = u["lay"], u["i"]
                P = self.P[i % len(self.P)]
                u["P"] = P
                st = self.st[:, i % 4, :]
                pf = self.Pfree[i % len(self.P)]
                rd = {}
                for t, L, bi, off in lay:
                    b = u["b"][bi]
                    src, o = ps[b][:, off:off + L], bi * 512 + off
                    if "bias" in u:
                        m = dve.do(lambda e, t=t, src=src, o=o, L=L: e.tensor_tensor_reduce(
                            P[:, o:o + L], src, u["bias"](L), 1.0, -3e38, ALU.add, ALU.max,
                            st[:, t:t + 1]), u["sm"][bi], pf, *u.get("bm", []))
                        bank_free[b] = m
                    else:
                        m = dve.do(lambda e, t=t, src=src: e.tensor_reduce(
                            st[:, t:t + 1], src, AX.X, ALU.max), u["sm"][bi])
                    rd[t] = m
                m = dve.do(lambda e: e.tensor_scalar(st[:, 4:8], st[:, 0:4], -1.0, None, ALU.mult), m)
                for t, L, bi, off in lay:
                    b = u["b"][bi]
                    o = bi * 512 + off
                    src = P[:, o:o + L] if "bias" in u else ps[b][:, off:off + L]
                    x = act.do(lambda e, t=t, src=src, o=o, L=L: e.activation(
                        P[:, o:o + L], src, ACT.Exp, bias=st[:, 4 + t:5 + t],
                        accum_out=st[:, 8 + t:9 + t]), m, pf)
                    if "bias" not in u:
                        bank_free[b] = x
                u["xm"] = x

            def scale(self, u):
                lay, P, x = u["lay"], u["P"], u["xm"]
                st = self.st[:, u["i"] % 4, :]
                rc = dve.do(lambda e: e.reciprocal(st[:, 12:16], st[:, 8:12]), x)
                if u.get("neg") is not None:
                    nm, nmm = u["neg"]
                    rc = dve.do(lambda e: e.tensor_scalar(st[:, 12:16], st[:, 12:16], nm, None, ALU.mult),
                                rc, nmm)
                prev = u.get("prev")
                ys = []
                for t, L, bi, off in lay:
                    o = bi * 512 + off
                    if prev is None:
                        eng = pool if L == 384 else dve
                        y = eng.do(lambda e, t=t, o=o, L=L: e.tensor_scalar(
                            P[:, o:o + L], P[:, o:o + L], st[:, 12 + t:13 + t], None, ALU.mult), rc)
                    else:
                        y = dve.do(lambda e, t=t, o=o, L=L: e.scalar_tensor_tensor(
                            out=P[:, o:o + L], in0=P[:, o:o + L], scalar=st[:, 12 + t:13 + t],
                            in1=prev["P"][:, o:o + L], op0=ALU.mult, op1=ALU.add), rc, *prev["pm"])
                    ys.append(y)
                if prev is not None:
                    self.Pfree[prev["i"] % len(self.P)] = y
                u["pm"] = ys

            def turn(self, u):
                if u.get("part"):
                    return
                lay = u["lay"]
                PT = self.PT[self.npt % 2]
                u["PT"] = PT
                u["ipt"] = self.npt
                ptf = self.PTfree[self.npt % 2]
                self.npt += 1
                bs = [bank() for _ in range(max(x[2] for x in lay) + 1)]
                mk = {}
                P = u["P"]
                for t, L, bi, off in lay:
                    b = bs[bi]
                    pe.wait(bank_free[b], *u["pm"])
                    for j in range(L // 128):
                        f = (lambda e, b=b, o=off + j * 128, s=bi * 512 + off + j * 128: e.transpose(
                            ps[b][:, o:o + 128], P[:, s:s + 128], ident))
                        if j == L // 128 - 1:
                            mk[bi] = pe.do(f)
                        else:
                            pe.go(f)
                self.Pfree[u["i"] % len(self.P)] = mk[bi]
                out = []
                for t, L, bi, off in lay:
                    b = bs[bi]
                    eng = act if bi == 0 else dve
                    src = ps[b][:, off:off + L].rearrange("p (j t) -> p j t", t=128)
                    bank_free[b] = copy(eng, PT[:, 0:L // 128, t * 128:t * 128 + 128], src, mk[bi], ptf)
                    out.append(bank_free[b])
                u["tm"] = out

            def values(self, u):
                if "sink" not in u:
                    return
                us = [u["pair"], u] if u.get("pair") else [u]
                b = bank()
                pe.wait(bank_free[b])
                nj = 2 if u["lay"] is FULL256 else 4
                for w in us:
                    pe.wait(*w["tm"])
                    pe.wait(*w["vm"])
                for j in range(nj):
                    t0 = 0 if nj == 2 else j * 128
                    for w in us:
                        f = (lambda e, j=j, t0=t0, w=w: e.matmul(
                            ps[b][w["rows"], t0:512], w["v"](j), w["PT"][:, j, t0:512],
                            start=(j == 0), stop=(j == nj - 1)))
                        if j == nj - 1:
                            m = pe.do(f)
                        else:
                            pe.go(f)
                for w in us:
                    self.PTfree[w["ipt"] % 2] = m
                u["sink"](b, m)

            def run(self, us, gens=(), per=0, before=None, after=None):
                n = len(us)
                for s in range(n + 3):
                    if s < n:
                        if before:
                            before(s)
                        self.scores(us[s])
                        self.probs(us[s])
                        if after:
                            after(s)
                    if 1 <= s <= n:
                        self.scale(us[s - 1])
                    fill(gens, per(s) if callable(per) else per)
                    if s >= 3:
                        self.values(us[s - 3])
                    if 2 <= s <= n + 1:
                        self.turn(us[s - 2])

        def to_parts(H, L, k, free, marks, km):
            def sink(b, m):
                hi = copy(act, H[:, k, :], ps[b][:, :], m, *free)
                lo = dve.do(lambda e: e.tensor_tensor(L[:, k, :], ps[b][:, :], H[:, k, :].bitcast(F32),
                                                      ALU.subtract), hi)
                bank_free[b] = lo
                marks[km] = [hi, lo]
            return sink

        def pair_units(nh, lay, q, k, v, kw, sink):
            us = []
            for h in range(nh):
                r = slice(64 * (h % 2), 64 * (h % 2) + 64)
                u = {"lay": lay, "q": q(h, r), "k": k(h, r), "v": v(h), "rows": r, "bank": None}
                u.update(kw(h))
                if h % 2:
                    u["pair"] = us[-1]
                    u["sink"] = sink(h // 2)
                us.append(u)
            return us

        def mem_load(cc, layer, lane=act):
            mr = sbt(cc, f"mr{layer}", [128, 8, 256])
            mH = sbt(cc, f"mH{layer}", [128, 8, 256], F32R)
            mL = sbt(cc, f"mL{layer}", [128, 8, 256], F32R)
            mv = memt.rearrange("p (k t) -> p k t", k=8)
            lds = [lane.load(lambda e, i=i: e.dma_start(mr[:, 2 * i:2 * i + 2, :], mv[:, 2 * i:2 * i + 2, :]),
                            s_m[i], 16 * (layer + 1)) for i in range(4)]
            return mr, mH, mL, lds

        def mem_parts(loaded):
            mr, mH, mL, lds = loaded
            marks = []
            for k in range(0, 8, 2):
                hi = copy(act, mH[:, k:k + 2, :], mr[:, k:k + 2, :], lds[k // 2])
                eng = (dve, pool)[k // 2 % 2]
                lo = eng.do(lambda e, k=k: e.tensor_tensor(mL[:, k:k + 2, :], mr[:, k:k + 2, :],
                                                            mH[:, k:k + 2, :].bitcast(F32), ALU.subtract), hi)
                marks += [[hi, lo], [hi, lo]]
            return mH, mL, marks

        def mem_kv(parts, mk_t, mv_t, between=None):
            mH, mL, marks = parts
            got = []

            def sink(m, b, mk):
                bank_free[b] = copy(act, mk_t[:, m, :], ps[b][:, 0:256], mk)
                got.append(bank_free[b])

            def vsink(t0, un, b, mk):
                bank_free[b] = copy(act, mv_t[:, t0:t0 + 2, :], ps[b][:, :].rearrange("p (t c) -> p t c", t=2),
                                    mk)
                got.append(bank_free[b])

            linear_fm(1, mH, mL, marks, sink, N=256)
            if between:
                convert_ahead(wst["next"] + 2)
                between()
            linear_tm(1, mH, mL, marks, vsink, ntt=2)
            return got

        def mem_units(qm, qmm, mk_t, mv_t, kvm, MH, ML, marks):
            return pair_units(
                4, FULL256,
                lambda h, r: (lambda t: qm[r, h // 2, t * 128:t * 128 + 128]),
                lambda h, r: (lambda L: mk_t[r, h // 2, 0:256]),
                lambda h: (lambda j: mv_t[:, j, 64 * h:64 * h + 64]),
                lambda h: {"qk": [qmm, kvm], "vm": kvm},
                lambda tile: to_parts(MH, ML, tile, [], marks, 6 + tile))

        def ffn(tag, h, conv, then=None, gain=None):
            c = ExitStack()
            fen = fence()
            for x in (act, dve, pool):
                x.wait(*fen)
            fH = sbt(c, f"fH{tag}", [128, 12, 512], F32R)
            fL = sbt(c, f"fL{tag}", [128, 12, 512], F32R)
            Y = [sbt(c, f"Y{tag}{i}", [128, 512]) for i in range(4)]
            Z = [sbt(c, f"Z{tag}{i}", [128, 512]) for i in range(2)]
            GG = [sbt(c, f"GG{tag}{i}", [128, 512]) for i in range(2)]
            gfree = [None] * 2
            yfree = [None] * 4
            zfree = [None] * 2
            ffree = [None]
            for half, (j0, j1, ks) in enumerate(((0, 6, (4, 4, 4)), (6, 11, (4, 3, 3)))):
                fm = {}
                ym = {}

                def gsink(m, b, mk):
                    y, gg = Y[m % 4], GG[m % 2]
                    bank_free[b] = g = times_R(gg[:, :], ps[b][:, :], mk, gfree[m % 2])
                    if conv is None:
                        gfree[m % 2] = s = act.do(lambda e: e.activation(y[:, :], gg[:, :], ACT.Silu), g,
                                                  yfree[m % 4])
                    else:
                        fw, fb = conv
                        s = act.do(lambda e: e.activation(y[:, :], gg[:, :], ACT.Identity,
                                                          bias=col(fb, m), scale=col(fw, 44 + m)),
                                   g, yfree[m % 4])
                        for d, w in ((1, 22 + m), (2, m)):
                            s = dve.do(lambda e, d=d, w=w: e.scalar_tensor_tensor(
                                out=y[:, d:512], in0=gg[:, 0:512 - d], scalar=col(fw, w),
                                in1=y[:, d:512], op0=ALU.mult, op1=ALU.add), s)
                        gfree[m % 2] = s
                        s = act.do(lambda e: e.activation(y[:, :], y[:, :], ACT.Silu), s)
                    ym[m] = R["pool"] = pool.do(
                        lambda e: e.tensor_tensor(y[:, :], y[:, :], Rsb[:, :], ALU.mult), s, R["m"])

                def usink(m, b, mk):
                    y, z, k = Y[m % 4], Z[m % 2], m - 2 * j0
                    bank_free[b] = yfree[m % 4] = s = dve.do(lambda e: e.tensor_tensor(
                        z[:, :], ps[b][:, :], y[:, :], ALU.mult), mk, ym[m], zfree[m % 2])
                    hi = copy(act, fH[:, k, :], z[:, :], s, ffree[0])
                    lo = pool.do(lambda e: e.tensor_tensor(fL[:, k, :], z[:, :], fH[:, k, :].bitcast(F32),
                                                           ALU.subtract), hi, ffree[0])
                    zfree[m % 2] = lo
                    fm[k] = [hi, lo]

                for j in range(j0, j1):
                    linear_fm(1, hH, hL, h, gsink, m0=2 * j)
                    linear_fm(1, hH, hL, h, usink, m0=2 * j)
                hread = pe.last()
                res = residual(half == 1, (lambda m: then(m, hread)) if then else None,
                               dve if gain else pool)
                for mg in range(2):
                    bs = [bank() for _ in range(4)]
                    k0 = 0
                    for gi, nk in enumerate(ks):
                        n, _, _, ncl, (wh, wl) = take()
                        for mi in range(4):
                            b = bs[mi]
                            pe.wait(bank_free[b])
                            for kk in range(nk):
                                pe.wait(*fm[k0 + kk])
                                for i, (w, x) in enumerate(((wh, fH), (wh, fL), (wl, fH))):
                                    f = (lambda e, b=b, w=w, x=x, k=k0 + kk, kk=kk, mi=mi, i=i, gi=gi, nk=nk: e.matmul(
                                        ps[b][:, :], w[:, kk, mi * 128:mi * 128 + 128], x[:, k, :],
                                        start=(gi == 0 and kk == 0 and i == 0),
                                        stop=(gi == len(ks) - 1 and kk == nk - 1 and i == 2)))
                                    if kk == nk - 1 and i == 2:
                                        mk = pe.do(f)
                                    else:
                                        pe.go(f)
                            if gi == len(ks) - 1:
                                res(4 * mg + mi, b, mk)
                                if gain and half:
                                    m = 4 * mg + mi
                                    x_mark[m] = act.do(lambda e, m=m: e.activation(
                                        X[:, m, :], X[:, m, :], ACT.Copy, scale=col(gain, m)), x_mark[m])
                                    if m == 7:
                                        rstd(61)
                        w_free[n] = mk
                        k0 += nk
                ffree[0] = mk
            c.close()

        s_x = [sem(f"s_x{i}") for i in range(8)]
        xv = xt.rearrange("p (k t) -> p k t", k=8)
        A = ExitStack()
        q, mixL = sbt2(A, "q", [128, 6, 512])
        kk_, mixH = sbt2(A, "k", [128, 6, 512])
        v = sbt(A, "v", [128, 4, 768])
        O = sbt(A, "O", [128, 6, 512])
        MH = sbt(A, "MHA", [128, 2, 512], F32R)
        ML = sbt(A, "MLA", [128, 2, 512], F32R)
        Mrow = sbt(A, "Mrow", [4, 512])
        colA = sbt(A, "colA", [128, 4, 4])
        Erow = sbt(A, "Erow", [4, 512])
        M = ExitStack()
        qm = sbt(M, "qm", [128, 2, 512])
        mkA = sbt(M, "mkA", [128, 2, 256])
        mvA = sbt(M, "mvA", [128, 2, 256])
        T = ExitStack()
        w_load(0)
        loaded = mem_load(T, 0, sp)
        c_cols = sp.load(lambda e: e.dma_start(cols[:, :], colsd), s_c[0], 16)
        c_K = sp.load(lambda e: e.dma_start(K[:, :, :], consts.rearrange("p (i c) -> p i c", i=5)), s_c[1], 16)
        w_load(1)
        h = [None] * 8
        for k in range(8):
            x_mark[k] = sp.load(lambda e, k=k: e.dma_start(X[:, k, :], xv[:, k, :]), s_x[k], 16)
        for i, j in ((0, 0), (1, 2), (2, 3)):
            pool.do(lambda e, i=i, j=j: e.tensor_copy(KB[:, i, :], K[:, j, :]), c_K)
        for x in (act, dve, pool):
            x.wait(eps5)
        act.do(lambda e: e.activation(small[:, 62:63], small[:, 60:61], ACT.Copy), eps6)

        def x_ready():
            act.wait(c_cols)
            dve.wait(c_cols, c_K)
            pe.wait(c_K)
            convert_ahead(2)
            for k in range(8):
                scaled(k, col("mix0", k), None, h)

        convert_ahead(1)
        parts = mem_parts(loaded)
        x_ready()
        kvm = mem_kv(parts, mkA, mvA)
        T.close()
        convert_ahead(4)
        for k in range(8):
            square(k, x_mark[k], dve, pool if k % 2 else act)
        rstd(60)
        G = O[0:8, 0, :]
        G2 = [O[0:4, 1, :], O[0:4, 2, :], O[0:4, 3, :], Mrow[:, :]]
        gm = {}

        def gate_sink(m, b, mk):
            bank_free[b] = gm["G"] = times_R(G, ps[b][0:8, :], mk, scale=(None, slice(0, 8)))
            timed.extend([[1, gates_later], [2, gates_rest], [9, gate_columns]])

        def gates_later():
            b = bank()
            m = pe.do(lambda e: e.matmul(ps[b][0:4, :], ident[0:8, 4:8], G, start=True, stop=True),
                      gm["G"], bank_free[b])
            z, t, a, mm = G2
            bank_free[b] = m = dve.do(lambda e: e.tensor_scalar(z, ps[b][0:4, :], col("gf", p=slice(0, 4)),
                                                                None, ALU.add), m)
            m1 = dve.do(lambda e: e.scalar_tensor_tensor(out=t, in0=z, scalar=-1.0, in1=z, op0=ALU.mult,
                                                         op1=ALU.max), m)
            m1 = act.do(lambda e: e.activation(t, t, ACT.Exp, scale=-1.0), m1)
            gm["ln"] = act.do(lambda e: e.activation(t, t, ACT.Ln, bias=1.0), m1)

        def gates_rest():
            z, t, a, mm = G2
            m2 = dve.do(lambda e: e.tensor_scalar(z, z, -1.0, 0.0, ALU.mult, ALU.max), gm["ln"])
            m2 = dve.do(lambda e: e.tensor_tensor(t, t, z, ALU.add), m2)
            onem = dve.do(lambda e: e.memset(a, 1.0))
            m2 = dve.do(lambda e: e.tensor_tensor_scan(z, a, t, 0.0, ALU.mult, ALU.add), m2, onem)
            m3 = dve.do(lambda e: e.tensor_scalar(t, O[0:4, 0, :], col("gi", p=slice(0, 4)), None, ALU.add), m2)
            m3 = dve.do(lambda e: e.tensor_tensor(t, t, z, ALU.add), m3)
            m4 = dve.do(lambda e: e.tensor_tensor_scan(mm, a, t, 0.0, ALU.mult, ALU.max), m3)
            m5 = dve.do(lambda e: e.tensor_tensor(z, z, mm, ALU.subtract), m4)
            gm["rows"], gm["m"] = m4, m5

        def gate_columns():
            z, t, _, _ = G2
            b2 = bank()
            pe.wait(bank_free[b2], gm["m"])
            for i in range(4):
                m = pe.do(lambda e, i=i: e.transpose(ps[b2][:, 4 * i:4 * i + 4], t[:, i * 128:i * 128 + 128],
                                                     ident[0:4, 0:4]))
            bank_free[b2] = gm["col"] = copy(dve, colA[:, :, :],
                                             ps[b2][:, 0:16].rearrange("p (i c) -> p i c", i=4), m)
            gm["em"] = act.do(lambda e: e.activation(Erow[:, :], z, ACT.Exp), gm["m"])

        qmm, qkm, vm, om = [], {}, [], {}
        linear_fm(1, hH, hL, h, gate_sink)
        linear_fm(1, hH, hL, h, R_sink(qm, qmm, 0.125))

        def conv_sink(dst, base):
            def sink(m, b, mk):
                y, i = dst[:, m, :], m % 2
                bank_free[b] = g = times_R(sq[i][:, :], ps[b][:, :], mk, sq_free[i])
                s = act.do(lambda e: e.activation(y, sq[i][:, :], ACT.Identity, bias=col("cb", base + m),
                                                  scale=col("cw", 36 + base + m)), g)
                for d in (1, 2, 3):
                    s = dve.do(lambda e, d=d: e.scalar_tensor_tensor(
                        out=dst[:, m, d:512], in0=sq[i][:, 0:512 - d], scalar=col("cw", 12 * (3 - d) + base + m),
                        in1=dst[:, m, d:512], op0=ALU.mult, op1=ALU.add), s)
                sq_free[i] = s

                def silu():
                    qkm[(base, m)] = act.do(lambda e: e.activation(y, y, ACT.Silu), s)

                deferred.append(silu)
            return sink

        def o_sink(m, b, mk):
            bank_free[b] = x = times_R(O[:, m, :], ps[b][:, :], mk)
            om[m] = act.do(lambda e: e.activation(O[:, m, :], O[:, m, :], ACT.Sigmoid), x)

        fen = fence()
        for x in (act, dve, pool):
            x.wait(*fen)
        def qk_unit(j):
            return [g_linear_fm(1, hH, hL, h, conv_sink(q, 0), m0=2 * j),
                    g_linear_fm(1, hH, hL, h, conv_sink(kk_, 6), m0=2 * j)]

        gens = qk_unit(0) + qk_unit(1) + [g_linear_tm(2, hH, hL, h, v_sink(v, vm))]
        gens += qk_unit(2) + [g_linear_tm(1, hH, hL, h, v_sink(v, vm), u0=2)]
        S = Soft(M, "mA", width=1024)
        fill(gens, 2)
        mix = [None] * 8
        S.run(mem_units(qm, qmm, mkA, mvA, kvm, MH, ML, mix), gens, 2,
              lambda s: convert_ahead(wst["next"] + 2) if s else None)
        M.close()
        fen = fence()
        for x in (act, dve, pool):
            x.wait(*fen)
        B = ExitStack()
        den = [sbt(B, f"den{i}", [128, 512]) for i in range(2)]
        fac = [sbt(B, f"fac{i}", [128, 512]) for i in range(2)]
        Mb = [sbt(B, f"Mb{i}", [128, 512]) for i in range(2)]
        Eb = sbt(B, "Eb", [128, 1280])
        Pm = [sbt(B, f"Pm{i}", [128, 1280]) for i in range(2)]
        gens.append(g_linear_fm(3, hH, hL, h, o_sink))

        SC = 192.0 ** -0.5
        JL = [(0, 512, 0, 0), (1, 384, 1, 0), (3, 128, 1, 384), (2, 256, 2, 0)]
        mbf = [None, None]
        pf = [None, None]
        eb_free = [None]
        numm = {}
        hs = {}

        def pieces(hd):
            t = 3 * (hd // 2)
            if hd % 2 == 0:
                return [(t, slice(0, 128), 192 * hd, 128), (t + 1, slice(0, 64), 192 * hd + 128, 64)]
            return [(t + 2, slice(0, 128), 192 * hd + 64, 128), (t + 1, slice(64, 128), 192 * hd, 64)]

        def m_scores(hd):
            bm = bank()
            m = pe.do(lambda e: e.matmul(ps[bm][:, :], ident[0:4, hd:hd + 1].broadcast_to([4, 128]), G2[3], start=True, stop=True),
                      gm["rows"], bank_free[bm])
            i = hd % 2
            bank_free[bm] = mb = copy(act, Mb[i][:, :], ps[bm][:, :], m, mbf[i])
            bs = [bank() for _ in range(3)]
            hs[hd] = {"b": bs, "s": {}}
            for j, L, bi, off in JL:
                pe.wait(bank_free[bs[bi]])
                for n, (t, r, _, _) in enumerate(pieces(hd)):
                    pe.wait(qkm[(0, t)], qkm[(6, t)])
                    f = (lambda e, j=j, L=L, b=bs[bi], off=off, t=t, r=r, n=n: e.matmul(
                        ps[b][:, off:off + L], kk_[r, t, j * 128:j * 128 + 128], q[r, t, j * 128:512],
                        start=(n == 0), stop=(n == 1)))
                    if n:
                        hs[hd]["s"][bi] = pe.do(f)
                    else:
                        pe.go(f)
            P = Pm[i]
            for j, L, bi, off in JL:
                o = bi * 512 + off
                m = dve.do(lambda e, j=j, o=o, L=L: e.tensor_scalar(
                    Eb[:, o:o + L], Mb[i][:, j * 128:512], colA[:, j, hd:hd + 1], 0.0,
                    ALU.subtract, ALU.max), mb, gm["col"], eb_free[0])
            mbf[i] = m
            m = act.do(lambda e: e.activation(Eb[:, 0:1280], Eb[:, 0:1280], ACT.Exp, scale=-1.0), m)
            for j, L, bi, off in JL:
                o = bi * 512 + off
                b = bs[bi]
                y = dve.do(lambda e, o=o, L=L, b=b, off=off: e.scalar_tensor_tensor(
                    out=P[:, o:o + L], in0=ps[b][:, off:off + L], scalar=SC, in1=Eb[:, o:o + L],
                    op0=ALU.mult, op1=ALU.mult), m, hs[hd]["s"][bi], pf[i])
                bank_free[b] = y
            eb_free[0] = y
            for j, L, bi, off in JL:
                o = bi * 512 + off
                z = pool.do(lambda e, o=o: e.affine_select(
                    out=P[:, o:o + 128], in_=P[:, o:o + 128], compare_op=ALU.is_ge, fill=0.0, base=0,
                    pattern=[[1, 128]], channel_multiplier=-1), y)
            hs[hd]["P"] = z

        nb = {}
        fins, normed = {}, {}

        def m_values(hd):
            P = Pm[hd % 2]
            pos = {j: bi * 512 + off for j, L, bi, off in JL}
            pe.wait(hs[hd]["P"], *vm)
            squares = []
            for t, r, c0, w in pieces(hd):
                if t not in nb:
                    nb[t] = bank(w == 64)
                    pe.wait(bank_free[nb[t]])
                b = nb[t]
                for j in range(4):
                    o = pos[j]
                    f = (lambda e, b=b, j=j, r=r, c0=c0, w=w, o=o: e.matmul(
                        ps[b][r, j * 128:512], v[:, j, c0:c0 + w], P[:, o:o + 512 - j * 128],
                        start=(j == 0), stop=(j == 3)))
                    if j == 3:
                        mk = pe.do(f)
                    else:
                        pe.go(f)
                m = copy(act, q[r, t, :], ps[b][r, :], mk)
                numm[(t, r.start)] = bank_free[b] = m
                if r.start == 64:
                    release(b)
                si = t % 2
                s2 = (pool if w == 128 else dve).do(lambda e, r=r, t=t, si=si: e.tensor_tensor(
                    sq[si][r, :], q[r, t, :], q[r, t, :], ALU.mult), m, sq_free[si])
                squares.append((r, si, s2))
            bd, be = bank(), bank()
            pe.wait(bank_free[bd])
            for j in range(4):
                f = (lambda e, j=j: e.matmul(ps[bd][:, j * 128:512], ones, P[:, pos[j]:pos[j] + 512 - j * 128],
                                             start=(j == 0), stop=(j == 3)))
                if j == 3:
                    mk = pe.do(f)
                else:
                    pe.go(f)
            pf[hd % 2] = mk
            me = pe.do(lambda e: e.matmul(ps[be][:, :], ident[0:4, hd:hd + 1].broadcast_to([4, 128]),
                                          Erow[:, :], start=True, stop=True), gm["em"], bank_free[be])
            i = hd % 2
            D = den[i][:, :]
            bank_free[be] = m = copy(act, D, ps[be][:, :], me, fins.get(hd - 2))
            m = dve.do(lambda e: e.tensor_tensor(D, ps[bd][:, :], D, ALU.max), mk, m)
            bank_free[bd] = m = dve.do(lambda e: e.scalar_tensor_tensor(
                out=D, in0=ps[bd][:, :], scalar=-1.0, in1=D, op0=ALU.mult, op1=ALU.max), m)
            deferred.append(lambda: sums(hd, squares, m))

        def sums(hd, squares, dm):
            D, F = den[hd % 2][:, :], fac[hd % 2][:, :]
            bs = bank()
            pe.wait(bank_free[bs])
            for n, (r, si, s2) in enumerate(squares):
                sq_free[si] = m = pe.do(lambda e, r=r, si=si, n=n: e.matmul(
                    ps[bs][:, :], ones[r, :], sq[si][r, :], start=(n == 0), stop=(n == 1)), s2)
            d2 = act.do(lambda e: e.activation(D, D, ACT.Square, scale=1e-3), dm)
            bank_free[bs] = m = dve.do(lambda e: e.scalar_tensor_tensor(
                out=F, in0=ps[bs][:, :], scalar=1.0 / 192, in1=D, op0=ALU.mult, op1=ALU.add), m, d2)
            fins[hd] = m
            m = dve.do(lambda e: e.tensor_scalar(F, F, 1e-34, 1e35, ALU.max, ALU.min), m)
            m = act.do(lambda e: e.activation(F, F, ACT.Sqrt), m)
            m = dve.do(lambda e: e.reciprocal(F, F), m)
            for t, r, _, _ in pieces(hd):
                normed[(t, r.start)] = dve.do(lambda e, t=t, r=r: e.scalar_tensor_tensor(
                    out=q[r, t, :], in0=q[r, t, :], scalar=col("hg", t, p=r), in1=fac[hd % 2][r, :],
                    op0=ALU.mult, op1=ALU.mult), m, numm[(t, r.start)])

        def gated(t):
            m = pool.do(lambda e: e.tensor_tensor(q[:, t, :], q[:, t, :], O[:, t, :], ALU.mult),
                       [normed[x] for x in normed if x[0] == t], om[t])
            hi = copy(act, mixH[:, t, :], q[:, t, :], m)
            mix[t] = [hi, dve.do(lambda e: e.tensor_tensor(mixL[:, t, :], q[:, t, :],
                                                           mixH[:, t, :].bitcast(F32), ALU.subtract), hi)]

        class Out:

            def __init__(self, H0, L0, H1, L1, k1, order, early):
                self.H = lambda k: H1[:, k - k1, :] if k >= k1 else H0[:, k, :]
                self.L = lambda k: L1[:, k - k1, :] if k >= k1 else L0[:, k, :]
                self.order, self.early, self.open = order, early, []

            def part(self, wh, wl, c, b, ks):
                for k in ks:
                    pe.wait(mix[k])
                    for i, (w, x) in enumerate(((wh, self.H(k)), (wh, self.L(k)), (wl, self.H(k)))):
                        end = k == self.order[-1] and i == 2
                        f = (lambda e, w=w, x=x, k=k, i=i, end=end: e.matmul(
                            ps[b][:, :], w[:, k, c:c + 128], x, start=(k == self.order[0] and i == 0), stop=end))
                        if end:
                            return pe.do(f)
                        pe.go(f)

            def first(self):
                for u in range(2):
                    n, _, _, _, (wh, wl) = take(2 if u == 0 else 1)
                    for c in (0, 128):
                        b = bank(True)
                        pe.wait(bank_free[b])
                        self.part(wh, wl, c, b, self.order[:self.early])
                        self.open.append((n, wh, wl, c, b))
                        yield

            def rest(self, g):
                h = [None] * 8
                res = residual(True, lambda m: scaled(m, g(m), None, h))
                for m, (n, wh, wl, c, b) in enumerate(self.open):
                    mk = self.part(wh, wl, c, b, self.order[self.early:])
                    if c:
                        w_free[n] = mk
                        convert_ahead(n + 3)
                    release(b)
                    tile_done(res, m, b, mk)
                for u in range(2, 4):
                    n, _, _, _, (wh, wl) = take()
                    for c in (0, 128):
                        b = bank()
                        pe.wait(bank_free[b])
                        mk = self.part(wh, wl, c, b, self.order)
                        if c:
                            w_free[n] = mk
                        tile_done(res, 2 * u + (c > 0), b, mk)
                return h

        outA = Out(mixH, mixL, MH, ML, 6, [6, 7, 0, 1, 2, 3, 5, 4], 5)
        tiles = ((0, 1, 0), (1, 1, 1), (0, 1, 1), (0, 0, 1))
        m_scores(0)
        for hd in range(4):
            fill(gens, tiles[hd][0])
            if hd < 3:
                m_scores(hd + 1)
            fill(gens, tiles[hd][1])
            m_values(hd)
            fill(gens, tiles[hd][2])
            if hd == 2:
                for t in range(3):
                    gated(t)
        run_deferred()
        fill(gens, 99)
        early = [outA.first()]
        fill(early, 1)
        for t in (3, 5, 4):
            gated(t)
        fill(early, 3)
        B.close()

        h = outA.rest(lambda k: col("ffn0", k))
        A.close()
        rstd(60)

        s_out = sem("s_out")

        def body(h):
            hn = [None] * 8
            ffn("a", h, ("fw0", "fb0"), lambda m, rd: scaled(m, col("kv", m), rd, hn))
            h = hn
            rstd(60)
            fen = fence()
            for x in (act, dve, pool):
                x.wait(*fen)
            A = ExitStack()
            k, mixL = sbt2(A, "kB", [128, 6, 512])
            v = sbt(A, "vB", [128, 4, 768])
            qm = sbt(A, "qmB", [128, 2, 512])
            mk_t = sbt(A, "mkB", [128, 2, 256])
            mv_t = sbt(A, "mvB", [128, 2, 256])
            T = ExitStack()
            loaded = mem_load(T, 1)
            km, qmk, qmm, vm = [], [], [], []
            linear_fm(3, hH, hL, h, R_sink(k, km))
            parts = mem_parts(loaded)
            linear_tm(3, hH, hL, h, v_sink(v, vm))
            rd, h = pe.last(), [None] * 8
            convert_ahead(wst["next"] + 2)
            for i in range(4):
                scaled(i, col("mix1", i), rd, h)
            kvm = mem_kv(parts, mk_t, mv_t, lambda: [scaled(i, col("mix1", i), rd, h) for i in range(4, 8)])
            T.close()
            q, mixH = sbt2(A, "qB", [128, 6, 512])
            MH = sbt(A, "MHB", [128, 2, 512], F32R)
            ML = sbt(A, "MLB", [128, 2, 512], F32R)
            linear_fm(1, hH, hL, h, R_sink(qm, qmm, 0.125))
            gens = [g_linear_fm(3, hH, hL, h, R_sink(q, qmk, 0.125))]
            fen = fence()
            for x in (act, dve, pool):
                x.wait(*fen)
            C = ExitStack()
            bias = [sbt(C, f"bias{i}", [128, 512]) for i in range(3)]
            s_b = [sem(f"s_b{i}") for i in range(3)]
            S = Soft(C, "B")
            mix[:] = [None] * 8
            bmm = {}
            bfree = [None] * 3

            def load_bias(h):
                i = h % 3
                l = act.load(lambda e: e.dma_start(bias[i][:, :], biasd[:, h * 512:h * 512 + 512]), s_b[i],
                             16 * (h // 3 + 1), bfree[i])
                bmm[h] = pool.do(lambda e: e.memset(bias[i][0:64, 448:512], NEG), l)

            us = mem_units(qm, qmm, mk_t, mv_t, kvm, MH, ML, mix)
            us += pair_units(
                12, CAUSAL,
                lambda h, r: (lambda t: q[r, h // 2, t * 128:t * 128 + 128]),
                lambda h, r: (lambda L: k[r, h // 2, 0:L]),
                lambda h: (lambda j: v[:, j, 64 * h:64 * h + 64]),
                lambda h: {"qk": lambda: [qmk[h // 2], km], "vm": vm, "bias": lambda L: bias[h % 3][:, 512 - L:512]},
                lambda tile: to_parts(mixH, mixL, tile, [], mix, tile))

            def before(s):
                if s >= 4:
                    us[s]["bm"] = [bmm[s - 4]]

            def after(s):
                if s >= 4:
                    bfree[(s - 4) % 3] = dve.last()
                if 1 <= s - 2 < 12:
                    load_bias(s - 2)

            load_bias(0)
            outB = Out(mixH, mixL, MH, ML, 6, [6, 7, 0, 1, 2, 3, 4, 5], 6)
            gens.append(outB.first())
            S.run(us, gens, lambda s: {16: 2, 17: 1, 18: 1}.get(s, s in (0, 1, 3, 5, 8, 11)), before, after)
            C.close()
            A.close()
            h = outB.rest(lambda k: col("ffn1", k))
            rstd(60)
            D = ExitStack()
            fen = fence()
            dve.wait(*fen)
            pool.wait(*fen)
            acc2 = sbt(D, "acc2", [128, 512])
            gg = sbt(D, "gg", [128, 8])
            ggm = dve.do(lambda e: e.tensor_tensor(gg[:, :], col("final", 0, 8), col("n1", 0, 8), ALU.mult))
            act.wait(ggm)
            dve.wait(ggm)
            hn = [None] * 8
            a2 = {}

            def then(m, rd):
                scaled(m, gg[:, m:m + 1], rd, hn)
                if m == 0:
                    a2["m"] = act.do(lambda e: e.activation(acc2[:, :], X[:, 0, :], ACT.Square,
                                                            scale=col("final")), x_mark[0])
                    return
                i = (m + 1) % 2
                x = act.do(lambda e: e.activation(sq[i][:, :], X[:, m, :], ACT.Square, scale=col("final", m)),
                           x_mark[m], sq_free[i])
                a2["m"] = sq_free[i] = dve.do(lambda e: e.tensor_tensor(
                    acc2[:, :], acc2[:, :], sq[i][:, :], ALU.add), x, a2["m"])

            ffn("b", h, ("fw1", "fb1"), then)
            h = hn
            xs = [list(m) for m in h]

            def first():
                b = bank()
                pe.wait(bank_free[b])
                acc_free[0] = m = token_sums(acc, acc_mark[0], b, 0)
                m2 = token_sums(acc2, a2["m"], b, 4)
                m = act.do(lambda e: e.activation(small[:, 0:4], ps[b][:, 0:4], ACT.Sqrt,
                                                  bias=small[:, 60:61], scale=1.0 / 1024), m2)
                m = dve.do(lambda e: e.reciprocal(small[:, 32:36], small[:, 0:4]), m)
                R["r1"] = m
                m = dve.do(lambda e: e.scalar_tensor_tensor(
                    out=small[:, 40:44], in0=ps[b][:, 4:8], scalar=1.0 / 1024, in1=small[:, 32:36],
                    op0=ALU.mult, op1=ALU.mult), m)
                bank_free[b] = m
                m = dve.do(lambda e: e.tensor_tensor(small[:, 40:44], small[:, 40:44], small[:, 32:36],
                                                     ALU.mult), m)
                m = act.do(lambda e: e.activation(small[:, 44:48], small[:, 40:44], ACT.Sqrt,
                                                  bias=small[:, 61:62]), m)
                m = dve.do(lambda e: e.reciprocal(small[:, 36:40], small[:, 44:48]), m)
                R["col"] = dve.do(lambda e: e.tensor_tensor(small[:, 4:8], small[:, 36:40], small[:, 32:36],
                                                            ALU.mult), m, act.last())

            def second():
                b = bank()
                m = bcast(small[:, 4:8], R["col"], bnk=b)
                bank_free[b] = R["m"] = copy(act, Rsb[:, :], ps[b][:, :], m, R.get("dve"), R.get("pool"))
                b = bank()
                m = bcast(small[:, 32:36], R["r1"], bnk=b)
                bank_free[b] = R["m1"] = copy(act, acc2[:, :], ps[b][:, :], m)

            norm_steps.extend([first, second])
            A = ExitStack()
            dq, dmL = sbt2(A, "dq", [128, 4, 512])
            dk, dmH = sbt2(A, "dk", [128, 4, 512])
            fq, fmH = sbt2(A, "fq", [128, 4, 512])
            fk, fmL = sbt2(A, "fk", [128, 4, 512])
            dv = sbt(A, "dv", [128, 4, 512])
            fv = sbt(A, "fv", [128, 4, 512])
            ncum = sbt(A, "ncum", [8, 512])
            B = ExitStack()
            RC = sbt(B, "RC", [128, 512])
            RS = sbt(B, "RS", [128, 512])
            U1 = [sbt(B, f"U1{i}", [128, 512]) for i in range(2)]
            U2 = [sbt(B, f"U2{i}", [128, 512]) for i in range(2)]
            Gf = sbt(B, "Gf", [128, 512])
            g3 = [sbt(B, f"g3{i}", [8, 512]) for i in range(3)]
            fen = fence()
            for x in (act, dve, pool):
                x.wait(*fen)
            c_r1 = act.load(lambda e: e.dma_start(RC[:, :], rope[:, 0:512]), s_c[2], 16)
            c_r2 = act.load(lambda e: e.dma_start(RS[:, :], rope[:, 512:1024]), s_c[3], 16)
            fgm = {}

            def fg_sink(m, b, mk):
                bank_free[b] = fgm["G"] = times_R(Gf[96:128, :], ps[b][96:128, :], mk,
                                                  scale=(None, slice(96, 128)))
                timed.extend([[0, fg_later], [1, fg_rest]])

            def fg_later():
                b = bank()
                m = pe.do(lambda e: e.matmul(ps[b][0:8, :], ident[96:128, 120:128], Gf[96:128, :],
                                             start=True, stop=True), fgm["G"], bank_free[b])
                z, t, a = g3
                bank_free[b] = m = dve.do(lambda e: e.tensor_scalar(z[:, :], ps[b][0:8, :], col("bf", p=slice(0, 8)),
                                                                    None, ALU.add), m)
                m1 = dve.do(lambda e: e.scalar_tensor_tensor(out=t[:, :], in0=z[:, :], scalar=-1.0, in1=z[:, :],
                                                             op0=ALU.mult, op1=ALU.max), m)
                m1 = act.do(lambda e: e.activation(t[:, :], t[:, :], ACT.Exp, scale=-1.0), m1)
                fgm["ln"] = act.do(lambda e: e.activation(t[:, :], t[:, :], ACT.Ln, bias=1.0), m1)

            def fg_rest():
                z, t, a = g3
                m2 = dve.do(lambda e: e.tensor_scalar(z[:, :], z[:, :], -1.0, 0.0, ALU.mult, ALU.max), fgm["ln"])
                m2 = dve.do(lambda e: e.tensor_tensor(t[:, :], t[:, :], z[:, :], ALU.add), m2)
                onem = dve.do(lambda e: e.memset(a[:, :], 1.0))
                fgm["n"] = dve.do(lambda e: e.tensor_tensor_scan(ncum[:, :], a[:, :], t[:, :], 0.0, ALU.mult,
                                                                 ALU.add), m2, onem)

            lm = dve.do(lambda e: e.tensor_tensor(small[0:64, 8:10], col("lam", 0, 2, slice(0, 64)),
                                                  col("lam", 2, 2, slice(0, 64)), ALU.mult))
            lmx = {}

            def lam_later():
                bl = bank()
                x = pe.do(lambda e: e.matmul(ps[bl][:, 0:2], ones[0:64, :], small[0:64, 8:10], start=True,
                                             stop=True), lm, bank_free[bl])
                bank_free[bl] = x = act.do(lambda e: e.activation(small[:, 10:12], ps[bl][:, 0:2], ACT.Exp), x)
                x = dve.do(lambda e: e.tensor_tensor(small[:, 12:13], small[:, 11:12], small[:, 10:11],
                                                     ALU.subtract), x)
                lmx["m"] = dve.do(lambda e: e.tensor_scalar(small[:, 12:13], small[:, 12:13], -0.2, None,
                                                            ALU.add), x)

            deferred.append(lam_later)
            u1f, u2f = [None] * 2, [None] * 2
            dqm, dkm = [], []

            def rope_sink(dst, lst, scale, cnt=[0]):
                def sink(m, b, mk):
                    i = cnt[0] % 2
                    cnt[0] += 1
                    bank_free[b] = a = times_R(U1[i][:, :], ps[b][:, :], mk, u1f[i], scale=scale)

                    def later():
                        b2 = bank()
                        r = pe.do(lambda e: e.matmul(ps[b2][:, :], rotm, U1[i][:, :], start=True, stop=True),
                                  a, bank_free[b2])
                        x = dve.do(lambda e: e.tensor_tensor(U2[i][:, :], ps[b2][:, :], RS[:, :], ALU.mult),
                                   r, c_r2, u2f[i])
                        bank_free[b2] = x
                        y = pool.do(lambda e: e.tensor_tensor(dst[:, m, :], U1[i][:, :], RC[:, :], ALU.mult),
                                    a, c_r1)
                        u1f[i] = [r, y]
                        z = dve.do(lambda e: e.tensor_tensor(dst[:, m, :], dst[:, m, :], U2[i][:, :], ALU.add), x, y)
                        u2f[i] = z
                        lst.append(z)
                    deferred.append(later)
                return sink

            dvm, fqm, fkm, fvm = [], [], [], []
            linear_fm(1, hH, hL, h, fg_sink)
            linear_fm(2, hH, hL, h, rope_sink(dq, dqm, 0.125))
            for kx in range(8):
                x_mark[kx] = dve.do(lambda e, kx=kx: e.scalar_tensor_tensor(
                    out=X[:, kx, :], in0=X[:, kx, :], scalar=col("final", kx), in1=acc2[:, :],
                    op0=ALU.mult, op1=ALU.mult), R["m1"], xs[kx])
            linear_fm(2, hH, hL, h, rope_sink(dk, dkm, 1.0))
            linear_tm(2, hH, hL, h, v_sink(dv, dvm))
            run_deferred()
            gens = []
            for j in range(2):
                gens += [g_linear_fm(1, hH, hL, h, R_sink(fq, fqm, 0.125), m0=2 * j),
                         g_linear_fm(1, hH, hL, h, R_sink(fk, fkm), m0=2 * j),
                         g_linear_tm(1, hH, hL, h, v_sink(fv, fvm), u0=j)]
            B.close()
            fen = fence()
            for x in (act, dve, pool):
                x.wait(*fen)
            C = ExitStack()
            S = Soft(C, "C", 3)
            CB = [sbt(C, f"CB{i}", [128, 512]) for i in range(2)]
            mix[:] = [None] * 8
            post = []

            def od_sink(hd):
                def sink(b, m):
                    i, od = hd % 2, dq[:, hd, :]
                    bank_free[b] = a = copy(act, od, ps[b][:, :], m, scale=2.0 ** -40)
                    a = dve.do(lambda e: e.tensor_scalar(od, od, 2.0 ** 60, -2.0 ** 60, ALU.min, ALU.max), a)
                    ss = small[:, 16 + 8 * i:24 + 8 * i]
                    pm = {}

                    def one():
                        x = pool.do(lambda e: e.tensor_tensor(sq[i][:, :], od, od, ALU.mult), a, sq_free[i])
                        pm["s"] = x

                    def two():
                        b2 = bank()
                        pe.wait(bank_free[b2])
                        sq_free[i] = m = token_sums(sq[i], pm["s"], b2, 0)
                        m = dve.do(lambda e: e.tensor_scalar(
                            ss[:, 0:4], ps[b2][:, 0:4], 1.0 / 128, 1e-5 * 2.0 ** -80, ALU.mult, ALU.add), m)
                        m = dve.do(lambda e: e.reciprocal(ss[:, 4:8], ss[:, 0:4]), m)
                        m = act.do(lambda e: e.activation(ss[:, 0:4], ss[:, 4:8], ACT.Sqrt, scale=0.64), m)
                        pm["c"] = bank_free[b2] = dve.do(lambda e: e.scalar_tensor_tensor(
                            out=ss[:, 0:4], in0=ps[b2][:, 0:4], scalar=2.0 ** 48, in1=ss[:, 0:4],
                            op0=ALU.is_lt, op1=ALU.mult), m)

                    def three():
                        b3 = bank()
                        m = bcast(ss[:, 0:4], pm["c"], bnk=b3)
                        m = bank_free[b3] = dve.do(lambda e: e.scalar_tensor_tensor(
                            out=od, in0=od, scalar=col("sub"), in1=ps[b3][:, :], op0=ALU.mult, op1=ALU.mult), m)
                        hi = copy(act, dmH[:, hd, :], od, m)
                        mix[hd] = [hi, pool.do(lambda e: e.tensor_tensor(
                            dmL[:, hd, :], od, dmH[:, hd, :].bitcast(F32), ALU.subtract), hi)]
                    one()
                    post.extend([two, three])
                return sink

            us = []
            for hd in range(4):
                for mp in range(2):
                    r = slice(64 * mp, 64 * mp + 64)
                    u = {"lay": CAUSAL, "mask": mchunk,
                         "q": lambda t, r=r, hd=hd: dq[r, hd, t * 128:t * 128 + 128],
                         "k": lambda L, r=r, hd=hd: dk[r, hd, 0:L],
                         "qk": [dqm, dkm], "vm": dvm, "rows": slice(0, 128), "bank": None}
                    if mp == 0:
                        u["part"] = True
                    else:
                        u["prev"] = us[-1]
                        u["neg"] = (small[:, 12:13], lmx["m"])
                        u["v"] = lambda j, hd=hd: dv[:, j, hd * 128:hd * 128 + 128]
                        u["sink"] = od_sink(hd)
                    us.append(u)
            cbm = {}
            cbf = [None] * 2

            def load_cb(h):
                i = h % 2
                b = bank()
                m = pe.do(lambda e: e.matmul(ps[b][:, :], ident[0:8, h:h + 1].broadcast_to([8, 128]), ncum[:, :], start=True, stop=True),
                          fgm["n"], bank_free[b])
                bank_free[b] = cbm[h] = copy(act, CB[i][:, :], ps[b][:, :], m, cbf[i])

            us += pair_units(
                8, CAUSAL,
                lambda h, r: (lambda t: fq[r, h // 2, t * 128:t * 128 + 128]),
                lambda h, r: (lambda L: fk[r, h // 2, 0:L]),
                lambda h: (lambda j: fv[:, j, 64 * h:64 * h + 64]),
                lambda h: {"qk": lambda: [fqm[h // 2], fkm[h // 2]], "vm": fvm, "mask": mcaus, "bias": lambda L: CB[h % 2][:, 0:L]},
                lambda tile: to_parts(fmH, fmL, tile, [], mix, 4 + tile))

            def before(s):
                if s >= 8:
                    us[s]["bm"] = [cbm[s - 8]]

            def after(s):
                if s >= 8:
                    cbf[(s - 8) % 2] = dve.last()
                if 0 <= s - 7 < 8:
                    load_cb(s - 7)
                if s >= 5 and post:
                    post.pop(0)()

            outC = Out(dmH, dmL, fmH, fmL, 4, list(range(8)), 6)
            gens.append(outC.first())
            S.run(us, gens, lambda s: {16: 2, 17: 1, 18: 1}.get(s, s < 12), before, after)
            while post:
                post.pop(0)()
            C.close()
            h = outC.rest(lambda k: col("n2", k))
            A.close()
            D.close()
            rstd(61)
            ffn("c", h, None, None, "nf")
            while norm_steps:
                norm_steps.pop(0)()
            o = out.rearrange("p (k t) -> p k t", k=8)
            for kx in range(8):
                m = times_R(X[:, kx, :], X[:, kx, :], x_mark[kx], eng=pool if kx % 3 == 1 else dve)
                last = sp.load(lambda e, kx=kx: e.dma_start(o[:, kx, :], X[:, kx, :]),
                               s_out, 16 * (kx + 1), m)
            return last

        sp.wait(body(h))

        block = ctx.enter_context(nc.Block())

        @block.sync
        def _(e):
            sp.play(e)

        @block.scalar
        def _(e):
            act.play(e)

        @block.vector
        def _(e):
            dve.play(e)

        @block.gpsimd
        def _(e):
            pool.play(e)

        @block.tensor
        def _(e):
            pe.play(e)


def shape_constants():
    ident = np.eye(128, dtype=np.float32)
    ones = np.ones((128, 128), np.float32)
    chunk = np.zeros((128, 128), np.float32)
    chunk[0:64, 64:128] = NEG
    i = np.arange(128)
    causal = np.where(i[None, :] <= i[:, None], np.float32(0), np.float32(NEG)).astype(np.float32)
    rot = np.zeros((128, 128), np.float32)
    for b in (0, 64):
        for d in range(8):
            rot[b + d + 8, b + d] = -1.0
            rot[b + d, b + d + 8] = 1.0
    consts = np.concatenate([ident, ones, chunk, causal, rot], 1)
    inv = np.float32(500000.0) ** (-np.arange(0, 16, 2, dtype=np.float32) / np.float32(16))
    ang = np.arange(512, dtype=np.float32)[None, :] * inv.astype(np.float32)[:, None]
    C, S = np.ones((128, 512), np.float32), np.zeros((128, 512), np.float32)
    for b in (0, 8, 64, 72):
        C[b:b + 8] = np.cos(ang)
        S[b:b + 8] = np.sin(ang)
    return consts, np.concatenate([C, S], 1)


def kernel(**inputs):
    import concourse.bacc as _bacc
    from concourse.bass_utils import run_bass_kernel_spmd as _run

    z = {n: np.asarray(a) for n, a in inputs.items()}
    parts = []
    for name, idx, k0, nk, c0, ncl in plan():
        w = z[name] if idx is None else z[name][idx]
        w = w[k0 * 128:(k0 + nk) * 128, c0:c0 + ncl].reshape(nk, 128, ncl)
        parts.append(w.transpose(1, 0, 2).reshape(128, nk * ncl))
    wall = np.ascontiguousarray(np.concatenate(parts, 1))

    def pk(a):
        return np.asarray(a).reshape(-1, 128).T

    def short(a):
        a = np.asarray(a).reshape(-1, 1)
        return np.concatenate([a, np.zeros((128 - len(a), 1), np.float32)], 0)

    got = {
        "mix0": pk(z["norm_mix_g"][0]), "mix1": pk(z["norm_mix_g"][1]), "ffn0": pk(z["norm_ffn_g"][0]),
        "ffn1": pk(z["norm_ffn_g"][1]), "kv": pk(z["kv_norm_g"]), "final": pk(z["final_g"]),
        "n1": pk(z["norm1_g_2"][0]), "n2": pk(z["norm2_g_2"][0]), "nf": pk(z["normf_g_2"]),
        "cw": pk(z["a_conv_w"][0]), "cb": pk(z["a_conv_b"][0]), "hg": pk(z["a_head_g"][0]),
        "fw0": pk(z["ffn_conv_w"][0]), "fb0": pk(z["ffn_conv_b"][0]), "fw1": pk(z["ffn_conv_w"][1]),
        "fb1": pk(z["ffn_conv_b"][1]), "sub": pk(z["subln_g_2"][0]), "gi": short(z["a_gate_b"][0][0:4]),
        "gf": short(z["a_gate_b"][0][4:8]), "bf": short(z["b_f_2"][0]),
        "lam": np.concatenate([short(z[n][0]) for n in ("lam_q1_2", "lam_q2_2", "lam_k1_2", "lam_k2_2")], 1),
    }
    cols = np.ascontiguousarray(np.concatenate([got[n] for n in COLS], 1))
    t, c = np.arange(128)[:, None], np.arange(512)[None, :]
    idx = np.clip(t + 384 - c, -63, 128) + 63
    bias = np.ascontiguousarray(z["b_rel_bias"][0][:, idx].transpose(1, 0, 2).reshape(128, 12 * 512))
    consts, rope = shape_constants()
    arrays = {
        "wall": wall, "xt": z["x"][0].T.reshape(8, 128, 512).transpose(1, 0, 2).reshape(128, 4096),
        "memt": z["mem"][0].T.reshape(8, 128, 256).transpose(1, 0, 2).reshape(128, 2048),
        "cols": cols, "bias": bias, "consts": consts, "rope": rope,
    }
    arrays = {n: np.ascontiguousarray(a) for n, a in arrays.items()}
    nc = _bacc.Bacc("TRN2", target_bir_lowering=False, num_devices=1)
    args = [nc.dram_tensor("in_" + n, a.shape, F32, kind="ExternalInput").ap() for n, a in arrays.items()]
    args.append(nc.dram_tensor("out_y", (128, 4096), F32, kind="ExternalOutput").ap())
    program(nc, *args)
    r = _run(nc, [{"in_" + n: a for n, a in arrays.items()}], core_ids=[0])
    y = np.asarray(r.results[0]["out_y"])
    return np.ascontiguousarray(y.reshape(128, 8, 512).transpose(1, 0, 2).reshape(1024, 512).T.reshape(1, 512, 1024))
```
